# Optimizing a Trainium2 kernel written in Bass

```python
import jax, jax.numpy as jnp
from jax import lax
import numpy as np

D_MODEL = 1024
BATCH = 1
SEQ = 1024
DEPTH = 2
DEC_BATCH = 1
DEC_SEQ = 64
PAST_LEN = 256

CHUNK = 64
HEAD_DIM = 64
Q_BLOCK = 128
EPS = 1e-6
NEG_INF = -1e30

A_HEADS = 8
A_PAST_CHUNKS = 8
A_CACHE_ROWS = A_PAST_CHUNKS * CHUNK
A_REL_MAX = 256
B_HEADS = 8
C_HEADS = 8
C_Q_LORA = 384
C_KV_LORA = 256
C_NOPE = 64
C_ROPE = 32
C_V = 64
ROPE_BASE = 10000.0
MLA_SCALE = (C_NOPE + C_ROPE) ** -0.5
D_HEADS = 8
D_KV_HEADS = 2
D_REP = D_HEADS // D_KV_HEADS
D_WINDOW = 128
D_PAST_CHUNKS = -(-D_WINDOW // CHUNK)
D_CACHE_ROWS = D_PAST_CHUNKS * CHUNK
D_FF = 2816
CONV_W = 3

N_EVEN = (DEPTH + 1) // 2
N_ODD = DEPTH // 2
EVEN_SPLITS = (A_HEADS * HEAD_DIM,) * 3 + (B_HEADS * HEAD_DIM,) * 3
ODD_SPLITS = (C_Q_LORA, C_KV_LORA, C_ROPE, D_HEADS * HEAD_DIM, D_KV_HEADS * HEAD_DIM, D_KV_HEADS * HEAD_DIM)

kernel_name = 'hybrid_streaming_encoder_step'

def split_cols(x, sizes):
    return jnp.split(x, np.cumsum(sizes)[:-1].tolist(), axis=-1)

def rms_norm(x, g):
    xf = x.astype(jnp.float32)
    y = xf * lax.rsqrt(jnp.mean(xf * xf, axis=-1, keepdims=True) + EPS)
    return (y * g.astype(jnp.float32)).astype(x.dtype)

def rope(x, pos):
    half = C_ROPE // 2
    inv = ROPE_BASE ** (-jnp.arange(half, dtype=jnp.float32) / half)
    ang = pos.astype(jnp.float32)[:, None] * inv[None, :]
    shape = (pos.shape[0],) + (1,) * (x.ndim - 3) + (half,)
    cos, sin = jnp.cos(ang).reshape(shape), jnp.sin(ang).reshape(shape)
    x1 = x[..., :half].astype(jnp.float32)
    x2 = x[..., half:].astype(jnp.float32)
    return jnp.concatenate([x1 * cos - x2 * sin, x2 * cos + x1 * sin], axis=-1).astype(x.dtype)

def alibi_slopes(n):
    return 2.0 ** (-8.0 * jnp.arange(1, n + 1, dtype=jnp.float32) / n)

def softmax_attend(q, k, v, bias, mask, scale, sink=None):
    s = jnp.einsum('...qgrd,...kgd->...grqk', q, k, preferred_element_type=jnp.float32) * scale + bias
    s = jnp.where(mask, s, NEG_INF)
    if sink is not None:
        sk = jnp.broadcast_to(sink.astype(jnp.float32)[:, :, None, None], s.shape[:-1] + (1,))
        p = jax.nn.softmax(jnp.concatenate([s, sk], axis=-1), axis=-1)[..., :-1]
    else:
        p = jax.nn.softmax(s, axis=-1)
    return jnp.einsum('...grqk,...kgd->...qgrd', p.astype(v.dtype), v)

def stick_breaking(q, k, v, q_pos, k_pos):
    z = jnp.einsum('bqhd,bkhd->bhqk', q, k, preferred_element_type=jnp.float32) * (q.shape[-1] ** -0.5)
    vis = k_pos[None, :] < q_pos[:, None]
    log_beta = jnp.where(vis, jax.nn.log_sigmoid(z), NEG_INF)
    log_keep = jnp.where(vis, jax.nn.log_sigmoid(-z), 0.0)
    later = lax.cumsum(log_keep, axis=3, reverse=True) - log_keep
    w = jnp.exp(log_beta + later)
    return jnp.einsum('bhqk,bkhd->bqhd', w.astype(v.dtype), v)

def blocked_queries(fn, q):
    B, T = q.shape[:2]
    nb = T // Q_BLOCK
    qb = jnp.moveaxis(q.reshape((B, nb, Q_BLOCK) + q.shape[2:]), 1, 0)
    out = lax.map(lambda a: fn(a[0], a[1] * Q_BLOCK + jnp.arange(Q_BLOCK)), (qb, jnp.arange(nb)))
    return jnp.moveaxis(out, 0, 1).reshape((B, T) + out.shape[3:])

def band_gather(x, n_past):
    B, T = x.shape[:2]
    nc = T // CHUNK
    xc = x.reshape((B, nc, CHUNK) + x.shape[2:])
    xp = jnp.concatenate([jnp.zeros((B, n_past, CHUNK) + x.shape[2:], x.dtype), xc], axis=1)
    idx = jnp.arange(nc)[:, None] + jnp.arange(n_past + 1)[None, :]
    return xp[:, idx].reshape((B, nc, (n_past + 1) * CHUNK) + x.shape[2:])

def band_positions(T, n_past):
    nc = T // CHUNK
    q_pos = jnp.arange(T).reshape(nc, CHUNK)
    k_pos = (jnp.arange(nc)[:, None] - n_past) * CHUNK + jnp.arange((n_past + 1) * CHUNK)[None, :]
    return q_pos, k_pos

def band_mask(q_pos, k_pos, n_past):
    qc = q_pos[:, :, None] // CHUNK
    kc = k_pos[:, None, :] // CHUNK
    m = (k_pos[:, None, :] >= 0) & (kc <= qc) & (kc >= qc - n_past)
    return m[:, None, None]

def chunk_causal_mask(q_pos, k_pos):
    return (k_pos[None, :] // CHUNK) <= (q_pos[:, None] // CHUNK)

def rel_bias(table, q_pos, k_pos):
    rel = jnp.clip(q_pos[:, :, None] - k_pos[:, None, :], -A_REL_MAX, A_REL_MAX) + A_REL_MAX
    return jnp.moveaxis(table[:, rel], 0, 1)[:, :, None].astype(jnp.float32)

def alibi_bias(slopes, q_pos, k_pos):
    dist = jnp.abs(q_pos[:, :, None] - k_pos[:, None, :]).astype(jnp.float32)
    return -slopes[None, :, :, None, None] * dist[:, None, None]

def mla_inputs(cq, ckv, kpe, g_q, w_uq, g_kv, pos):
    q = jnp.einsum('btr,rhe->bthe', rms_norm(cq, g_q), w_uq)
    q = jnp.concatenate([q[..., :C_NOPE], rope(q[..., C_NOPE:], pos)], axis=-1)
    return q, rms_norm(ckv, g_kv), rope(kpe, pos)

def mla_keys(ckv, kpe, w_ukv):
    kv = jnp.einsum('bkr,rhe->bkhe', ckv, w_ukv)
    kr = jnp.broadcast_to(kpe[:, :, None, :], kpe.shape[:2] + (C_HEADS, C_ROPE))
    return jnp.concatenate([kv[..., :C_NOPE], kr], axis=-1), kv[..., C_NOPE:]

def even_prompt(h, w_in, table, w_out):
    B, T, _ = h.shape
    nc = T // CHUNK
    qa, ka, va, qb, kb, vb = [t.reshape(B, T, -1, HEAD_DIM) for t in split_cols(h @ w_in, EVEN_SPLITS)]
    q_pos, k_pos = band_positions(T, A_PAST_CHUNKS)
    oa = softmax_attend(qa.reshape(B, nc, CHUNK, A_HEADS, 1, HEAD_DIM),
                        band_gather(ka, A_PAST_CHUNKS), band_gather(va, A_PAST_CHUNKS),
                        rel_bias(table, q_pos, k_pos), band_mask(q_pos, k_pos, A_PAST_CHUNKS),
                        HEAD_DIM ** -0.5)
    pos = jnp.arange(T)
    ob = blocked_queries(lambda qblk, qp: stick_breaking(qblk, kb, vb, qp, pos), qb)
    y = jnp.concatenate([oa.reshape(B, T, -1), ob.reshape(B, T, -1)], axis=-1) @ w_out
    n = min(A_CACHE_ROWS, T)
    return y, (ka[:, -n:], va[:, -n:], kb, vb)

def even_sample(h, ck_a, cv_a, ck_b, cv_b, w_in, table, w_out):
    B, S, _ = h.shape
    past, n_a = ck_b.shape[1], ck_a.shape[1]
    qa, ka, va, qb, kb, vb = [t.reshape(B, S, -1, HEAD_DIM) for t in split_cols(h @ w_in, EVEN_SPLITS)]
    q_pos = past + jnp.arange(S)
    ka_all = jnp.concatenate([ck_a.astype(ka.dtype), ka], axis=1)
    va_all = jnp.concatenate([cv_a.astype(va.dtype), va], axis=1)
    k_pos_a = jnp.arange(past - n_a, past + S)
    oa = softmax_attend(qa[:, None, :, :, None], ka_all[:, None], va_all[:, None],
                        rel_bias(table, q_pos[None], k_pos_a[None]),
                        band_mask(q_pos[None], k_pos_a[None], A_PAST_CHUNKS), HEAD_DIM ** -0.5)[:, 0]
    kb_all = jnp.concatenate([ck_b.astype(kb.dtype), kb], axis=1)
    vb_all = jnp.concatenate([cv_b.astype(vb.dtype), vb], axis=1)
    ob = stick_breaking(qb, kb_all, vb_all, q_pos, jnp.arange(past + S))
    y = jnp.concatenate([oa.reshape(B, S, -1), ob.reshape(B, S, -1)], axis=-1) @ w_out
    return y, (ka_all[:, -n_a:], va_all[:, -n_a:], kb, vb)

def odd_prompt(h, w_in, g_q, w_uq, g_kv, w_ukv, sinks, w_out):
    B, T, _ = h.shape
    nc = T // CHUNK
    cq, ckv, kpe, qd, kd, vd = split_cols(h @ w_in, ODD_SPLITS)
    pos = jnp.arange(T)
    q, ckv, kpe = mla_inputs(cq, ckv, kpe, g_q, w_uq, g_kv, pos)
    k, v = mla_keys(ckv, kpe, w_ukv)
    oc = blocked_queries(lambda qblk, qp: softmax_attend(qblk[:, :, :, None], k, v, 0.0,
                                                         chunk_causal_mask(qp, pos), MLA_SCALE), q)
    kd = kd.reshape(B, T, D_KV_HEADS, HEAD_DIM)
    vd = vd.reshape(B, T, D_KV_HEADS, HEAD_DIM)
    q_pos, k_pos = band_positions(T, D_PAST_CHUNKS)
    od = softmax_attend(qd.reshape(B, nc, CHUNK, D_KV_HEADS, D_REP, HEAD_DIM),
                        band_gather(kd, D_PAST_CHUNKS), band_gather(vd, D_PAST_CHUNKS),
                        alibi_bias(alibi_slopes(D_HEADS).reshape(D_KV_HEADS, D_REP), q_pos, k_pos),
                        band_mask(q_pos, k_pos, D_PAST_CHUNKS), HEAD_DIM ** -0.5,
                        sinks.reshape(D_KV_HEADS, D_REP))
    y = jnp.concatenate([oc.reshape(B, T, -1), od.reshape(B, T, -1)], axis=-1) @ w_out
    n = min(D_CACHE_ROWS, T)
    return y, (ckv, kpe, kd[:, -n:], vd[:, -n:])

def odd_sample(h, c_kv, c_kpe, ck_d, cv_d, w_in, g_q, w_uq, g_kv, w_ukv, sinks, w_out):
    B, S, _ = h.shape
    past, n_d = c_kv.shape[1], ck_d.shape[1]
    cq, ckv, kpe, qd, kd, vd = split_cols(h @ w_in, ODD_SPLITS)
    q_pos = past + jnp.arange(S)
    q, ckv, kpe = mla_inputs(cq, ckv, kpe, g_q, w_uq, g_kv, q_pos)
    k, v = mla_keys(jnp.concatenate([c_kv.astype(ckv.dtype), ckv], axis=1),
                    jnp.concatenate([c_kpe.astype(kpe.dtype), kpe], axis=1), w_ukv)
    oc = softmax_attend(q[:, :, :, None], k, v, 0.0, chunk_causal_mask(q_pos, jnp.arange(past + S)), MLA_SCALE)
    kd_all = jnp.concatenate([ck_d.astype(kd.dtype), kd.reshape(B, S, D_KV_HEADS, HEAD_DIM)], axis=1)
    vd_all = jnp.concatenate([cv_d.astype(vd.dtype), vd.reshape(B, S, D_KV_HEADS, HEAD_DIM)], axis=1)
    k_pos_d = jnp.arange(past - n_d, past + S)
    od = softmax_attend(qd.reshape(B, 1, S, D_KV_HEADS, D_REP, HEAD_DIM), kd_all[:, None], vd_all[:, None],
                        alibi_bias(alibi_slopes(D_HEADS).reshape(D_KV_HEADS, D_REP), q_pos[None], k_pos_d[None]),
                        band_mask(q_pos[None], k_pos_d[None], D_PAST_CHUNKS), HEAD_DIM ** -0.5,
                        sinks.reshape(D_KV_HEADS, D_REP))[:, 0]
    y = jnp.concatenate([oc.reshape(B, S, -1), od.reshape(B, S, -1)], axis=-1) @ w_out
    return y, (ckv, kpe, kd_all[:, -n_d:], vd_all[:, -n_d:])

def conv_ffn(x, g, w_in, conv_w, conv_b, w_out, past):
    T = x.shape[1]
    u = rms_norm(x, g) @ w_in
    up = jnp.concatenate([past.astype(u.dtype), u], axis=1)
    c = conv_b
    for i in range(CONV_W):
        c = c + conv_w[i] * up[:, i:i + T]
    a, b = jnp.split(c, 2, axis=-1)
    return (jax.nn.silu(a) * b) @ w_out, up[:, -(CONV_W - 1):]

def setup_inputs(seed: int = 0) -> dict:
    key = jax.random.key(seed)
    ks = iter(jax.random.split(key, 32))
    nrm = lambda shape, scale: scale * jax.random.normal(next(ks), shape, jnp.float32)
    a_rows = min(A_CACHE_ROWS, PAST_LEN)
    d_rows = min(D_CACHE_ROWS, PAST_LEN)
    mix_e = A_HEADS * HEAD_DIM + B_HEADS * HEAD_DIM
    mix_o = C_HEADS * C_V + D_HEADS * HEAD_DIM
    return {
        'x_prompt': nrm((BATCH, SEQ, D_MODEL), 1.0),
        'x_sample': nrm((DEC_BATCH, DEC_SEQ, D_MODEL), 1.0),
        'cache_a_k': nrm((N_EVEN, DEC_BATCH, a_rows, A_HEADS, HEAD_DIM), 1.0),
        'cache_a_v': nrm((N_EVEN, DEC_BATCH, a_rows, A_HEADS, HEAD_DIM), 1.0),
        'cache_b_k': nrm((N_EVEN, DEC_BATCH, PAST_LEN, B_HEADS, HEAD_DIM), 1.0),
        'cache_b_v': nrm((N_EVEN, DEC_BATCH, PAST_LEN, B_HEADS, HEAD_DIM), 1.0),
        'cache_c_kv': nrm((N_ODD, DEC_BATCH, PAST_LEN, C_KV_LORA), 1.0),
        'cache_c_kpe': nrm((N_ODD, DEC_BATCH, PAST_LEN, C_ROPE), 1.0),
        'cache_d_k': nrm((N_ODD, DEC_BATCH, d_rows, D_KV_HEADS, HEAD_DIM), 1.0),
        'cache_d_v': nrm((N_ODD, DEC_BATCH, d_rows, D_KV_HEADS, HEAD_DIM), 1.0),
        'state_ffn_conv': nrm((DEPTH, DEC_BATCH, CONV_W - 1, 2 * D_FF), 1.0),
        'norm_mix': 1.0 + nrm((DEPTH, D_MODEL), 0.05),
        'norm_ffn': 1.0 + nrm((DEPTH, D_MODEL), 0.05),
        'norm_final': 1.0 + nrm((D_MODEL,), 0.05),
        'even_w_in': nrm((N_EVEN, D_MODEL, sum(EVEN_SPLITS)), D_MODEL ** -0.5),
        'even_rel_bias': nrm((N_EVEN, A_HEADS, 2 * A_REL_MAX + 1), 0.5),
        'even_w_out': nrm((N_EVEN, mix_e, D_MODEL), mix_e ** -0.5),
        'odd_w_in': nrm((N_ODD, D_MODEL, sum(ODD_SPLITS)), D_MODEL ** -0.5),
        'odd_norm_q': 1.0 + nrm((N_ODD, C_Q_LORA), 0.05),
        'odd_w_uq': nrm((N_ODD, C_Q_LORA, C_HEADS, C_NOPE + C_ROPE), C_Q_LORA ** -0.5),
        'odd_norm_kv': 1.0 + nrm((N_ODD, C_KV_LORA), 0.05),
        'odd_w_ukv': nrm((N_ODD, C_KV_LORA, C_HEADS, C_NOPE + C_V), C_KV_LORA ** -0.5),
        'odd_sinks': nrm((N_ODD, D_HEADS), 1.0),
        'odd_w_out': nrm((N_ODD, mix_o, D_MODEL), mix_o ** -0.5),
        'ffn_w_in': nrm((DEPTH, D_MODEL, 2 * D_FF), D_MODEL ** -0.5),
        'ffn_conv_w': nrm((DEPTH, CONV_W, 2 * D_FF), CONV_W ** -0.5),
        'ffn_conv_b': nrm((DEPTH, 2 * D_FF), 0.01),
        'ffn_w_out': nrm((DEPTH, D_FF, D_MODEL), D_FF ** -0.5),
    }

def reference(x_prompt, x_sample, cache_a_k, cache_a_v, cache_b_k, cache_b_v,
              cache_c_kv, cache_c_kpe, cache_d_k, cache_d_v, state_ffn_conv,
              norm_mix, norm_ffn, norm_final,
              even_w_in, even_rel_bias, even_w_out,
              odd_w_in, odd_norm_q, odd_w_uq, odd_norm_kv, odd_w_ukv, odd_sinks, odd_w_out,
              ffn_w_in, ffn_conv_w, ffn_conv_b, ffn_w_out):
    xp, xs = x_prompt, x_sample
    even_p, even_s, odd_p, odd_s, conv_p, conv_s = [], [], [], [], [], []
    for layer in range(DEPTH):
        i = layer // 2
        hp = rms_norm(xp, norm_mix[layer])
        hs = rms_norm(xs, norm_mix[layer])
        if layer % 2 == 0:
            w = (even_w_in[i], even_rel_bias[i], even_w_out[i])
            yp, sp = even_prompt(hp, *w)
            ys, ss = even_sample(hs, cache_a_k[i], cache_a_v[i], cache_b_k[i], cache_b_v[i], *w)
            even_p.append(sp)
            even_s.append(ss)
        else:
            w = (odd_w_in[i], odd_norm_q[i], odd_w_uq[i], odd_norm_kv[i], odd_w_ukv[i], odd_sinks[i], odd_w_out[i])
            yp, sp = odd_prompt(hp, *w)
            ys, ss = odd_sample(hs, cache_c_kv[i], cache_c_kpe[i], cache_d_k[i], cache_d_v[i], *w)
            odd_p.append(sp)
            odd_s.append(ss)
        xp = xp + yp
        xs = xs + ys
        f = (norm_ffn[layer], ffn_w_in[layer], ffn_conv_w[layer], ffn_conv_b[layer], ffn_w_out[layer])
        fp, cp = conv_ffn(xp, *f, jnp.zeros((xp.shape[0], CONV_W - 1, 2 * D_FF), xp.dtype))
        fs, cs = conv_ffn(xs, *f, state_ffn_conv[layer])
        xp = xp + fp
        xs = xs + fs
        conv_p.append(cp)
        conv_s.append(cs)
    y_prompt = rms_norm(xp, norm_final)
    y_sample = rms_norm(xs, norm_final)
    stk = lambda groups, j: jnp.stack([g[j] for g in groups])
    a_k_prompt, a_v_prompt = stk(even_p, 0), stk(even_p, 1)
    a_k_sample, a_v_sample = stk(even_s, 0), stk(even_s, 1)
    b_k_prompt, b_v_prompt = stk(even_p, 2), stk(even_p, 3)
    b_k_sample, b_v_sample = stk(even_s, 2), stk(even_s, 3)
    c_kv_prompt, c_kpe_prompt = stk(odd_p, 0), stk(odd_p, 1)
    c_kv_sample, c_kpe_sample = stk(odd_s, 0), stk(odd_s, 1)
    d_k_prompt, d_v_prompt = stk(odd_p, 2), stk(odd_p, 3)
    d_k_sample, d_v_sample = stk(odd_s, 2), stk(odd_s, 3)
    ffn_conv_prompt = jnp.stack(conv_p)
    ffn_conv_sample = jnp.stack(conv_s)
    return (y_prompt, y_sample,
            a_k_prompt, a_v_prompt, a_k_sample, a_v_sample,
            b_k_prompt, b_v_prompt, b_k_sample, b_v_sample,
            c_kv_prompt, c_kpe_prompt, c_kv_sample, c_kpe_sample,
            d_k_prompt, d_v_prompt, d_k_sample, d_v_sample,
            ffn_conv_prompt, ffn_conv_sample)


_drawn_inputs = setup_inputs


def setup_inputs(seed=0):
    import zlib

    import numpy as np

    out = dict(_drawn_inputs(seed))
    spreads = {}
    factors = {'odd_norm_q': 8.0, 'ffn_conv_b': 5.766}
    for name, (base, spread) in spreads.items():
        noise = np.random.default_rng([zlib.crc32(name.encode()), seed]).standard_normal(out[name].shape)
        drawn = base * np.exp(spread * noise) if base else spread * noise
        out[name] = __import__('jax').numpy.asarray(drawn.astype(out[name].dtype))
    for name, factor in factors.items():
        out[name] = (out[name] * factor).astype(out[name].dtype)
    return out
```

```python
from contextlib import ExitStack

import concourse.bass as bass
from concourse import mybir

ALU = mybir.AluOpType
ACT = mybir.ActivationFunctionType
AX = mybir.AxisListType
F32 = mybir.dt.float32
F32R = mybir.dt.float32r

P = 128
D_MODEL, SEQ, DEC_SEQ, PAST = 1024, 1024, 64, 256
KT = D_MODEL // P
HEAD = 64
PAIRS = 4
CHUNK = 64
D_FF = 2816
GAP = 2
S0 = SEQ + GAP
T = S0 + DEC_SEQ
CUTS = [(0, 384), (384, 768), (768, T)]
KEYS = SEQ + PAST + DEC_SEQ
D_CACHE = 128
KEYS_D = SEQ + D_CACHE + DEC_SEQ
NQT = SEQ // P + 1
UNITS = 2 * NQT
MASKED = -1e30
EPS = 1e-6
C_Q, C_KV, C_ROPE, C_NOPE = 384, 256, 32, 64
C_SCALE = float(C_NOPE + C_ROPE) ** -0.5
SCALE = float(HEAD) ** -0.5
GROUPS = D_FF // 256
GAIN_MIX, GAIN_FFN, GAIN_FINAL, GAIN_Q, GAIN_KV, N_GAINS = (0, KT), (2 * KT, 3 * KT), 4 * KT, 5 * KT, 5 * KT + 3, 5 * KT + 5


def bank_of(n):
    return (n % 4) // 2, 512 * (n % 2)


class Norm:

    def __init__(self, nc, ctx, mem, name, src, cols, tiles, width, gain0, dst=None, split=None):
        self.nc, self.mem, self.src, self.cols, self.tiles = nc, mem, src, cols, tiles
        self.width, self.gain0, self.dst, self.split = width, gain0, dst, split
        sem = lambda s: mem.sem(f"{name}_{s}")
        self.squared, self.summed = sem("squared"), sem("summed")
        self.var, self.std, self.inv = sem("var"), sem("std"), sem("inv")
        self.normed = sem("normed")
        if split:
            self.high, self.low_v, self.low_p = sem("high"), sem("low_v"), sem("low_p")
        self.items = [(c, k) for c in range(len(cols)) for k in range(tiles)]

    def scalar(self, e):
        m = self.mem
        for i, (c, k) in enumerate(self.items):
            a, b = self.cols[c]
            if i >= 4:
                e.wait_ge(self.summed, i - 3)
            e.activation(m.sq[:, i % 4, 0:b - a], self.src(k, a, b), ACT.Square).then_inc(self.squared, 1)
        for c, (a, b) in enumerate(self.cols):
            e.wait_ge(self.var, c + 1)
            e.activation(m.rms[:, c, 0:b - a], m.rms[:, c, 0:b - a], ACT.Sqrt).then_inc(self.std, 1)
        if self.split:
            for i, (c, k) in enumerate(self.items):
                a, b = self.cols[c]
                e.wait_ge(self.normed, i + 1)
                e.activation(self.split[0][:, k, a:b], m.tmp[:, i % 4, 0:b - a], ACT.Copy).then_inc(self.high, 1)

    def tensor(self, e):
        m = self.mem
        for i, (c, k) in enumerate(self.items):
            a, b = self.cols[c]
            e.wait_ge(self.squared, i + 1)
            pb, off = bank_of(c)
            e.matmul(m.ps[pb][:, off:off + b - a], m.ones[:, :], m.sq[:, i % 4, 0:b - a],
                     start=k == 0, stop=k == self.tiles - 1).then_inc(self.summed, 1)

    def low(self, e, i, sem):
        c, k = self.items[i]
        a, b = self.cols[c]
        e.wait_ge(self.high, i + 1)
        e.tensor_tensor(self.split[1][:, k, a:b], self.mem.tmp[:, i % 4, 0:b - a],
                        self.split[0][:, k, a:b].bitcast(F32), ALU.subtract).then_inc(sem, 1)

    def vector(self, e):
        m = self.mem
        for c, (a, b) in enumerate(self.cols):
            e.wait_ge(self.summed, self.tiles * (c + 1))
            pb, off = bank_of(c)
            e.tensor_scalar(m.rms[:, c, 0:b - a], m.ps[pb][:, off:off + b - a], 1.0 / self.width, EPS,
                            ALU.mult, ALU.add).then_inc(self.var, 1)
        for i, (c, k) in enumerate(self.items):
            a, b = self.cols[c]
            if k == 0:
                e.wait_ge(self.std, c + 1)
                e.reciprocal(m.rms[:, c, 0:b - a], m.rms[:, c, 0:b - a]).then_inc(self.inv, 1)
                e.wait_ge(self.inv, c + 1)
            g = m.gains[:, self.gain0 + k:self.gain0 + k + 1]
            if self.split:
                if i >= 4:
                    e.wait_ge(self.low_p if i % 2 else self.low_v, (i - 4) // 2 + 1)
                out = m.tmp[:, i % 4, 0:b - a]
            else:
                out = self.dst(k, a, b)
            e.scalar_tensor_tensor(out, self.src(k, a, b), g, m.rms[:, c, 0:b - a],
                                   ALU.mult, ALU.mult).then_inc(self.normed, 1)
            if self.split and i % 2 == 1:
                self.low(e, i - 1, self.low_v)
        e.wait_ge(self.normed, len(self.items))

    def gpsimd(self, e):
        if self.split:
            for i in range(1, len(self.items), 2):
                self.low(e, i, self.low_p)


class Attend:

    def __init__(self, nc, ctx, mem, kind, otile, proj_base, ring, io):
        self.nc, self.m, self.kind, self.otile, self.io = nc, mem, kind, otile, io
        self.base, self.ring = proj_base, ring
        sem = lambda s: mem.sem(f"{kind}_{s}")
        self.opened = sem("opened")
        self.proj_s, self.proj_v = sem("projected_by_scalar"), sem("projected_by_vector")
        self.roped = sem("rope_parts")
        if kind in "AB":
            self.cache_in, self.kv_out = (nc.alloc_semaphore(f"{kind}_{s}") for s in ("cache_in", "kv_out"))
        if kind in "AD":
            self.strip_in = nc.alloc_semaphore(f"{kind}_strip_in")
        self.strip_masked = sem("strip_masked")
        self.turned, self.back_s, self.back_v = sem("turned"), sem("turned_read_by_scalar"), sem("turned_read_by_vector")
        self.scores = sem("scores")
        self.v1, self.front, self.mid1, self.mid = sem("vector_part"), sem("front"), sem("mid_part"), sem("mid")
        self.s1, self.logs, self.probs = sem("scalar_part"), sem("logs"), sem("probs")
        self.out, self.inv, self.normed = sem("out"), sem("inverse"), sem("normed")
        self.oturned, self.odone = sem("out_turned"), sem("out_done")
        self.qcopied = sem("q_copied")
        if kind in "AB":
            self.proj = [(w, what, c) for w, what in enumerate(("q", "k", "v")) for c in range(3)]
        elif kind == "C":
            self.proj = [(w, what, c) for w, what in enumerate(("qn", "qr", "kn", "v")) for c in range(3)]
        else:
            self.proj = []
        self.nw = len(self.proj) // 3
        self.by = []
        for n, (w, what, c) in enumerate(self.proj):
            self.by.append("v" if what == "qr" or (kind != "C" and n % 2) or (kind == "C" and what == "v") else "s")
        self.uses = []
        if kind != "D":
            for blocks in ((0, 1, 2, 3), (4, 5, 6, 7), (8, 9), (10,)):
                self.uses.append(("v", blocks))
        self.unit_uses = []
        for u in range(UNITS):
            nb = len(self.blocks(u))
            mine = []
            for g in range(0, nb, 4):
                mine.append(len(self.uses))
                self.uses.append((u, tuple(range(g, min(g + 4, nb)))))
            self.unit_uses.append(mine)
        self.use_by = []
        for n, (u, bl) in enumerate(self.uses):
            if u == "v":
                self.use_by.append("s" if n % 2 == 0 else "v")
            elif kind == "B":
                self.use_by.append("s")
            else:
                self.use_by.append("v" if bl[0] >= 4 else "s")

    def keys(self, u):
        t = u // 2
        if t == NQT - 1:
            return (SEQ, KEYS_D) if self.kind == "D" else (SEQ, KEYS)
        back = {"A": 512, "D": 128, "B": SEQ, "C": SEQ}[self.kind]
        return max(0, P * t - back), P * t + P

    def nq(self, u):
        return DEC_SEQ if u // 2 == NQT - 1 else P

    def qcol(self, u):
        return S0 if u // 2 == NQT - 1 else P * (u // 2)

    def blocks(self, u):
        a, b = self.keys(u)
        return [(k, min(P, b - k)) for k in range(a, b, P)]

    def strip0(self, u):
        if self.kind == "A":
            return 256 if u // 2 == NQT - 1 else self.keys(u)[0] - (P * (u // 2) - 512)
        return 0 if u // 2 == NQT - 1 else self.keys(u)[0] - (P * (u // 2) - 128)

    def count(self, listing, n, who):
        return sum(1 for x in listing[:n] if x == who)

    def wait_proj(self, e, j, n):
        for who, s in (("s", self.proj_s), ("v", self.proj_v)):
            c = self.count(self.by, n, who)
            if c:
                e.wait_ge(s, j * self.by.count(who) + c)

    def wait_back(self, e, j, n):
        for who, s in (("s", self.back_s), ("v", self.back_v)):
            c = self.count(self.use_by, n, who)
            if c:
                e.wait_ge(s, j * self.use_by.count(who) + c)

    def wait_turned_unit(self, e, j, u):
        e.wait_ge(self.turned, j * len(self.uses) + self.unit_uses[u][-1] + 1)

    def open(self, e, j):
        e.drain().then_inc(self.opened, 1)
        e.wait_ge(self.opened, j * 4 + 4)

    def tensor(self, e):
        m = self.m
        with e.Fori(0, PAIRS) as j:
            self.open(e, j)
            for n, (w, what, c) in enumerate(self.proj):
                if c == 0:
                    first = self.base // 3 + w
                    e.wait_ge(m.w_in[first % self.ring], j * (16 * self.nw // self.ring) + 16 * (first // self.ring + 1))
                if n >= 4:
                    self.wait_proj(e, j, n - 3)
                tiles, cols, a, b = self.operand(what, c)
                pb, off = bank_of(n)
                for k in range(tiles):
                    mm = e.matmul(m.ps[pb][:, off:off + b - a], m.w[:, (self.base // 3 + w) % self.ring, k * P:(k + 1) * P],
                                  cols(k, a, b), start=k == 0, stop=k == tiles - 1)
                mm.then_inc(m.proj_ready, 1)
            if self.proj:
                self.wait_proj(e, j, len(self.proj))
                if self.kind == "C":
                    e.wait_ge(self.qcopied, j + 1)
                else:
                    e.wait_ge(self.cache_in, j * 32 + 32)
            else:
                e.wait_ge(self.qcopied, j + 1)
            for r, (u, blocks) in enumerate(self.uses):
                if u != "v":
                    break
                if r >= 2:
                    self.wait_back(e, j, r - 1)
                m.apart(e)
                for i, blk in enumerate(blocks):
                    kw = min(P, KEYS - P * blk)
                    mm = e.transpose(m.pst[r % 2][0:kw, P * i:P * i + P], m.vt[:, P * blk:P * blk + kw], m.ident[:, :])
                mm.then_inc(self.turned, 1)
            if self.proj:
                self.wait_back(e, j, 4)
            for step in range(-1, UNITS + 1):
                if step + 1 < UNITS:
                    self.pe_scores(e, j, step + 1)
                if step >= 1:
                    self.pe_out(e, j, step - 1)
                if 0 <= step < UNITS:
                    self.pe_turn(e, j, step)
                if step >= 1 and (step - 1) % 2:
                    t = (step - 1) // 2
                    nq = self.nq(step - 1)
                    e.wait_ge(self.normed, j * NQT + t + 1)
                    if t >= 1:
                        e.wait_ge(self.odone, j * NQT + t)
                    m.apart(e)
                    e.transpose(m.pot[:, 0:nq], m.otok[0:nq, :], m.ident[0:nq, 0:nq]).then_inc(self.oturned, 1)

    def pe_scores(self, e, j, u):
        m, hh = self.m, u % 2
        a, b = self.keys(u)
        nq, q0 = self.nq(u), self.qcol(u)
        if u >= 2:
            e.wait_ge({"A": self.front, "D": self.front, "B": self.mid, "C": self.probs}[self.kind], j * UNITS + u - 1)
        if self.kind == "C":
            q, k = m.qh[hh], m.kh[hh]
            lo, hi = 0, C_NOPE + C_ROPE
        else:
            q, k = m.q, (m.kd if self.kind == "D" else m.k)
            lo, hi = HEAD * hh, HEAD * hh + HEAD
        if nq < P:
            m.apart(e)
        for c in range(0, b - a, 512):
            n = min(512, b - a - c)
            mm = e.matmul(m.ps[u % 2][0:nq, c:c + n], q[lo:hi, q0:q0 + nq], k[lo:hi, a + c:a + c + n], start=True, stop=True)
        mm.then_inc(self.scores, 1)

    def pe_turn(self, e, j, u):
        m, nq = self.m, self.nq(u)
        e.wait_ge(self.probs, j * UNITS + u + 1)
        for r in self.unit_uses[u]:
            if r >= 2:
                self.wait_back(e, j, r - 1)
            m.apart(e)
            for i, blk in enumerate(self.uses[r][1]):
                kw = self.blocks(u)[blk][1]
                mm = e.transpose(m.pst[r % 2][0:kw, P * i:P * i + nq], m.wk[0:nq, u % 2, P * blk:P * blk + kw],
                                 m.ident[0:nq, 0:nq])
            mm.then_inc(self.turned, 1)

    def pe_out(self, e, j, u):
        m, nq, hh = self.m, self.nq(u), u % 2
        self.wait_back(e, j, self.unit_uses[u][-1] + 1)
        if hh == 0 and u >= 2:
            e.wait_ge(self.normed, j * NQT + u // 2)
        bl = self.blocks(u)
        v = m.vtok_d if self.kind == "D" else m.vtok
        m.apart(e)
        for i, (k, kw) in enumerate(bl):
            mm = e.matmul(m.po[0:nq, HEAD * hh:HEAD * hh + HEAD], m.pt[0:kw, P * i:P * i + nq],
                          v[0:kw, k // P, HEAD * hh:HEAD * hh + HEAD], start=i == 0, stop=i == len(bl) - 1,
                          skip_group_check=True)
        mm.then_inc(self.out, 1)

    def operand(self, what, c):
        m = self.m
        if what in ("q", "k", "v") and self.kind != "C":
            return KT, lambda k, a, b: m.hn[:, k, a:b], *CUTS[c]
        if what in ("qn", "qr"):
            return C_Q // P, lambda k, a, b: m.cq[:, k, a:b], *CUTS[c]
        return C_KV // P, lambda k, a, b: m.ckv[:, k, a:b], 448 * c, 448 * c + 448

    def evict(self, e, who, n):
        m = self.m
        w, what, c = self.proj[n]
        _, _, a, b = self.operand(what, c)
        pb, off = bank_of(n)
        src = m.ps[pb][:, off:off + b - a]
        sem = self.proj_s if who == "s" else self.proj_v

        def move(dst, src, scale=1.0):
            if who == "s":
                return e.activation(dst, src, ACT.Copy, scale=scale)
            return e.tensor_scalar(dst, src, scale, None, ALU.mult) if scale != 1.0 else e.tensor_copy(dst, src)

        if what == "q":
            move(m.q[:, a:b], src, SCALE).then_inc(sem, 1)
        elif what in ("k", "v") and self.kind != "C":
            dst = m.k if what == "k" else m.vt
            if c < 2:
                move(dst[:, a:b], src).then_inc(sem, 1)
            else:
                move(dst[:, a:SEQ], src[:, 0:SEQ - a])
                move(dst[:, KEYS - DEC_SEQ:KEYS], src[:, S0 - a:b - a]).then_inc(sem, 1)
        elif what == "v":
            move(m.vt[:, a:b], src).then_inc(sem, 1)
        elif what in ("qn", "kn"):
            dst = m.qh if what == "qn" else m.kh
            move(dst[0][0:HEAD, a:b], src[0:HEAD, :])
            move(dst[1][0:HEAD, a:b], src[HEAD:P, :]).then_inc(sem, 1)

    def scalar(self, e):
        m, kind = self.m, self.kind
        with e.Fori(0, PAIRS) as j:
            self.open(e, j)
            if kind == "D":
                e.activation(m.q[:, :], m.o[:, bass.ds(j + self.otile, 1), :], ACT.Copy).then_inc(self.qcopied, 1)
            for n in range(len(self.proj)):
                if self.by[n] == "s":
                    e.wait_ge(m.proj_ready, j * len(self.proj) + self.base + n + 1)
                    self.evict(e, "s", n)
            for r, (u, _) in enumerate(self.uses):
                if u == "v" and self.use_by[r] == "s":
                    self.read_turned(e, "s", j, r)
            for step in range(-1, UNITS + 2):
                if step + 1 < UNITS:
                    self.sc_weights(e, j, step + 1)
                if kind == "B" and 0 <= step < UNITS:
                    nq, w = self.nq(step), self.keys(step)[1] - self.keys(step)[0]
                    e.wait_ge(self.mid, j * UNITS + step + 1)
                    e.activation(m.wk[0:nq, step % 2, 0:w], m.wk[0:nq, step % 2, 0:w], ACT.Exp).then_inc(self.probs, 1)
                if 0 <= step < UNITS:
                    for r in self.unit_uses[step]:
                        if self.use_by[r] == "s":
                            self.read_turned(e, "s", j, r)
                if step >= 3 and step % 2 == 1:
                    t = (step - 3) // 2
                    self.sc_output(e, j, t)

    def sc_output(self, e, j, t):
        m = self.m
        u = 2 * t
        nq, q0 = self.nq(u), self.qcol(u)
        e.wait_ge(self.oturned, j * NQT + t + 1)
        m.apart(e)
        e.activation(m.o[:, bass.ds(j + self.otile, 1), q0:q0 + nq], m.pot[:, 0:nq], ACT.Copy).then_inc(self.odone, 1)

    def sc_weights(self, e, j, u):
        m, kind = self.m, self.kind
        nq, w = self.nq(u), self.keys(u)[1] - self.keys(u)[0]
        wk = m.wk[0:nq, u % 2, 0:w]
        s8 = u % 8
        total = m.rowsum[0:nq, s8:s8 + 1]
        neg = m.negmax[0:nq, u % 2:u % 2 + 1]
        e.wait_ge(self.front, j * UNITS + u + 1)
        if kind == "B":
            e.activation(wk, wk, ACT.Exp).then_inc(self.s1, 1)
            e.wait_ge(self.s1, j * UNITS + u + 1)
            e.activation(wk, wk, ACT.Ln, bias=1.0).then_inc(self.logs, 1)
        elif kind == "C":
            if u >= 2:
                self.wait_turned_unit(e, j, u - 2)
            e.activation(wk, m.ps[u % 2][0:nq, 0:w], ACT.Exp, bias=neg, scale=C_SCALE, accum_out=total).then_inc(self.probs, 1)
        else:
            if kind == "D":
                e.activation(m.esink[0:nq, s8:s8 + 1], m.sink[0:nq, u % 2:u % 2 + 1], ACT.Exp, bias=neg)
            e.activation(wk, wk, ACT.Exp, bias=neg, accum_out=total).then_inc(self.probs, 1)

    def read_turned(self, e, who, j, r):
        m = self.m
        u, bl = self.uses[r]
        bank = m.pst[r % 2]
        e.wait_ge(self.turned, j * len(self.uses) + r + 1)
        sem = self.back_s if who == "s" else self.back_v

        def move(dst, src):
            return e.activation(dst, src, ACT.Copy) if who == "s" else e.tensor_copy(dst, src)

        if u == "v":
            rows = min(P, KEYS - P * bl[0])
            move(m.vtok[0:rows, bl[0]:bl[-1] + 1, :],
                 bank[0:rows, 0:P * len(bl)].rearrange("p (b f) -> p b f", f=P)).then_inc(sem, 1)
            return
        nq = self.nq(u)
        kws = [self.blocks(u)[b][1] for b in bl]
        full = [b for b, kw in zip(bl, kws) if kw == P]
        ops = []
        if nq == P:
            ops.append((m.pt[:, P * bl[0]:P * (bl[-1] + 1)], bank[:, 0:P * len(bl)]))
        else:
            n = len(full)
            v = lambda x: x.rearrange("p (b f) -> p b f", f=P)[:, :, 0:nq]
            ops.append((v(m.pt[:, P * bl[0]:P * (bl[0] + n)]), v(bank[:, 0:P * n])))
            if len(full) < len(bl):
                ops.append((m.pt[0:HEAD, P * (bl[0] + n):P * (bl[0] + n) + nq], bank[0:HEAD, P * n:P * n + nq]))
        for dst, src in ops:
            ins = move(dst, src)
        ins.then_inc(sem, 1)

    def vector(self, e):
        m, kind = self.m, self.kind
        with e.Fori(0, PAIRS) as j:
            self.open(e, j)
            if kind == "C":
                for h in range(2):
                    ins = e.tensor_copy(m.kh[h][HEAD:HEAD + C_ROPE, :], m.kp[HEAD:HEAD + C_ROPE, :])
                ins.then_inc(self.qcopied, 1)
            if kind == "A":
                e.wait_ge(self.strip_in, j * 16 + 16)
                e.memset(m.strip[0:64, :, 576:640], MASKED)
                e.memset(m.strip[64:128, :, 0:64], MASKED).then_inc(self.strip_masked, 1)
            for n in range(len(self.proj)):
                if self.by[n] == "v":
                    e.wait_ge(m.proj_ready, j * len(self.proj) + self.base + n + 1)
                    if self.proj[n][1] == "qr":
                        self.rope(e, j, n)
                    else:
                        self.evict(e, "v", n)
            for r, (u, _) in enumerate(self.uses):
                if u == "v" and self.use_by[r] == "v":
                    self.read_turned(e, "v", j, r)
            if kind in "D":
                e.wait_ge(self.strip_in, j * 32 + 32)
            if kind == "A":
                e.wait_ge(self.strip_masked, j + 1)
            for step in range(-1, UNITS + 1):
                if step + 1 < UNITS:
                    self.ve_front(e, j, step + 1)
                if kind == "B" and 0 <= step < UNITS:
                    self.ve_sticks(e, j, step)
                if step >= 1 and step % 2 == 0:
                    self.ve_normalise(e, j, step // 2 - 1)
                if 0 <= step < UNITS:
                    for r in self.unit_uses[step]:
                        if self.use_by[r] == "v":
                            self.read_turned(e, "v", j, r)

    def rope(self, e, j, n):
        m = self.m
        c = self.proj[n][2]
        a, b = CUTS[c]
        pb, off = bank_of(n)
        w = b - a
        ta, tb = m.wk[0:64, 0, 0:w], m.wk[0:64, 1, 0:w]
        e.tensor_tensor(ta, m.ps[pb][0:64, off:off + w], m.rot[0:64, a:b], ALU.mult)
        e.tensor_tensor(tb, m.ps[pb][64:128, off:off + w], m.rot[64:128, a:b], ALU.mult).then_inc(self.roped, 1)
        e.wait_ge(self.roped, j * 3 + c + 1)
        e.tensor_tensor(m.qh[0][64:96, a:b], ta[0:32, :], tb[0:32, :], ALU.add)
        e.tensor_tensor(m.qh[1][64:96, a:b], ta[32:64, :], tb[32:64, :], ALU.add).then_inc(self.proj_v, 1)
        done = self.count(self.by, n + 1, "v")
        e.wait_ge(self.proj_v, j * self.by.count("v") + done)

    def ve_front(self, e, j, u):
        m, kind = self.m, self.kind
        nq, w = self.nq(u), self.keys(u)[1] - self.keys(u)[0]
        t = u // 2
        ps = m.ps[u % 2]
        wk = m.wk[0:nq, u % 2, 0:w]
        mx, neg = m.mx[0:nq, u % 2:u % 2 + 1], m.negmax[0:nq, u % 2:u % 2 + 1]
        e.wait_ge(self.scores, j * UNITS + u + 1)
        if u >= 2:
            self.wait_turned_unit(e, j, u - 2)
        if kind in "AD":
            s0 = self.strip0(u)
            m.apart(e)
            e.tensor_tensor_reduce(wk, ps[0:nq, 0:w], m.strip[0:nq, u % 2, s0:s0 + w], 1.0, -3e38,
                                   ALU.add, ALU.max, mx).then_inc(self.v1, 1)
            e.wait_ge(self.v1, j * UNITS + u + 1)
            if kind == "A":
                e.tensor_scalar(neg, mx, -1.0, None, ALU.mult).then_inc(self.front, 1)
            else:
                e.tensor_scalar(neg, mx, m.sink[0:nq, u % 2:u % 2 + 1], -1.0, ALU.max, ALU.mult).then_inc(self.front, 1)
        elif kind == "C":
            if t < NQT - 1:
                e.memset(ps[0:64, w - CHUNK:w], MASKED).then_inc(self.v1, 1)
                e.wait_ge(self.v1, j * 2 * (NQT - 1) + u + 1)
            e.tensor_reduce(mx, ps[0:nq, 0:w], AX.X, ALU.max).then_inc(self.mid1, 1)
            e.wait_ge(self.mid1, j * UNITS + u + 1)
            e.tensor_scalar(neg, mx, -C_SCALE, None, ALU.mult).then_inc(self.front, 1)
        else:
            d = min(P, nq)
            e.tensor_tensor(ps[0:nq, w - d:w], ps[0:nq, w - d:w], m.causal[0:nq, 0:d], ALU.add).then_inc(self.v1, 1)
            e.wait_ge(self.v1, j * UNITS + u + 1)
            e.tensor_scalar(wk, ps[0:nq, 0:w], 44.0, None, ALU.min).then_inc(self.front, 1)

    def ve_sticks(self, e, j, u):
        m = self.m
        nq, w = self.nq(u), self.keys(u)[1] - self.keys(u)[0]
        wk, run = m.wk[0:nq, u % 2, 0:w], m.run[0:nq, 0:w]
        z = m.ps[u % 2][0:nq, 0:w]
        e.wait_ge(self.logs, j * UNITS + u + 1)
        e.tensor_tensor(wk, z, wk, ALU.max).then_inc(self.mid1, 1)
        e.wait_ge(self.mid1, j * (2 * UNITS) + 2 * u + 1)
        if u:
            e.wait_ge(self.mid, j * UNITS + u)
        e.tensor_tensor_scan(run[:, ::-1], wk[:, ::-1], wk[:, ::-1], 0.0, ALU.add, ALU.max).then_inc(self.mid1, 1)
        e.wait_ge(self.mid1, j * (2 * UNITS) + 2 * u + 2)
        e.tensor_tensor(wk, z, run, ALU.subtract).then_inc(self.mid, 1)

    def ve_normalise(self, e, j, t):
        m, kind = self.m, self.kind
        nq = self.nq(2 * t)
        e.wait_ge(self.out, j * UNITS + 2 * t + 2)
        if t >= 1:
            e.wait_ge(self.oturned, j * NQT + t)
        if kind == "B":
            e.tensor_copy(m.otok[0:nq, :], m.po[0:nq, 0:P]).then_inc(self.normed, 1)
            return
        s8 = (2 * t) % 8
        total = m.rowsum[0:nq, s8:s8 + 2]
        per = 2 if kind == "D" else 1
        if kind == "D":
            e.tensor_tensor(total, total, m.esink[0:nq, s8:s8 + 2], ALU.add).then_inc(self.inv, 1)
            e.wait_ge(self.inv, j * per * NQT + per * t + 1)
        e.reciprocal(total, total).then_inc(self.inv, 1)
        e.wait_ge(self.inv, j * per * NQT + per * t + per)
        for hh in range(2):
            ins = e.tensor_scalar(m.otok[0:nq, HEAD * hh:HEAD * hh + HEAD], m.po[0:nq, HEAD * hh:HEAD * hh + HEAD],
                                  total[:, hh:hh + 1], None, ALU.mult)
        ins.then_inc(self.normed, 1)

    def gpsimd(self, e):
        m, kind, io = self.m, self.kind, self.io
        with e.Fori(0, PAIRS) as j:
            self.open(e, j)
            if kind == "A":
                e.dma_start(m.strip[:, :, :], io.bias[bass.ds(j, 1)].rearrange("a p h c -> p (a h) c")).then_inc(self.strip_in, 16)
            if kind == "D":
                e.dma_start(m.strip[:, :, 0:256], io.alibi[bass.ds(j, 1)].rearrange("a p h c -> p (a h) c")).then_inc(self.strip_in, 16)
                with self.nc.allow_non_contiguous_dma(reason="two sinks per row"):
                    e.dma_start(m.sink[:, :], io.sinks[bass.ds(j, 1)].rearrange("a p h -> p (a h)")).then_inc(self.strip_in, 16)
            if kind in "AB":
                ck, cv, ok, ov, oks, ovs, k0, s0 = io.caches[kind]
                e.dma_start(m.k[:, SEQ:SEQ + PAST], ck[bass.ds(j, 1)].rearrange("a p c -> (a p) c")).then_inc(self.cache_in, 16)
                e.dma_start(m.vt[:, SEQ:SEQ + PAST], cv[bass.ds(j, 1)].rearrange("a p c -> (a p) c")).then_inc(self.cache_in, 16)
                self.wait_proj(e, j, len(self.proj))
                e.wait_ge(self.cache_in, j * 32 + 32)
                for dst, a, b, buf in ((ok, k0, SEQ, m.k), (ov, k0, SEQ, m.vt), (oks, s0, KEYS, m.k), (ovs, s0, KEYS, m.vt)):
                    e.dma_start(dst[bass.ds(j, 1)].rearrange("a p c -> (a p) c"), buf[:, a:b]).then_inc(self.kv_out, 16)
                e.wait_ge(self.kv_out, j * 64 + 64)


class Mem:
    pass


def weight_stream(e, m, parts, ring):
    n = 0
    for src, width, count in parts:
        done = 0
        if n == 0:
            for s in range(ring):
                e.dma_start(m.w[:, s, 0:width], src[s]).then_inc(m.w_in[s], 16)
            n, done = ring, ring
        loops = (count - done) // ring
        if loops:
            with e.Fori(0, loops) as i:
                for s in range(ring):
                    slot = (n + s) % ring
                    e.wait_ge(m.proj_ready, i * (3 * ring) + 3 * (n + s - ring + 1))
                    e.dma_start(m.w[:, slot, 0:width],
                                src[bass.ds(i * ring + done + s, 1)].rearrange("a p c -> (a p) c")).then_inc(m.w_in[slot], 16)
            n += loops * ring
            done += loops * ring
        while done < count:
            e.wait_ge(m.proj_ready, 3 * (n - ring + 1))
            e.dma_start(m.w[:, n % ring, 0:width], src[done]).then_inc(m.w_in[n % ring], 16)
            n, done = n + 1, done + 1


class Project:

    def __init__(self, nc, ctx, mem, name, base, ring, units, moving):
        self.m, self.base, self.ring, self.units, self.moving = mem, base, ring, units, moving
        self.left = mem.sem(f"{name}_left_psum")

    def tensor(self, e):
        m = self.m
        n = 0
        for w in range(self.units):
            unit = self.base // 3 + w
            e.wait_ge(m.w_in[unit % self.ring], 16 * (unit // self.ring + 1))
            for c, (a, b) in enumerate(CUTS):
                if n >= 4:
                    e.wait_ge(self.left, n - 3)
                pb, off = bank_of(n)
                for k in range(KT):
                    mm = e.matmul(m.ps[pb][:, off:off + b - a], m.w[:, unit % self.ring, k * P:(k + 1) * P],
                                  self.moving(k, a, b), start=k == 0, stop=k == KT - 1)
                mm.then_inc(m.proj_ready, 1)
                n += 1

    def results(self, e):
        m = self.m
        for n in range(3 * self.units):
            w, c = divmod(n, 3)
            a, b = CUTS[c]
            pb, off = bank_of(n)
            e.wait_ge(m.proj_ready, self.base + n + 1)
            yield n, w, c, a, b, m.ps[pb], off


class Ffn:
    RING = 3

    def __init__(self, nc, ctx, mem, name, weights, params, tails):
        self.nc, self.m, self.weights, self.params, self.tails = nc, mem, weights, params, tails
        sem = lambda s: mem.sem(f"{name}_{s}")
        self.raw_in = [sem(f"raw_in{i}") for i in range(self.RING)]
        self.high, self.low = sem("weight_high"), sem("weight_low")
        self.par_in = [sem(f"params_in{i}") for i in range(2)]
        self.tails_out = sem("tails_out")
        self.up, self.left = sem("up"), sem("up_left_psum")
        self.c1, self.conv = sem("conv_part"), sem("conv")
        self.silu, self.gate, self.ghigh, self.glow = sem("silu"), sem("gate"), sem("gate_high"), sem("gate_low")
        self.down, self.banks_free = sem("down"), sem("down_banks_free")

    def sync(self, e):
        m = self.m
        for s in range(self.RING):
            e.dma_start(m.raw[:, s, :], self.weights[s]).then_inc(self.raw_in[s], 16)
        e.dma_start(m.par[:, 0, :, :], self.params[0]).then_inc(self.par_in[0], 16)
        e.wait_ge(self.low, 1)
        e.dma_start(m.raw[:, 0, :], self.weights[3]).then_inc(self.raw_in[0], 16)
        with e.Fori(0, (GROUPS - 1) // 2) as i:
            for s in range(12):
                n = 4 + s
                e.wait_ge(self.low, i * 12 + n - 2)
                e.dma_start(m.raw[:, n % 3, :], self.weights[bass.ds(i * 12 + n, 1)].rearrange("a p c -> (a p) c")).then_inc(self.raw_in[n % 3], 16)
                if s in (0, 6):
                    q = 1 if s == 0 else 0
                    e.wait_ge(self.conv, i * 8 + (1 if s == 0 else 4))
                    e.dma_start(m.par[:, q, :, :], self.params[bass.ds(i * 2 + (1 if s == 0 else 2), 1)].rearrange("a p t c -> (a p) t c")).then_inc(self.par_in[q], 16)
        for n in (64, 65):
            e.wait_ge(self.low, n - 2)
            e.dma_start(m.raw[:, n % 3, :], self.weights[n]).then_inc(self.raw_in[n % 3], 16)

    def pe_up(self, e, i, g):
        m = self.m
        for tile in range(4):
            n = tile if g == 0 else 4 + 6 * (g - 1) + tile
            e.wait_ge(self.low, i * 12 + n + 1)
            for c, (a, b) in enumerate(CUTS):
                q = 12 * g + 3 * tile + c
                if q >= 4:
                    e.wait_ge(self.left, i * 24 + q - 3)
                bank = m.ps4[q % 4]
                for k in range(KT):
                    for x, w, first in ((m.hh, m.wh, True), (m.hl, m.wh, False), (m.hh, m.wl, False)):
                        mm = e.matmul(bank[:, 0:b - a], w[:, n % 3, k * P:(k + 1) * P], x[:, k, a:b],
                                      start=k == 0 and first, stop=k == KT - 1 and w is m.wl)
                mm.then_inc(self.up, 1)

    def pe_down(self, e, i, g, last=False):
        m = self.m
        par = g % 2
        e.wait_ge(self.glow, i * 4 + 2 * g + 2)
        for mt in range(KT):
            n = (4 if last else 8) + 6 * g + mt // 4
            if mt % 4 == 0:
                e.wait_ge(self.low, i * 12 + n + 1)
            for c, (a, b) in enumerate(CUTS):
                q = 24 * g + 3 * mt + c
                e.wait_ge(self.banks_free, i * 48 + q + 1)
                bank = m.ps4[4 + q % 4]
                for k in range(2):
                    col = (mt % 4) * 2 * P + k * P
                    for x, w, first in ((m.gh, m.wh, True), (m.gl, m.wh, False), (m.gh, m.wl, False)):
                        mm = e.matmul(bank[:, 0:b - a], w[:, n % 3, col:col + P], x[:, 2 * par + k, a:b],
                                      start=k == 0 and first, stop=k == 1 and w is m.wl)
                mm.then_inc(self.down, 1)

    def tensor(self, e):
        self.pe_up(e, 0, 0)
        with e.Fori(0, (GROUPS - 1) // 2) as i:
            self.pe_up(e, i, 1)
            self.pe_down(e, i, 0)
            self.pe_up(e, i, 2)
            self.pe_down(e, i, 1)
        self.pe_down(e, (GROUPS - 1) // 2, 0, last=True)

    def wait_used(self, e, i, n):
        if n < 3:
            e.wait_ge(self.up, i * 24 + 3 * (n + 1))
            return
        if n == 3:
            e.wait_ge(self.up, i * 24 + 13)
            return
        g, s = divmod(n - 4, 6)
        if s < 4:
            e.wait_ge(self.up, i * 24 + 12 * (g + 1) + 3 * (s + 1))
        else:
            e.wait_ge(self.down, i * 48 + 24 * g + 12 * (s - 3))

    def sc_high(self, e, i, n):
        m = self.m
        s = n % 3
        e.wait_ge(self.raw_in[s], i * 64 + 16 * (n // 3 + 1))
        if n >= 3:
            self.wait_used(e, i, n - 3)
        e.activation(m.wh[:, s, :], m.raw[:, s, :], ACT.Copy).then_inc(self.high, 1)

    def sc_leave(self, e, i, g, tile, c):
        m = self.m
        q = 12 * g + 3 * tile + c
        tt = 4 * g + tile
        row = m.u[:, tt % 2, :]
        a, b = CUTS[c]
        bank = m.ps4[q % 4]
        e.wait_ge(self.up, i * 24 + q + 1)
        if c == 0:
            if tt >= 2:
                e.wait_ge(self.conv, i * 8 + tt - 1)
            if tile == 0:
                e.wait_ge(self.par_in[g % 2], i * 16 + 16 * (g // 2 + 1))
            e.activation(row[:, S0:S0 + 2], m.par[:, g % 2, tile, 4:6], ACT.Copy)
        if c < 2:
            e.activation(row[:, 2 + a:2 + b], bank[:, 0:b - a], ACT.Copy).then_inc(self.left, 1)
        else:
            if tile == 0 and g:
                e.wait_ge(self.tails_out, i * 32 + 16 * g)
            e.activation(row[:, 2 + a:2 + SEQ], bank[:, 0:SEQ - a], ACT.Copy)
            e.activation(row[:, 2 + S0:2 + T], bank[:, S0 - a:b - a], ACT.Copy)
            e.activation(m.tail[:, g % 2, 2 * tile, :], bank[:, SEQ - 2 - a:SEQ - a], ACT.Copy)
            e.activation(m.tail[:, g % 2, 2 * tile + 1, :], bank[:, T - 2 - a:T - a], ACT.Copy).then_inc(self.left, 1)

    def sc_up(self, e, i, g):
        m = self.m
        for tile in range(4):
            n = tile if g == 0 else 4 + 6 * (g - 1) + tile
            for c in range(3):
                self.sc_leave(e, i, g, tile, c)
                if c == 0:
                    self.sc_high(e, i, n + 2)
                    if tile % 2 == 0 and (g or tile):
                        self.sc_ghigh(e, i, 2 * g + tile // 2 - 1)
            if tile == 3:
                e.wait_ge(self.left, i * 24 + 12 * g + 12)
                dst = self.tails[0] if g == 0 else self.tails[bass.ds(i * 2 + g, 1)].rearrange("a p t c -> (a p) t c")
                e.dma_start(dst, m.tail[:, g % 2, :, :]).then_inc(self.tails_out, 16)
            if tile % 2:
                f = 2 * g + tile // 2
                e.wait_ge(self.conv, i * 8 + 2 * f + 1)
                if f:
                    e.wait_ge(self.glow, i * 4 + f)
                e.activation(m.sa[:, :], m.ca[:, :], ACT.Silu).then_inc(self.silu, 1)

    def sc_ghigh(self, e, i, f):
        m = self.m
        e.wait_ge(self.gate, i * 4 + f + 1)
        e.activation(m.gh[:, f % 4, :], m.sa[:, :], ACT.Copy).then_inc(self.ghigh, 1)

    def scalar(self, e):
        L = (GROUPS - 1) // 2
        self.sc_high(e, 0, 0)
        self.sc_high(e, 0, 1)
        self.sc_up(e, 0, 0)
        with e.Fori(0, L) as i:
            self.sc_up(e, i, 1)
            self.sc_high(e, i, 4 + 6)
            self.sc_high(e, i, 4 + 7)
            self.sc_up(e, i, 2)
            self.sc_high(e, i, 4 + 12)
            self.sc_high(e, i, 4 + 13)
        self.sc_ghigh(e, L, 1)
        e.wait_ge(self.tails_out, 16 * GROUPS)

    def po_low(self, e, i, n):
        m = self.m
        e.wait_ge(self.high, i * 12 + n + 1)
        e.tensor_tensor(m.wl[:, n % 3, :], m.raw[:, n % 3, :], m.wh[:, n % 3, :].bitcast(F32),
                        ALU.subtract).then_inc(self.low, 1)

    def po_glow(self, e, i, f):
        m = self.m
        e.wait_ge(self.ghigh, i * 4 + f + 1)
        e.tensor_tensor(m.gl[:, f % 4, :], m.sa[:, :], m.gh[:, f % 4, :].bitcast(F32), ALU.subtract).then_inc(self.glow, 1)

    def po_up(self, e, i, g):
        for tile in range(4):
            n = tile if g == 0 else 4 + 6 * (g - 1) + tile
            self.po_low(e, i, n + 2)
            if tile % 2 == 0 and (g or tile):
                self.po_glow(e, i, 2 * g + tile // 2 - 1)

    def gpsimd(self, e):
        L = (GROUPS - 1) // 2
        self.po_low(e, 0, 0)
        self.po_low(e, 0, 1)
        self.po_up(e, 0, 0)
        with e.Fori(0, L) as i:
            self.po_up(e, i, 1)
            self.po_low(e, i, 10)
            self.po_low(e, i, 11)
            self.po_up(e, i, 2)
            self.po_low(e, i, 16)
            self.po_low(e, i, 17)
        self.po_glow(e, L, 1)

    def ve_conv(self, e, i, g, tile):
        m = self.m
        tt = 4 * g + tile
        out = m.ca if tile % 2 == 0 else m.cb
        row = m.u[:, tt % 2, :]
        w = lambda x: m.par[:, g % 2, tile, x:x + 1]
        e.wait_ge(self.left, i * 24 + 3 * tt + 3)
        if tile % 2 == 0 and tt >= 2:
            e.wait_ge(self.silu, i * 4 + tt // 2)
        if tile % 2 and tt >= 2:
            e.wait_ge(self.gate, i * 4 + tt // 2)
        e.tensor_scalar(out[:, :], row[:, 0:T], w(0), w(3), ALU.mult, ALU.add).then_inc(self.c1, 1)
        e.wait_ge(self.c1, i * 16 + 2 * tt + 1)
        e.scalar_tensor_tensor(out[:, :], row[:, 1:T + 1], w(1), out[:, :], ALU.mult, ALU.add).then_inc(self.c1, 1)
        e.wait_ge(self.c1, i * 16 + 2 * tt + 2)
        e.scalar_tensor_tensor(out[:, :], row[:, 2:T + 2], w(2), out[:, :], ALU.mult, ALU.add).then_inc(self.conv, 1)

    def ve_gate(self, e, i, f):
        m = self.m
        e.wait_ge(self.silu, i * 4 + f + 1)
        e.wait_ge(self.conv, i * 8 + 2 * f + 2)
        e.tensor_tensor(m.sa[:, :], m.sa[:, :], m.cb[:, :], ALU.mult).then_inc(self.gate, 1)

    def ve_add(self, e, i, g, q0, q1):
        m = self.m
        for q in range(q0, q1):
            mt, c = divmod(q, 3)
            a, b = CUTS[c]
            bank = m.ps4[4 + (24 * g + q) % 4]
            e.wait_ge(self.down, i * 48 + 24 * g + q + 1)
            e.tensor_tensor(m.x[:, mt, a:b], bank[:, 0:b - a], m.x[:, mt, a:b], ALU.add).then_inc(self.banks_free, 1)

    def ve_up(self, e, i, g, head=0):
        self.ve_conv(e, i, g, 0)
        self.ve_conv(e, i, g, 1)
        self.ve_gate(e, i, 2 * g)
        self.ve_conv(e, i, g, 2)
        self.ve_conv(e, i, g, 3)
        if head:
            self.ve_add(e, i, g - 1, 0, head)
        self.ve_gate(e, i, 2 * g + 1)

    def vector(self, e):
        L = (GROUPS - 1) // 2
        e.sem_inc(self.banks_free, 4)
        self.ve_up(e, 0, 0)
        with e.Fori(0, L) as i:
            for g in (1, 2):
                self.ve_up(e, i, g, head=6)
                self.ve_add(e, i, g - 1, 6, 24)
        self.ve_add(e, L, 0, 0, 24)



def build(nc, io):
    with ExitStack() as top:
        m = Mem()
        sem = lambda s: top.enter_context(nc.semaphore(s))

        def sb(ctx, name, shape, dt=F32):
            return ctx.enter_context(nc.sbuf_tensor(name, shape, dt))

        m.ps = [top.enter_context(nc.psum_tensor(f"ps{i}", [P, 1024], F32)) for i in range(2)]
        m.pst = [top.enter_context(nc.psum_tensor(f"pst{i}", [P, 512], F32)) for i in range(2)]
        m.po = top.enter_context(nc.psum_tensor("po", [P, 512], F32))
        m.pot = top.enter_context(nc.psum_tensor("pot", [P, 512], F32))
        m.ps4 = [m.ps[0][:, 0:512], m.ps[0][:, 512:1024], m.ps[1][:, 0:512], m.ps[1][:, 512:1024],
                 m.pst[0], m.pst[1], m.po, m.pot]
        m.x = sb(top, "x", [P, KT, T])
        m.ident = sb(top, "ident", [P, P])
        m.ones = sb(top, "ones", [P, P])
        m.causal = sb(top, "causal", [P, P])
        m.gains = sb(top, "gains", [P, N_GAINS])
        loaded, consts = sem("loaded"), sem("consts")
        waited = sem("waited")

        def apart(e):
            e.sem_inc(waited, 1)
        m.apart = apart

        phase = []

        def phase_sem(name):
            phase.append(nc.alloc_semaphore(name))
            return phase[-1]
        m.sem = phase_sem

        def end_phase():
            nums = sorted(s.num for s in phase)
            runs = [[nums[0], nums[0]]]
            for n in nums[1:]:
                if n == runs[-1][1] + 1:
                    runs[-1][1] = n
                else:
                    runs.append([n, n])
            with nc.Block() as block:
                @block.gpsimd
                def _(e):
                    for a, b in runs:
                        e.sem_clear(range(a, b + 1))
            for s in phase:
                nc.release_semaphore(s)
            phase.clear()

        def norm_scratch(ctx, tag):
            m.sq = sb(ctx, f"sq{tag}", [P, 4, 384])
            m.tmp = sb(ctx, f"tmp{tag}", [P, 4, 384])
            m.rms = sb(ctx, f"rms{tag}", [P, 3, 384])

        def norm_block(name, gain0, dst=None, split=None, before=None):
            with ExitStack() as ctx:
                norm_scratch(ctx, name)
                norm = Norm(nc, ctx, m, name, lambda k, a, b: m.x[:, k, a:b], CUTS, KT, D_MODEL, gain0, dst, split)
                with nc.Block() as block:
                    @block.sync
                    def _(e):
                        if before:
                            e.dma_start(m.gains[:, :], io.gains).then_inc(loaded, 16)
                            for k in range(KT):
                                e.dma_start(m.x[:, k, :], io.x[:, k, :]).then_inc(loaded, 16)

                    @block.gpsimd
                    def _(e):
                        if before:
                            e.memset(m.ident[:, :], 0.0).then_inc(consts, 1)
                            e.memset(m.causal[:, :], 0.0).then_inc(consts, 1)
                            e.memset(m.ones[:, :], 1.0).then_inc(consts, 1)
                            e.wait_ge(consts, 3)
                            e.affine_select(out=m.ident[:, :], in_=m.ident[:, :], compare_op=ALU.not_equal, fill=1.0,
                                            base=0, pattern=[[-1, P]], channel_multiplier=1).then_inc(consts, 1)
                            e.affine_select(out=m.causal[:, :], in_=m.causal[:, :], compare_op=ALU.is_gt, fill=MASKED,
                                            base=0, pattern=[[-1, P]], channel_multiplier=1).then_inc(consts, 1)
                        norm.gpsimd(e)

                    @block.scalar
                    def _(e):
                        if before:
                            e.wait_ge(loaded, 16 * (KT + 1))
                        norm.scalar(e)

                    @block.tensor
                    def _(e):
                        if before:
                            e.wait_ge(consts, 5)
                        norm.tensor(e)

                    @block.vector
                    def _(e):
                        if before:
                            e.wait_ge(loaded, 16 * (KT + 1))
                        norm.vector(e)

        def ffn_layer(layer):
            with ExitStack() as ctx:
                m.hh = sb(ctx, f"hh{layer}", [P, KT, T], F32R)
                m.hl = sb(ctx, f"hl{layer}", [P, KT, T], F32R)
                norm_block(f"norm_ffn{layer}", GAIN_FFN[layer], split=(m.hh, m.hl))
                m.raw = sb(ctx, f"raw{layer}", [P, 3, 1024])
                m.wh = sb(ctx, f"wh{layer}", [P, 3, 1024], F32R)
                m.wl = sb(ctx, f"wl{layer}", [P, 3, 1024], F32R)
                m.u = sb(ctx, f"u{layer}", [P, 2, T + 2])
                m.ca, m.cb, m.sa = (sb(ctx, f"{n}{layer}", [P, T]) for n in ("ca", "cb", "sa"))
                m.gh = sb(ctx, f"gh{layer}", [P, 4, T], F32R)
                m.gl = sb(ctx, f"gl{layer}", [P, 4, T], F32R)
                m.par = sb(ctx, f"par{layer}", [P, 2, 4, 6])
                m.tail = sb(ctx, f"tail{layer}", [P, 2, 8, 2])
                f = Ffn(nc, ctx, m, f"ffn{layer}", io.ffn_w[layer], io.ffn_p[layer], io.tails[layer])
                halo0 = m.sem(f"halo_zero{layer}")
                with nc.Block() as block:
                    @block.sync
                    def _(e):
                        f.sync(e)

                    @block.gpsimd
                    def _(e):
                        e.memset(m.u[:, :, 0:2], 0.0).then_inc(halo0, 1)
                        f.gpsimd(e)

                    @block.scalar
                    def _(e):
                        f.scalar(e)

                    @block.tensor
                    def _(e):
                        f.tensor(e)

                    @block.vector
                    def _(e):
                        e.wait_ge(halo0, 1)
                        f.vector(e)

        def add_to_x(e, proj):
            for n, w, c, a, b, ps, off in proj.results(e):
                e.tensor_tensor(m.x[:, w, a:b], ps[:, off:off + b - a], m.x[:, w, a:b], ALU.add).then_inc(proj.left, 1)

        def attention_scratch(ctx, layer, ring):
            m.w = sb(ctx, f"w{layer}", [P, ring, 1024])
            m.o = sb(ctx, f"o{layer}", [P, KT, T])
            m.wk = sb(ctx, f"wk{layer}", [P, 2, 1024])
            m.run = sb(ctx, f"run{layer}", [P, KEYS_D])
            m.pt = sb(ctx, f"pt{layer}", [P, 1024])
            m.strip = sb(ctx, f"strip{layer}", [P, 2, 640])
            m.otok = sb(ctx, f"otok{layer}", [P, P])
            m.mx, m.negmax = sb(ctx, f"mx{layer}", [P, 2]), sb(ctx, f"negmax{layer}", [P, 2])
            m.rowsum, m.esink = sb(ctx, f"rowsum{layer}", [P, 8]), sb(ctx, f"esink{layer}", [P, 8])
            m.sink = sb(ctx, f"sink{layer}", [P, 2])
            m.w_in = [m.sem(f"w_in{layer}_{i}") for i in range(ring)]
            m.proj_ready = m.sem(f"projected{layer}")

        with ExitStack() as ctx:
            m.hn = sb(ctx, "hn0", [P, KT, T])
            norm_block("norm_mix0", GAIN_MIX[0], dst=lambda k, a, b: m.hn[:, k, a:b], before=True)
            attention_scratch(ctx, 0, 3)
            m.q, m.k, m.vt = sb(ctx, "q", [P, T]), sb(ctx, "k", [P, KEYS]), sb(ctx, "vt", [P, KEYS])
            m.vtok = sb(ctx, "vtok", [P, 11, P])
            a = Attend(nc, ctx, m, "A", 0, 0, 3, io)
            b = Attend(nc, ctx, m, "B", PAIRS, 36, 3, io)
            out = Project(nc, ctx, m, "out0", 72, 3, KT, lambda k, a, b: m.o[:, k, a:b])
            gap = m.sem("gap0")
            with nc.Block() as block:
                @block.sync
                def _(e):
                    weight_stream(e, m, [(io.w0, 1024, 32)], 3)

                @block.gpsimd
                def _(e):
                    e.memset(m.o[:, :, SEQ:S0], 0.0).then_inc(gap, 1)
                    a.gpsimd(e)
                    b.gpsimd(e)

                @block.scalar
                def _(e):
                    a.scalar(e)
                    b.scalar(e)

                @block.tensor
                def _(e):
                    a.tensor(e)
                    b.tensor(e)
                    e.wait_ge(gap, 1)
                    e.wait_ge(a.odone, PAIRS * NQT)
                    e.wait_ge(b.odone, PAIRS * NQT)
                    out.tensor(e)

                @block.vector
                def _(e):
                    a.vector(e)
                    b.vector(e)
                    add_to_x(e, out)
        ffn_layer(0)
        end_phase()

        with ExitStack() as ctx:
            m.hn = sb(ctx, "hn1", [P, KT, T])
            norm_block("norm_mix1", GAIN_MIX[1], dst=lambda k, a, b: m.hn[:, k, a:b])
            attention_scratch(ctx, 1, 4)
            m.q = sb(ctx, "q1", [P, T])
            m.cq, m.ckv = sb(ctx, "cq", [P, C_Q // P, T]), sb(ctx, "ckv", [P, C_KV // P, KEYS])
            m.kd, m.vtok_d = sb(ctx, "kd", [P, KEYS_D]), sb(ctx, "vtok_d", [P, 10, P])
            m.kp, m.rot = sb(ctx, "kp", [P, KEYS]), sb(ctx, "rot", [P, T])
            m.rms = sb(ctx, "rms1", [P, 4, 384])
            m.sq = m.wk[:, :, :].rearrange("p a b -> p (a b)")[:, 0:4 * 384].rearrange("p (a b) -> p a b", a=4)
            flat = m.hn[:, :, :].rearrange("p a b -> p (a b)")
            m.qh = [flat[:, i * T:(i + 1) * T] for i in range(2)]
            m.kh = [flat[:, 2 * T + i * KEYS:2 * T + (i + 1) * KEYS] for i in range(2)]
            at = 2 * T + 2 * KEYS
            m.vt = flat[:, at:at + KEYS]
            m.vtok = flat[:, at + KEYS:at + KEYS + 11 * P].rearrange("p (b f) -> p b f", f=P)
            inp = Project(nc, ctx, m, "in1", 0, 4, 12, lambda k, a, b: m.hn[:, k, a:b])
            kv_cols = [(0, 384), (384, 768), (768, SEQ), (SEQ + PAST, KEYS)]
            nq = Norm(nc, ctx, m, "norm_q", lambda k, a, b: m.cq[:, k, a:b], CUTS, 3, C_Q, GAIN_Q, lambda k, a, b: m.cq[:, k, a:b])
            nkv = Norm(nc, ctx, m, "norm_kv", lambda k, a, b: m.ckv[:, k, a:b], kv_cols, 2, C_KV, GAIN_KV, lambda k, a, b: m.ckv[:, k, a:b])
            c = Attend(nc, ctx, m, "C", 0, 36, 4, io)
            d = Attend(nc, ctx, m, "D", PAIRS, 84, 4, io)
            out = Project(nc, ctx, m, "out1", 84, 4, KT, lambda k, a, b: m.o[:, k, a:b])
            s = m.sem
            gap, roped, vturned, vleft = s("gap1"), s("roped1"), s("vd_turned"), s("vd_left")
            cache_in, stored = nc.alloc_semaphore("cache_in1"), nc.alloc_semaphore("stored1")
            new0 = SEQ + PAST
            vd_uses = ((0, 1, 2, 3), (4, 5, 6, 7), (8,), (9,))
            with nc.Block() as block:
                @block.sync
                def _(e):
                    weight_stream(e, m, [(io.w1, 1024, 12)], 4)
                    with e.Fori(0, PAIRS) as j:
                        for s, (src, width) in enumerate(((io.c_q, 384), (io.c_q, 384), (io.c_kv, 256), (io.c_kv, 256))):
                            e.wait_ge(m.proj_ready, j * 12 + 3 * (12 + s - 3))
                            e.dma_start(m.w[:, s, 0:width], src[bass.ds(j * 2 + s % 2, 1)].rearrange("a p c -> (a p) c")).then_inc(m.w_in[s], 16)
                    with e.Fori(0, 2) as i:
                        for s in range(4):
                            e.wait_ge(m.proj_ready, i * 12 + 3 * (28 + s - 3))
                            e.dma_start(m.w[:, s, :], io.w1_out[bass.ds(i * 4 + s, 1)].rearrange("a p c -> (a p) c")).then_inc(m.w_in[s], 16)

                @block.gpsimd
                def _(e):
                    e.dma_start(m.rot[:, :], io.rot).then_inc(cache_in, 16)
                    e.dma_start(m.ckv[:, :, SEQ:new0], io.cache_c).then_inc(cache_in, 16)
                    e.dma_start(m.kp[HEAD:HEAD + C_ROPE, SEQ:new0], io.cache_pe).then_inc(cache_in, 16)
                    e.dma_start(m.kd[:, SEQ:SEQ + D_CACHE], io.cache_dk).then_inc(cache_in, 16)
                    e.dma_start(m.run[:, SEQ:SEQ + D_CACHE], io.cache_dv).then_inc(cache_in, 16)
                    e.memset(m.o[:, 0:PAIRS, SEQ:S0], 0.0).then_inc(gap, 1)
                    e.wait_ge(inp.left, 36)
                    e.wait_ge(cache_in, 80)
                    for dst, src in ((io.dk, m.kd[:, SEQ - P:SEQ]), (io.dks, m.kd[:, KEYS_D - D_CACHE:KEYS_D]),
                                     (io.dv, m.run[:, SEQ - P:SEQ]), (io.dvs, m.run[:, KEYS_D - D_CACHE:KEYS_D]),
                                     (io.kpe, m.kp[HEAD:HEAD + C_ROPE, 0:SEQ]), (io.kpes, m.kp[HEAD:HEAD + C_ROPE, new0:KEYS])):
                        e.dma_start(dst, src).then_inc(stored, 16)
                    e.wait_ge(nkv.normed, 8)
                    e.dma_start(io.ckv, m.ckv[:, :, 0:SEQ]).then_inc(stored, 16)
                    e.dma_start(io.ckvs, m.ckv[:, :, new0:KEYS]).then_inc(stored, 16)
                    e.wait_ge(stored, 128)
                    c.gpsimd(e)
                    d.gpsimd(e)

                @block.scalar
                def _(e):
                    e.wait_ge(inp.left, 36)
                    e.wait_ge(roped, 3)
                    nq.scalar(e)
                    e.wait_ge(nq.normed, 9)
                    nkv.scalar(e)
                    c.scalar(e)
                    d.scalar(e)

                @block.tensor
                def _(e):
                    inp.tensor(e)
                    e.wait_ge(inp.left, 36)
                    e.wait_ge(cache_in, 80)
                    for r, blocks in enumerate(vd_uses):
                        if r >= 2:
                            e.wait_ge(vleft, r - 1)
                        for i, blk in enumerate(blocks):
                            kw = min(P, KEYS_D - P * blk)
                            mm = e.transpose(m.pst[r % 2][0:kw, P * i:P * i + P], m.run[:, P * blk:P * blk + kw], m.ident[:, :])
                        mm.then_inc(vturned, 1)
                    nq.tensor(e)
                    e.wait_ge(nq.normed, 9)
                    nkv.tensor(e)
                    c.tensor(e)
                    d.tensor(e)
                    e.wait_ge(gap, 1)
                    e.wait_ge(c.odone, PAIRS * NQT)
                    e.wait_ge(d.odone, PAIRS * NQT)
                    out.tensor(e)

                @block.vector
                def _(e):
                    for n, w, cut, a_, b_, ps, off in inp.results(e):
                        src = ps[:, off:off + b_ - a_]
                        if w < 3:
                            e.tensor_copy(m.cq[:, w, a_:b_], src).then_inc(inp.left, 1)
                        elif w < 5 or w in (6, 7):
                            dst = m.ckv[:, w - 3, :] if w < 5 else (m.kd if w == 6 else m.run)
                            end = KEYS if w < 5 else KEYS_D
                            if cut < 2:
                                e.tensor_copy(dst[:, a_:b_], src).then_inc(inp.left, 1)
                            else:
                                e.tensor_copy(dst[:, a_:SEQ], src[:, 0:SEQ - a_])
                                e.tensor_copy(dst[:, end - DEC_SEQ:end], src[:, S0 - a_:b_ - a_]).then_inc(inp.left, 1)
                        elif w == 5:
                            n_ = b_ - a_
                            ta, tb = m.wk[0:32, 0, 0:n_], m.wk[0:32, 1, 0:n_]
                            if cut == 0:
                                e.wait_ge(cache_in, 80)
                            else:
                                e.wait_ge(inp.left, n)
                            e.tensor_tensor(ta, src[0:32, :], m.rot[0:32, a_:b_], ALU.mult)
                            e.tensor_tensor(tb, src[64:96, :], m.rot[64:96, a_:b_], ALU.mult).then_inc(roped, 1)
                            e.wait_ge(roped, cut + 1)
                            kp = m.kp[HEAD:HEAD + C_ROPE, :]
                            if cut < 2:
                                e.tensor_tensor(kp[:, a_:b_], ta, tb, ALU.add).then_inc(inp.left, 1)
                            else:
                                e.tensor_tensor(kp[:, a_:SEQ], ta[:, 0:SEQ - a_], tb[:, 0:SEQ - a_], ALU.add)
                                e.tensor_tensor(kp[:, new0:KEYS], ta[:, S0 - a_:n_], tb[:, S0 - a_:n_], ALU.add).then_inc(inp.left, 1)
                        else:
                            e.tensor_scalar(m.o[:, PAIRS + w - 8, a_:b_], src, SCALE, None, ALU.mult).then_inc(inp.left, 1)
                    for r, blocks in enumerate(vd_uses):
                        rows = min(P, KEYS_D - P * blocks[0])
                        e.wait_ge(vturned, r + 1)
                        e.tensor_copy(m.vtok_d[0:rows, blocks[0]:blocks[-1] + 1, :],
                                      m.pst[r % 2][0:rows, 0:P * len(blocks)].rearrange("p (b f) -> p b f", f=P)).then_inc(vleft, 1)
                    nq.vector(e)
                    nkv.vector(e)
                    c.vector(e)
                    d.vector(e)
                    add_to_x(e, out)
        end_phase()
        ffn_layer(1)
        norm_block("norm_final", GAIN_FINAL, dst=lambda k, a, b: m.x[:, k, a:b])
        with nc.Block() as block:
            @block.sync
            def _(e):
                for k in range(KT):
                    e.dma_start(io.y[:, k, :], m.x[:, k, :]).then_inc(loaded, 16)
                e.wait_ge(loaded, 16 * (2 * KT + 1))


def kernel(**inputs):
    import numpy as np
    import concourse.bacc as bacc
    from concourse.bass_utils import run_bass_kernel_spmd

    g = {k: np.asarray(v) for k, v in inputs.items()}
    f32 = np.float32
    feat = lambda a, n=P: np.ascontiguousarray(a)

    def tiles(w):
        k, n = w.shape
        return w.reshape(k // P, P, n // P, P).transpose(2, 1, 0, 3).reshape(n // P, P, k)

    def cols(w, size=HEAD):
        return w.reshape(w.shape[0], -1, size)

    arrays = {}
    x = np.zeros((T, D_MODEL), f32)
    x[:SEQ], x[S0:] = g["x_prompt"][0], g["x_sample"][0]
    arrays["x"] = x.T.reshape(KT, P, T).transpose(1, 0, 2)
    gains = [g["norm_mix"][0], g["norm_mix"][1], g["norm_ffn"][0], g["norm_ffn"][1], g["norm_final"],
             g["odd_norm_q"][0], g["odd_norm_kv"][0]]
    arrays["gains"] = np.concatenate(gains).reshape(N_GAINS, P).T
    w = g["even_w_in"][0]
    a_and_b = tiles(w).reshape(2, 3, PAIRS, P, D_MODEL).transpose(0, 2, 1, 3, 4).reshape(24, P, D_MODEL)
    arrays["w0"] = np.concatenate([a_and_b, tiles(g["even_w_out"][0])])
    idx = np.clip(512 + np.arange(P)[:, None] - np.arange(640), -256, 256) + 256
    arrays["bias"] = g["even_rel_bias"][0].reshape(PAIRS, 2, -1)[:, :, idx].transpose(0, 2, 1, 3)
    pair = lambda c: np.moveaxis(c.reshape(c.shape[-3], PAIRS, P), 0, -1)
    for n in "ab":
        for kv in "kv":
            arrays[f"cache_{n}{kv}"] = pair(g[f"cache_{n}_{kv}"][0, 0])
    w = g["odd_w_in"][0]
    o = np.cumsum([0, C_Q, C_KV, C_ROPE, 512, 128, 128])
    part = [w[:, o[i]:o[i + 1]] for i in range(6)]
    swap = lambda z: np.concatenate([z[..., C_ROPE // 2:], z[..., :C_ROPE // 2]], axis=-1)
    kpe = part[2]
    qd = cols(part[3])
    qd = np.stack([qd[:, :PAIRS], qd[:, PAIRS:]], axis=2).reshape(D_MODEL, 512)
    arrays["w1"] = tiles(np.concatenate([part[0], part[1], kpe, kpe, swap(kpe), swap(kpe), part[4], part[5], qd], axis=1))
    uq = g["odd_w_uq"][0]
    nope, rope = uq[:, :, :C_NOPE], uq[:, :, C_NOPE:]
    both = lambda z: z.reshape(C_Q, PAIRS, 1, -1)
    r2 = np.concatenate([both(rope), both(swap(rope))], axis=2).reshape(C_Q, PAIRS, 1, P)
    arrays["c_q"] = tiles(np.concatenate([both(nope), r2], axis=2).reshape(C_Q, 2 * PAIRS * P))
    ukv = g["odd_w_ukv"][0].reshape(C_KV, PAIRS, 2, 2, HEAD).transpose(0, 1, 3, 2, 4)
    arrays["c_kv"] = tiles(ukv.reshape(C_KV, 2 * PAIRS * P))
    wo = g["odd_w_out"][0]
    d_rows = wo[512:].reshape(2, PAIRS, HEAD, D_MODEL).transpose(1, 0, 2, 3).reshape(512, D_MODEL)
    arrays["w1_out"] = tiles(np.concatenate([wo[:512], d_rows]))
    arrays["cache_c"] = g["cache_c_kv"][0, 0].T.reshape(C_KV // P, P, PAST).transpose(1, 0, 2)
    arrays["cache_pe"] = g["cache_c_kpe"][0, 0].T
    arrays["cache_dk"] = g["cache_d_k"][0, 0].reshape(D_CACHE, P).T
    arrays["cache_dv"] = g["cache_d_v"][0, 0].reshape(D_CACHE, P).T
    arrays["sinks"] = g["odd_sinks"][0]
    pos = np.zeros(T, f32)
    pos[:SEQ], pos[S0:] = np.arange(SEQ), PAST + np.arange(DEC_SEQ)
    inv = (f32(10000.0) ** (-np.arange(16, dtype=f32) / f32(16))).astype(f32)
    ang = (pos[None, :] * inv[:, None]).astype(f32)
    cos, sin = np.cos(ang).astype(f32), np.sin(ang).astype(f32)
    arrays["rot"] = np.concatenate([cos, cos, cos, cos, -sin, sin, -sin, sin])
    p_, c_ = np.arange(P)[:, None], np.arange(256)[None, :]
    seen = np.where(p_ < CHUNK, c_ < 192, c_ >= 64)
    slopes = (f32(2.0) ** (f32(-8.0) * np.arange(1, 9, dtype=f32) / f32(8))).astype(f32)
    pen = np.where(seen[None], -slopes[:, None, None] * np.abs(128 + p_ - c_)[None].astype(f32), f32(MASKED)).astype(f32)
    arrays["alibi"] = pen.reshape(2, PAIRS, P, 256).transpose(1, 2, 0, 3)
    for layer in range(2):
        wi = tiles(g["ffn_w_in"][layer]).reshape(2, GROUPS, 2, P, D_MODEL).transpose(1, 2, 0, 3, 4).reshape(GROUPS, 4, P, 1024)
        wo = g["ffn_w_out"][layer].reshape(GROUPS, 2, P, 2, 4, P).transpose(0, 3, 2, 4, 1, 5).reshape(GROUPS, 2, P, 1024)
        order = [wi[0]] + [z for k in range(1, GROUPS) for z in (wi[k], wo[k - 1])] + [wo[GROUPS - 1]]
        arrays[f"ffn_w{layer}"] = np.concatenate(order)
        pr = np.concatenate([g["ffn_conv_w"][layer], g["ffn_conv_b"][layer][None], g["state_ffn_conv"][layer, 0]])
        arrays[f"ffn_p{layer}"] = pr.reshape(6, 2, GROUPS, 2, P).transpose(2, 4, 3, 1, 0).reshape(GROUPS, P, 4, 6)
    arrays = {k: np.ascontiguousarray(v, dtype=v.dtype) for k, v in arrays.items()}

    outs = {"y": (P, KT, T), "ckv": (P, 2, SEQ), "ckvs": (P, 2, DEC_SEQ), "kpe": (C_ROPE, SEQ), "kpes": (C_ROPE, DEC_SEQ),
            "dk": (P, P), "dv": (P, P), "dks": (P, P), "dvs": (P, P)}
    for kv in "kv":
        outs |= {f"a{kv}": (PAIRS, P, 512), f"a{kv}s": (PAIRS, P, PAST), f"b{kv}": (PAIRS, P, SEQ), f"b{kv}s": (PAIRS, P, DEC_SEQ)}
    for layer in range(2):
        outs[f"tails{layer}"] = (GROUPS, P, 8, 2)

    nc = bacc.Bacc("TRN2", target_bir_lowering=False, num_devices=1)
    ap = {k: nc.dram_tensor(f"in_{k}", a.shape, mybir.dt.from_np(a.dtype), kind="ExternalInput").ap() for k, a in arrays.items()}
    ap |= {f"o_{k}": nc.dram_tensor(f"out_{k}", s, F32, kind="ExternalOutput").ap() for k, s in outs.items()}
    program(nc, ap)
    r = run_bass_kernel_spmd(nc, [{f"in_{k}": a for k, a in arrays.items()}], core_ids=[0]).results[0]
    r = {k: np.asarray(r[f"out_{k}"]) for k in outs}

    y = r["y"].transpose(2, 1, 0).reshape(T, D_MODEL)
    rows = lambda z, heads: np.moveaxis(z, -1, 0).reshape(1, 1, z.shape[-1], heads, HEAD)
    seq = lambda z: z.transpose(2, 1, 0).reshape(1, 1, z.shape[2], C_KV)
    tails = [r[f"tails{l}"].reshape(GROUPS, P, 2, 2, 2, 2).transpose(4, 5, 3, 0, 2, 1).reshape(2, 2, 2 * D_FF) for l in range(2)]
    conv = [np.stack([t[s] for t in tails])[:, None] for s in range(2)]
    return (y[None, :SEQ], y[None, S0:],
            rows(r["ak"], 8), rows(r["av"], 8), rows(r["aks"], 8), rows(r["avs"], 8),
            rows(r["bk"], 8), rows(r["bv"], 8), rows(r["bks"], 8), rows(r["bvs"], 8),
            seq(r["ckv"]), r["kpe"].T[None, None], seq(r["ckvs"]), r["kpes"].T[None, None],
            rows(r["dk"], 2), rows(r["dv"], 2), rows(r["dks"], 2), rows(r["dvs"], 2),
            conv[0], conv[1])


def program(nc, ap):
    io = Mem()
    io.x, io.gains, io.w0, io.w1, io.c_q, io.c_kv, io.w1_out = (ap[k] for k in ("x", "gains", "w0", "w1", "c_q", "c_kv", "w1_out"))
    io.cache_c, io.cache_pe, io.cache_dk, io.cache_dv = (ap[f"cache_{k}"] for k in ("c", "pe", "dk", "dv"))
    io.rot, io.alibi, io.bias = ap["rot"], ap["alibi"], ap["bias"]
    io.y, io.ckv, io.ckvs, io.kpe, io.kpes = (ap[f"o_{k}"] for k in ("y", "ckv", "ckvs", "kpe", "kpes"))
    io.dk, io.dv, io.dks, io.dvs = (ap[f"o_{k}"] for k in ("dk", "dv", "dks", "dvs"))
    io.sinks = bass.AP(ap["sinks"].tensor, 0, [[1, PAIRS], [0, P], [PAIRS, 2]])
    io.caches = {n.upper(): tuple(ap[k] for k in (f"cache_{n}k", f"cache_{n}v", f"o_{n}k", f"o_{n}v", f"o_{n}ks", f"o_{n}vs"))
                 + ((SEQ - 512, SEQ + DEC_SEQ) if n == "a" else (0, SEQ + PAST)) for n in "ab"}
    io.ffn_w = [ap["ffn_w0"], ap["ffn_w1"]]
    io.ffn_p = [ap["ffn_p0"], ap["ffn_p1"]]
    io.tails = [ap["o_tails0"], ap["o_tails1"]]
    build(nc, io)
```

```python
from contextlib import ExitStack

import concourse.bass as bass
from concourse import mybir

ALU = mybir.AluOpType
ACT = mybir.ActivationFunctionType
AX = mybir.AxisListType
F32 = mybir.dt.float32
F32R = mybir.dt.float32r

P = 128
D_MODEL, SEQ, DEC_SEQ, PAST = 1024, 1024, 64, 256
KT = D_MODEL // P
HEAD = 64
PAIRS = 4
CHUNK = 64
D_FF = 2816
GAP = 2
S0 = SEQ + GAP
T = S0 + DEC_SEQ
CUTS = [(0, 384), (384, 768), (768, T)]
KEYS = SEQ + PAST + DEC_SEQ
D_CACHE = 128
KEYS_D = SEQ + D_CACHE + DEC_SEQ
NQT = SEQ // P + 1
UNITS = 2 * NQT
MASKED = -1e30
EPS = 1e-6
C_Q, C_KV, C_ROPE, C_NOPE = 384, 256, 32, 64
C_SCALE = float(C_NOPE + C_ROPE) ** -0.5
SCALE = float(HEAD) ** -0.5
GROUPS = D_FF // 256
GAIN_MIX, GAIN_FFN, GAIN_FINAL, GAIN_Q, GAIN_KV, N_GAINS = (0, KT), (2 * KT, 3 * KT), 4 * KT, 5 * KT, 5 * KT + 3, 5 * KT + 5


def bank_of(n):
    return (n % 4) // 2, 512 * (n % 2)


class Norm:

    def __init__(self, nc, ctx, mem, name, src, cols, tiles, width, gain0, dst=None, split=None):
        self.nc, self.mem, self.src, self.cols, self.tiles = nc, mem, src, cols, tiles
        self.width, self.gain0, self.dst, self.split = width, gain0, dst, split
        sem = lambda s: mem.sem(f"{name}_{s}")
        self.squared, self.summed = sem("squared"), sem("summed")
        self.var, self.std, self.inv = sem("var"), sem("std"), sem("inv")
        self.normed = sem("normed")
        if split:
            self.high, self.low_v, self.low_p = sem("high"), sem("low_v"), sem("low_p")
        self.items = [(c, k) for c in range(len(cols)) for k in range(tiles)]

    def scalar(self, e):
        m = self.mem
        for i, (c, k) in enumerate(self.items):
            a, b = self.cols[c]
            if i >= 4:
                e.wait_ge(self.summed, i - 3)
            e.activation(m.sq[:, i % 4, 0:b - a], self.src(k, a, b), ACT.Square).then_inc(self.squared, 1)
        for c, (a, b) in enumerate(self.cols):
            e.wait_ge(self.var, c + 1)
            e.activation(m.rms[:, c, 0:b - a], m.rms[:, c, 0:b - a], ACT.Sqrt).then_inc(self.std, 1)
        if self.split:
            for i, (c, k) in enumerate(self.items):
                a, b = self.cols[c]
                e.wait_ge(self.normed, i + 1)
                e.activation(self.split[0][:, k, a:b], m.tmp[:, i % 4, 0:b - a], ACT.Copy).then_inc(self.high, 1)

    def tensor(self, e):
        m = self.mem
        for i, (c, k) in enumerate(self.items):
            a, b = self.cols[c]
            e.wait_ge(self.squared, i + 1)
            pb, off = bank_of(c)
            e.matmul(m.ps[pb][:, off:off + b - a], m.ones[:, :], m.sq[:, i % 4, 0:b - a],
                     start=k == 0, stop=k == self.tiles - 1).then_inc(self.summed, 1)

    def low(self, e, i, sem):
        c, k = self.items[i]
        a, b = self.cols[c]
        e.wait_ge(self.high, i + 1)
        e.tensor_tensor(self.split[1][:, k, a:b], self.mem.tmp[:, i % 4, 0:b - a],
                        self.split[0][:, k, a:b].bitcast(F32), ALU.subtract).then_inc(sem, 1)

    def vector(self, e):
        m = self.mem
        for c, (a, b) in enumerate(self.cols):
            e.wait_ge(self.summed, self.tiles * (c + 1))
            pb, off = bank_of(c)
            e.tensor_scalar(m.rms[:, c, 0:b - a], m.ps[pb][:, off:off + b - a], 1.0 / self.width, EPS,
                            ALU.mult, ALU.add).then_inc(self.var, 1)
        for i, (c, k) in enumerate(self.items):
            a, b = self.cols[c]
            if k == 0:
                e.wait_ge(self.std, c + 1)
                e.reciprocal(m.rms[:, c, 0:b - a], m.rms[:, c, 0:b - a]).then_inc(self.inv, 1)
                e.wait_ge(self.inv, c + 1)
            g = m.gains[:, self.gain0 + k:self.gain0 + k + 1]
            if self.split:
                if i >= 4:
                    e.wait_ge(self.low_p if i % 2 else self.low_v, (i - 4) // 2 + 1)
                out = m.tmp[:, i % 4, 0:b - a]
            else:
                out = self.dst(k, a, b)
            e.scalar_tensor_tensor(out, self.src(k, a, b), g, m.rms[:, c, 0:b - a],
                                   ALU.mult, ALU.mult).then_inc(self.normed, 1)
            if self.split and i % 2 == 1:
                self.low(e, i - 1, self.low_v)
        e.wait_ge(self.normed, len(self.items))

    def gpsimd(self, e):
        if self.split:
            for i in range(1, len(self.items), 2):
                self.low(e, i, self.low_p)


class Stream:
    STEPS = UNITS + 1

    def __init__(self, nc, mem, name, what, base, ring, pairs):
        self.m, self.what, self.base, self.ring, self.pairs = mem, what, base, ring, pairs
        self.latent = "qn" in what
        self.results = [(w, x, c) for w, x in enumerate(what) for c in range(3)]
        self.by = ["v" if x == "qr" or n % 2 else "s" for n, (w, x, c) in enumerate(self.results)]
        sem = lambda s: mem.sem(f"{name}_{s}")
        self.left_s, self.left_v = sem("left_by_scalar"), sem("left_by_vector")
        self.moved_s, self.moved_v = sem("moved_by_scalar"), sem("moved_by_vector")
        self.roped = sem("rope_parts")
        self.pieces = [(n, k) for n, (w, x, c) in enumerate(self.results) for k in range(self.depth(x))]

    def depth(self, what):
        return {"q": KT, "k": KT, "v": KT}[what] if not self.latent else (C_Q // P if what[0] == "q" else C_KV // P)

    def source(self, what):
        return self.m.hn if not self.latent else (self.m.cq if what[0] == "q" else self.m.ckv)

    def cut(self, what, c):
        return CUTS[c] if not self.latent or what[0] == "q" else (448 * c, 448 * c + 448)

    def wait_left(self, e, p, n):
        for who, s in (("s", self.left_s), ("v", self.left_v)):
            c = self.by[:n].count(who)
            if c:
                e.wait_ge(s, p * self.by.count(who) + c)

    def wait_moved(self, e, p):
        e.wait_ge(self.moved_s, p + 1)
        e.wait_ge(self.moved_v, p + 1)

    def products(self, e, p, lo, hi):
        m = self.m
        for n, k in self.pieces[lo:hi]:
            w, what, c = self.results[n]
            a, b = self.cut(what, c)
            if k == 0:
                if c == 0:
                    unit = self.base // 3 + w
                    e.wait_ge(m.w_in[unit % self.ring], p * (16 * len(self.what) // self.ring) + 16 * (unit // self.ring + 1))
                if n:
                    e.wait_ge(self.left_s if self.by[n - 1] == "s" else self.left_v,
                              p * self.by.count(self.by[n - 1]) + self.by[:n].count(self.by[n - 1]))
            last = k == self.depth(what) - 1
            mm = e.matmul(m.pnext[:, 0:b - a], m.w[:, (self.base // 3 + w) % self.ring, k * P:(k + 1) * P],
                          self.source(what)[:, k, a:b], start=k == 0, stop=last)
            if last:
                mm.then_inc(m.proj_ready, 1)

    def leave(self, e, who, p, n, out_sem=None):
        m = self.m
        w, what, c = self.results[n]
        a, b = self.cut(what, c)
        src = m.pnext[:, 0:b - a]
        sem = self.left_s if who == "s" else self.left_v
        e.wait_ge(m.proj_ready, p * len(self.results) + self.base + n + 1)

        def move(dst, src, scale=1.0):
            if who == "s":
                return e.activation(dst, src, ACT.Copy, scale=scale)
            return e.tensor_scalar(dst, src, scale, None, ALU.mult) if scale != 1.0 else e.tensor_copy(dst, src)

        if what == "qr":
            x = m.ropes[:, 0, 0:b - a]
            y = m.ropes[:, 1, 0:b - a]
            e.tensor_tensor(x, src[0:64, :], m.rot[0:64, a:b], ALU.mult)
            e.tensor_tensor(y, src[64:128, :], m.rot[64:128, a:b], ALU.mult).then_inc(self.roped, 1)
            e.wait_ge(self.roped, p * 3 + c + 1)
            e.tensor_tensor(m.qr_next[0:64, a:b], x, y, ALU.add).then_inc(sem, 1)
            e.wait_ge(sem, p * self.by.count("v") + self.by[:n + 1].count("v"))
        elif what in ("q", "qn"):
            move(m.q_next[:, a:b], src, SCALE if what == "q" else 1.0).then_inc(sem, 1)
        elif self.latent:
            dst = m.k_next if what == "kn" else m.vt
            move(dst[:, a:b], src).then_inc(sem, 1)
        else:
            dst = m.k_next if what == "k" else m.vt
            if c < 2:
                move(dst[:, a:b], src).then_inc(sem, 1)
            else:
                move(dst[:, a:SEQ], src[:, 0:SEQ - a])
                move(dst[:, KEYS - DEC_SEQ:KEYS], src[:, S0 - a:b - a]).then_inc(sem, 1)

    def move_scalar(self, e, p):
        m = self.m
        self.wait_left(e, p, len(self.results))
        if self.latent:
            e.activation(m.qh[0][0:HEAD, :], m.q_next[0:HEAD, :], ACT.Copy)
            e.activation(m.qh[1][0:HEAD, :], m.q_next[HEAD:P, :], ACT.Copy).then_inc(self.moved_s, 1)
        else:
            e.activation(m.q[:, :], m.q_next[:, :], ACT.Copy).then_inc(self.moved_s, 1)

    def move_vector(self, e, p):
        m = self.m
        self.wait_left(e, p, len(self.results))
        if self.latent:
            for h in range(2):
                e.tensor_copy(m.kh[h][0:HEAD, :], m.k_next[HEAD * h:HEAD * h + HEAD, :])
                ins = e.tensor_copy(m.qh[h][HEAD:HEAD + C_ROPE, :], m.qr_next[C_ROPE * h:C_ROPE * h + C_ROPE, :])
            ins.then_inc(self.moved_v, 1)
        else:
            e.tensor_copy(m.k[:, :], m.k_next[:, :]).then_inc(self.moved_v, 1)

    def first(self, e, who):
        for n, by in enumerate(self.by):
            if by == who:
                self.leave(e, who, 0, n)

    def share(self, step):
        if step < 0:
            return 0
        count = len(self.results)
        n = next(n for n in range(count) if (n + 1) * self.STEPS // count > step)
        first, end = n * self.STEPS // count, (n + 1) * self.STEPS // count
        before = sum(self.depth(x) for _, x, _ in self.results[:n])
        return before + -(-self.depth(self.results[n][1]) * (step + 1 - first) // (end - first))

    def done_by(self, step):
        count = len(self.results)
        return sum(1 for n in range(count) if (n + 1) * self.STEPS // count <= step)


class Attend:

    def __init__(self, nc, mem, kind, otile, io, stream=None, first=0):
        self.nc, self.m, self.kind, self.otile, self.io = nc, mem, kind, otile, io
        self.stream, self.p0 = stream, first
        self.tail = None
        sem = lambda s: mem.sem(f"{kind}_{s}")
        self.opened = sem("opened")
        if kind in "AB":
            self.kv_out = nc.alloc_semaphore(f"{kind}_kv_out")
        if kind in "AD":
            self.strip_in = nc.alloc_semaphore(f"{kind}_strip_in")
        self.strip_masked = sem("strip_masked")
        self.turned, self.back_s, self.back_v = sem("turned"), sem("turned_read_by_scalar"), sem("turned_read_by_vector")
        self.scores = sem("scores")
        self.v1, self.front, self.mid1, self.mid = sem("vector_part"), sem("front"), sem("mid_part"), sem("mid")
        self.s1, self.logs, self.probs = sem("scalar_part"), sem("logs"), sem("probs")
        self.out, self.inv, self.normed = sem("out"), sem("inverse"), sem("normed")
        self.qcopied = sem("q_copied")
        self.uses = []
        if kind != "D":
            for blocks in ((0, 1, 2, 3), (4, 5, 6, 7), (8, 9), (10,)):
                self.uses.append(("v", blocks))
        self.unit_uses, self.out_use = [], {}
        for u in range(UNITS):
            nb = len(self.blocks(u))
            mine = []
            for g in range(0, nb, 4):
                mine.append(len(self.uses))
                self.uses.append((u, tuple(range(g, min(g + 4, nb)))))
            self.unit_uses.append(mine)
            if u >= 2 and u % 2 == 0:
                self.out_use[u // 2 - 1] = len(self.uses)
                self.uses.append(("o", (u // 2 - 1,)))
        self.out_use[NQT - 1] = len(self.uses)
        self.uses.append(("o", (NQT - 1,)))
        self.use_by = []
        for n, (u, bl) in enumerate(self.uses):
            if u == "v":
                self.use_by.append("s" if n % 2 == 0 else "v")
            elif u == "o" or kind == "B":
                self.use_by.append("s")
            else:
                self.use_by.append("v" if bl[0] >= 4 else "s")

    def keys(self, u):
        t = u // 2
        if t == NQT - 1:
            return (SEQ, KEYS_D) if self.kind == "D" else (SEQ, KEYS)
        back = {"A": 512, "D": 128, "B": SEQ, "C": SEQ}[self.kind]
        return max(0, P * t - back), P * t + P

    def nq(self, u):
        return DEC_SEQ if u // 2 == NQT - 1 else P

    def qcol(self, u):
        return S0 if u // 2 == NQT - 1 else P * (u // 2)

    def blocks(self, u):
        a, b = self.keys(u)
        return [(k, min(P, b - k)) for k in range(a, b, P)]

    def strip0(self, u):
        if self.kind == "A":
            return 256 if u // 2 == NQT - 1 else self.keys(u)[0] - (P * (u // 2) - 512)
        return 0 if u // 2 == NQT - 1 else self.keys(u)[0] - (P * (u // 2) - 128)

    def count(self, listing, n, who):
        return sum(1 for x in listing[:n] if x == who)

    def wait_back(self, e, j, n):
        for who, s in (("s", self.back_s), ("v", self.back_v)):
            c = self.count(self.use_by, n, who)
            if c:
                e.wait_ge(s, j * self.use_by.count(who) + c)

    def wait_turned_unit(self, e, j, u):
        e.wait_ge(self.turned, j * len(self.uses) + self.unit_uses[u][-1] + 1)

    def open(self, e, j):
        e.drain().then_inc(self.opened, 1)
        e.wait_ge(self.opened, j * 4 + 4)

    def wait_output(self, e, j, t):
        e.wait_ge(self.turned, j * len(self.uses) + self.out_use[t] + 1)

    def wait_all(self, e):
        e.wait_ge(self.back_s, PAIRS * self.use_by.count("s"))

    def pairs(self, e, body, last=False):
        if body == self.scalar:
            e.preload_act_table_set("natural_log_exp_and_others")
        if last:
            with e.Fori(0, PAIRS - 1) as j:
                body(e, j, True)
            body(e, PAIRS - 1, False)
        else:
            with e.Fori(0, PAIRS) as j:
                body(e, j, self.stream is not None)

    def tensor(self, e, j, more):
        m, st = self.m, self.stream
        self.open(e, j)
        if st:
            st.wait_left(e, j + self.p0, len(st.results))
            if self.kind != "C":
                e.wait_ge(m.cache_in, (j + self.p0) * 32 + 32)
            st.wait_moved(e, j + self.p0)
        else:
            e.wait_ge(self.qcopied, j + 1)
        for step in range(-1, UNITS + 2):
            if step + 1 < UNITS:
                self.pe_scores(e, j, step + 1)
            if step == -1 and st:
                self.pe_turn_v(e, j)
            if 1 <= step <= UNITS:
                self.pe_out(e, j, step - 1)
            if step >= 3 and step % 2:
                self.pe_turn_out(e, j, (step - 3) // 2)
            if more and step < UNITS:
                lo, hi = st.share(step), st.share(step + 1)
                mid = (lo + hi) // 2
                st.products(e, j + self.p0 + 1, lo, mid)
            elif self.tail and 0 <= step < UNITS:
                lo, hi = self.tail.share(step - 1) if step else 0, self.tail.share(step)
                mid = (lo + hi) // 2
                self.tail.products(e, j if self.kind == "D" else 0, lo, mid)
            if 0 <= step < UNITS:
                self.pe_turn(e, j, step)
            if more and step < UNITS:
                st.products(e, j + self.p0 + 1, mid, hi)
            elif self.tail and 0 <= step < UNITS:
                self.tail.products(e, j if self.kind == "D" else 0, mid, hi)

    def pe_turn_out(self, e, j, t):
        m = self.m
        nq, r = self.nq(2 * t), self.out_use[t]
        e.wait_ge(self.normed, j * NQT + t + 1)
        self.wait_back(e, j, r - 1)
        m.apart(e)
        e.transpose(m.pst[r % 2][:, 0:nq], m.otok[0:nq, :], m.ident[0:nq, 0:nq]).then_inc(self.turned, 1)

    def pe_turn_v(self, e, j):
        m = self.m
        for r in range(4):
            blocks = self.uses[r][1]
            if r >= 2:
                self.wait_back(e, j, r - 1)
            m.apart(e)
            for i, blk in enumerate(blocks):
                kw = min(P, KEYS - P * blk)
                mm = e.transpose(m.pst[r % 2][0:kw, P * i:P * i + P], m.vt[:, P * blk:P * blk + kw], m.ident[:, :])
            mm.then_inc(self.turned, 1)

    def pe_scores(self, e, j, u):
        m, hh = self.m, u % 2
        a, b = self.keys(u)
        nq, q0 = self.nq(u), self.qcol(u)
        if u >= 2:
            e.wait_ge({"A": self.front, "D": self.front, "B": self.mid, "C": self.probs}[self.kind], j * UNITS + u - 1)
        if self.kind == "C":
            q, k = m.qh[hh], m.kh[hh]
            lo, hi = 0, C_NOPE + C_ROPE
        else:
            q, k = m.q, (m.kd if self.kind == "D" else m.k)
            lo, hi = HEAD * hh, HEAD * hh + HEAD
        if nq < P:
            m.apart(e)
        for c in range(0, b - a, 512):
            n = min(512, b - a - c)
            mm = e.matmul(m.ps[u % 2][0:nq, c:c + n], q[lo:hi, q0:q0 + nq], k[lo:hi, a + c:a + c + n], start=True, stop=True)
        mm.then_inc(self.scores, 1)

    def pe_turn(self, e, j, u):
        m, nq = self.m, self.nq(u)
        e.wait_ge(self.probs, j * UNITS + u + 1)
        for r in self.unit_uses[u]:
            if r >= 2:
                self.wait_back(e, j, r - 1)
            m.apart(e)
            for i, blk in enumerate(self.uses[r][1]):
                kw = self.blocks(u)[blk][1]
                mm = e.transpose(m.pst[r % 2][0:kw, P * i:P * i + nq], m.wk[0:nq, u % 2, P * blk:P * blk + kw],
                                 m.ident[0:nq, 0:nq])
            mm.then_inc(self.turned, 1)

    def pe_out(self, e, j, u):
        m, nq, hh = self.m, self.nq(u), u % 2
        self.wait_back(e, j, self.unit_uses[u][-1] + 1)
        if hh == 0 and u >= 2:
            e.wait_ge(self.normed, j * NQT + u // 2)
        bl = self.blocks(u)
        v = m.vtok_d if self.kind == "D" else m.vtok
        m.apart(e)
        for i, (k, kw) in enumerate(bl):
            mm = e.matmul(m.po[0:nq, HEAD * hh:HEAD * hh + HEAD], m.pt[0:kw, P * i:P * i + nq],
                          v[0:kw, k // P, HEAD * hh:HEAD * hh + HEAD], start=i == 0, stop=i == len(bl) - 1,
                          skip_group_check=True)
        mm.then_inc(self.out, 1)

    def scalar(self, e, j, more):
        m, kind, st = self.m, self.kind, self.stream
        self.open(e, j)
        if st:
            st.move_scalar(e, j + self.p0)
        else:
            e.activation(m.q[:, :], m.o[:, bass.ds(j + self.otile, 1), :], ACT.Copy).then_inc(self.qcopied, 1)
        if more:
            st.wait_moved(e, j + self.p0)
        for step in range(-1, UNITS + 2):
            self.leave_next(e, "s", j, step, more)
            if kind == "B" and 0 <= step < UNITS:
                nq, w = self.nq(step), self.keys(step)[1] - self.keys(step)[0]
                e.wait_ge(self.mid, j * UNITS + step + 1)
                e.activation(m.wk[0:nq, step % 2, 0:w], m.wk[0:nq, step % 2, 0:w], ACT.Exp).then_inc(self.probs, 1)
            if step + 1 < UNITS:
                self.sc_weights(e, j, step + 1)
            if step == -1:
                self.read_v(e, "s", j)
            if step >= 3 and step % 2 == 1:
                self.sc_output(e, j, (step - 3) // 2)
            if 0 <= step < UNITS:
                for r in self.unit_uses[step]:
                    if self.use_by[r] == "s":
                        self.read_turned(e, "s", j, r)

    def leave_next(self, e, who, j, step, more):
        st = self.stream
        if more and 0 <= step <= UNITS:
            for n in range(st.done_by(step), st.done_by(step + 1)):
                if st.by[n] == who:
                    if st.results[n][1] == "v":
                        self.wait_v_free(e, j)
                    st.leave(e, who, j + self.p0 + 1, n)

    def wait_v_free(self, e, j):
        e.wait_ge(self.turned, j * len(self.uses) + 4)
        if self.kind in "AB":
            e.wait_ge(self.kv_out, j * 64 + 64)

    def sc_output(self, e, j, t):
        m = self.m
        nq, q0, r = self.nq(2 * t), self.qcol(2 * t), self.out_use[t]
        e.wait_ge(self.turned, j * len(self.uses) + r + 1)
        m.apart(e)
        e.activation(m.o[:, bass.ds(j + self.otile, 1), q0:q0 + nq], m.pst[r % 2][:, 0:nq], ACT.Copy).then_inc(self.back_s, 1)

    def sc_weights(self, e, j, u):
        m, kind = self.m, self.kind
        nq, w = self.nq(u), self.keys(u)[1] - self.keys(u)[0]
        wk = m.wk[0:nq, u % 2, 0:w]
        s8 = u % 8
        total = m.rowsum[0:nq, s8:s8 + 1]
        neg = m.negmax[0:nq, u % 2:u % 2 + 1]
        e.wait_ge(self.front, j * UNITS + u + 1)
        if kind == "B":
            e.activation(wk, wk, ACT.Exp).then_inc(self.s1, 1)
            e.wait_ge(self.s1, j * UNITS + u + 1)
            e.activation(wk, wk, ACT.Ln, bias=1.0).then_inc(self.logs, 1)
        elif kind == "C":
            if u >= 2:
                self.wait_turned_unit(e, j, u - 2)
            e.activation(wk, m.ps[u % 2][0:nq, 0:w], ACT.Exp, bias=neg, scale=C_SCALE, accum_out=total).then_inc(self.probs, 1)
        else:
            if kind == "D":
                e.activation(m.esink[0:nq, s8:s8 + 1], m.sink[0:nq, u % 2:u % 2 + 1], ACT.Exp, bias=neg)
            e.activation(wk, wk, ACT.Exp, bias=neg, accum_out=total).then_inc(self.probs, 1)

    def read_turned(self, e, who, j, r):
        m = self.m
        u, bl = self.uses[r]
        bank = m.pst[r % 2]
        e.wait_ge(self.turned, j * len(self.uses) + r + 1)
        sem = self.back_s if who == "s" else self.back_v

        def move(dst, src):
            return e.activation(dst, src, ACT.Copy) if who == "s" else e.tensor_copy(dst, src)

        if u == "v":
            rows = min(P, KEYS - P * bl[0])
            move(m.vtok[0:rows, bl[0]:bl[-1] + 1, :],
                 bank[0:rows, 0:P * len(bl)].rearrange("p (b f) -> p b f", f=P)).then_inc(sem, 1)
            return
        nq = self.nq(u)
        kws = [self.blocks(u)[b][1] for b in bl]
        full = [b for b, kw in zip(bl, kws) if kw == P]
        ops = []
        if nq == P:
            ops.append((m.pt[:, P * bl[0]:P * (bl[-1] + 1)], bank[:, 0:P * len(bl)]))
        else:
            n = len(full)
            v = lambda x: x.rearrange("p (b f) -> p b f", f=P)[:, :, 0:nq]
            ops.append((v(m.pt[:, P * bl[0]:P * (bl[0] + n)]), v(bank[:, 0:P * n])))
            if len(full) < len(bl):
                ops.append((m.pt[0:HEAD, P * (bl[0] + n):P * (bl[0] + n) + nq], bank[0:HEAD, P * n:P * n + nq]))
        for dst, src in ops:
            ins = move(dst, src)
        ins.then_inc(sem, 1)

    def read_v(self, e, who, j):
        for r, (u, _) in enumerate(self.uses):
            if u == "v" and self.use_by[r] == who:
                self.read_turned(e, who, j, r)

    def vector(self, e, j, more):
        m, kind, st = self.m, self.kind, self.stream
        self.open(e, j)
        if st:
            if kind != "C":
                e.wait_ge(m.cache_in, (j + self.p0) * 32 + 32)
            st.move_vector(e, j + self.p0)
        if kind == "A":
            e.wait_ge(self.strip_in, j * 16 + 16)
            e.memset(m.strip[0:64, :, 576:640], MASKED)
            e.memset(m.strip[64:128, :, 0:64], MASKED).then_inc(self.strip_masked, 1)
        if kind in "D":
            e.wait_ge(self.strip_in, j * 32 + 32)
        if kind == "A":
            e.wait_ge(self.strip_masked, j + 1)
        if more:
            st.wait_moved(e, j + self.p0)
        for step in range(-1, UNITS + 1):
            self.leave_next(e, "v", j, step, more)
            if not more and self.tail:
                self.tail.leave(e, j if kind == "D" else 0, step)
            if kind == "B" and 0 <= step < UNITS:
                self.ve_sticks(e, j, step)
            if step + 1 < UNITS:
                self.ve_front(e, j, step + 1)
            if step == -1:
                self.read_v(e, "v", j)
            if step >= 1 and step % 2 == 0:
                self.ve_normalise(e, j, step // 2 - 1)
            if 0 <= step < UNITS:
                for r in self.unit_uses[step]:
                    if self.use_by[r] == "v":
                        self.read_turned(e, "v", j, r)

    def ve_front(self, e, j, u):
        m, kind = self.m, self.kind
        nq, w = self.nq(u), self.keys(u)[1] - self.keys(u)[0]
        t = u // 2
        ps = m.ps[u % 2]
        wk = m.wk[0:nq, u % 2, 0:w]
        mx, neg = m.mx[0:nq, u % 2:u % 2 + 1], m.negmax[0:nq, u % 2:u % 2 + 1]
        e.wait_ge(self.scores, j * UNITS + u + 1)
        if u >= 2:
            self.wait_turned_unit(e, j, u - 2)
        if kind in "AD":
            s0 = self.strip0(u)
            m.apart(e)
            e.tensor_tensor_reduce(wk, ps[0:nq, 0:w], m.strip[0:nq, u % 2, s0:s0 + w], 1.0, -3e38,
                                   ALU.add, ALU.max, mx).then_inc(self.v1, 1)
            e.wait_ge(self.v1, j * UNITS + u + 1)
            if kind == "A":
                e.tensor_scalar(neg, mx, -1.0, None, ALU.mult).then_inc(self.front, 1)
            else:
                e.tensor_scalar(neg, mx, m.sink[0:nq, u % 2:u % 2 + 1], -1.0, ALU.max, ALU.mult).then_inc(self.front, 1)
        elif kind == "C":
            if t < NQT - 1:
                e.memset(ps[0:64, w - CHUNK:w], MASKED).then_inc(self.v1, 1)
                e.wait_ge(self.v1, j * 2 * (NQT - 1) + u + 1)
            e.tensor_reduce(mx, ps[0:nq, 0:w], AX.X, ALU.max).then_inc(self.mid1, 1)
            e.wait_ge(self.mid1, j * UNITS + u + 1)
            e.tensor_scalar(neg, mx, -C_SCALE, None, ALU.mult).then_inc(self.front, 1)
        else:
            d = min(P, nq)
            e.tensor_tensor(ps[0:nq, w - d:w], ps[0:nq, w - d:w], m.causal[0:nq, 0:d], ALU.add).then_inc(self.v1, 1)
            e.wait_ge(self.v1, j * UNITS + u + 1)
            e.tensor_scalar(wk, ps[0:nq, 0:w], 44.0, None, ALU.min).then_inc(self.front, 1)

    def ve_sticks(self, e, j, u):
        m = self.m
        nq, w = self.nq(u), self.keys(u)[1] - self.keys(u)[0]
        wk, run = m.wk[0:nq, u % 2, 0:w], m.run[0:nq, 0:w]
        z = m.ps[u % 2][0:nq, 0:w]
        e.wait_ge(self.logs, j * UNITS + u + 1)
        e.tensor_tensor(wk, z, wk, ALU.max).then_inc(self.mid1, 1)
        e.wait_ge(self.mid1, j * (2 * UNITS) + 2 * u + 1)
        if u:
            e.wait_ge(self.mid, j * UNITS + u)
        e.tensor_tensor_scan(run[:, ::-1], wk[:, ::-1], wk[:, ::-1], 0.0, ALU.add, ALU.max).then_inc(self.mid1, 1)
        e.wait_ge(self.mid1, j * (2 * UNITS) + 2 * u + 2)
        e.tensor_tensor(wk, z, run, ALU.subtract).then_inc(self.mid, 1)

    def ve_normalise(self, e, j, t):
        m, kind = self.m, self.kind
        nq = self.nq(2 * t)
        e.wait_ge(self.out, j * UNITS + 2 * t + 2)
        if t >= 1:
            self.wait_output(e, j, t - 1)
        if kind == "B":
            e.tensor_copy(m.otok[0:nq, :], m.po[0:nq, 0:P]).then_inc(self.normed, 1)
            return
        s8 = (2 * t) % 8
        total = m.rowsum[0:nq, s8:s8 + 2]
        per = 2 if kind == "D" else 1
        if kind == "D":
            e.tensor_tensor(total, total, m.esink[0:nq, s8:s8 + 2], ALU.add).then_inc(self.inv, 1)
            e.wait_ge(self.inv, j * per * NQT + per * t + 1)
        e.reciprocal(total, total).then_inc(self.inv, 1)
        e.wait_ge(self.inv, j * per * NQT + per * t + per)
        for hh in range(2):
            ins = e.tensor_scalar(m.otok[0:nq, HEAD * hh:HEAD * hh + HEAD], m.po[0:nq, HEAD * hh:HEAD * hh + HEAD],
                                  total[:, hh:hh + 1], None, ALU.mult)
        ins.then_inc(self.normed, 1)

    def gpsimd(self, e, j, more):
        m, kind, io, st = self.m, self.kind, self.io, self.stream
        self.open(e, j)
        if kind in "AB":
            ok, ov, oks, ovs, k0, s0 = io.stores[kind]
            st.wait_left(e, j + self.p0, len(st.results))
            e.wait_ge(m.cache_in, (j + self.p0) * 32 + 32)
            m.apart(e)
            for dst, a, b in ((ov, k0, SEQ), (ovs, s0, KEYS)):
                e.dma_start(dst[bass.ds(j, 1)].rearrange("a p c -> (a p) c"), m.vt[:, a:b]).then_inc(self.kv_out, 16)
            st.wait_moved(e, j + self.p0)
            m.apart(e)
            for dst, a, b in ((ok, k0, SEQ), (oks, s0, KEYS)):
                e.dma_start(dst[bass.ds(j, 1)].rearrange("a p c -> (a p) c"), m.k[:, a:b]).then_inc(self.kv_out, 16)
            if more:
                e.wait_ge(self.kv_out, j * 64 + 64)
                e.wait_ge(self.turned, j * len(self.uses) + 4)
                m.apart(e)
                load_caches(e, m, io, j + self.p0 + 1)
            else:
                e.wait_ge(self.kv_out, j * 64 + 64)
        if kind in "AD":
            e.wait_ge(self.front, j * UNITS + UNITS)
            e.wait_ge(self.probs, j * UNITS + UNITS)
            m.apart(e)
            self.load_strip(e, j + 1)

    def load_strip(self, e, j):
        m, io = self.m, self.io
        if self.kind == "A":
            e.dma_start(m.strip[:, :, :], io.bias[bass.ds(j, 1)].rearrange("a p h c -> p (a h) c")).then_inc(self.strip_in, 16)
        else:
            e.dma_start(m.strip[:, :, 0:256], io.alibi[bass.ds(j, 1)].rearrange("a p h c -> p (a h) c")).then_inc(self.strip_in, 16)
            with self.nc.allow_non_contiguous_dma(reason="two sinks per row"):
                e.dma_start(m.sink[:, :], io.sinks[bass.ds(j, 1)].rearrange("a p h -> p (a h)")).then_inc(self.strip_in, 16)


def load_caches(e, m, io, p):
    e.dma_start(m.k_next[:, SEQ:SEQ + PAST], io.cache_k[bass.ds(p, 1)].rearrange("a p c -> (a p) c")).then_inc(m.cache_in, 16)
    e.dma_start(m.vt[:, SEQ:SEQ + PAST], io.cache_v[bass.ds(p, 1)].rearrange("a p c -> (a p) c")).then_inc(m.cache_in, 16)


class Mem:
    pass


def weight_stream(e, m, parts, ring):
    n = 0
    for src, width, count in parts:
        done = 0
        if n == 0:
            for s in range(ring):
                e.dma_start(m.w[:, s, 0:width], src[s]).then_inc(m.w_in[s], 16)
            n, done = ring, ring
        loops = (count - done) // ring
        if loops:
            with e.Fori(0, loops) as i:
                for s in range(ring):
                    slot = (n + s) % ring
                    e.wait_ge(m.proj_ready, i * (3 * ring) + 3 * (n + s - ring + 1))
                    e.dma_start(m.w[:, slot, 0:width],
                                src[bass.ds(i * ring + done + s, 1)].rearrange("a p c -> (a p) c")).then_inc(m.w_in[slot], 16)
            n += loops * ring
            done += loops * ring
        while done < count:
            e.wait_ge(m.proj_ready, 3 * (n - ring + 1))
            e.dma_start(m.w[:, n % ring, 0:width], src[done]).then_inc(m.w_in[n % ring], 16)
            n, done = n + 1, done + 1


class Project:

    def __init__(self, nc, ctx, mem, name, base, ring, units, moving):
        self.m, self.base, self.ring, self.units, self.moving = mem, base, ring, units, moving
        self.left = mem.sem(f"{name}_left_psum")

    def tensor(self, e):
        m = self.m
        n = 0
        for w in range(self.units):
            unit = self.base // 3 + w
            e.wait_ge(m.w_in[unit % self.ring], 16 * (unit // self.ring + 1))
            for c, (a, b) in enumerate(CUTS):
                if n >= 4:
                    e.wait_ge(self.left, n - 3)
                pb, off = bank_of(n)
                for k in range(KT):
                    mm = e.matmul(m.ps[pb][:, off:off + b - a], m.w[:, unit % self.ring, k * P:(k + 1) * P],
                                  self.moving(k, a, b), start=k == 0, stop=k == KT - 1)
                mm.then_inc(m.proj_ready, 1)
                n += 1

    def results(self, e):
        m = self.m
        for n in range(3 * self.units):
            w, c = divmod(n, 3)
            a, b = CUTS[c]
            pb, off = bank_of(n)
            e.wait_ge(m.proj_ready, self.base + n + 1)
            yield n, w, c, a, b, m.ps[pb], off


class OutProject:

    def __init__(self, nc, mem, name, base, ring, filled, per_pair):
        self.m, self.base, self.ring, self.filled, self.per_pair = mem, base, ring, filled, per_pair
        self.looped = filled > per_pair // 3
        self.bank_free, self.left = mem.sem(f"{name}_bank_free"), mem.sem(f"{name}_left")
        self.steps = UNITS // per_pair
        self.half = KT // 2

    def share(self, step):
        n, s = divmod(step, self.steps)
        return self.half * n + -(-self.half * (s + 1) // self.steps)

    def products(self, e, j, lo, hi):
        m = self.m
        for i in range(lo, hi):
            n, k = divmod(i, self.half)
            c = n % 3
            a, b = CUTS[c]
            if k == 0:
                if c == 0:
                    e.wait_ge(m.w_in[self.slot(n // 3)], self.level(n // 3, j))
                e.wait_ge(self.bank_free, j * self.per_pair + n + 1)
            mm = e.matmul(m.pnext[:, 0:b - a], m.w[:, self.slot(n // 3), k * P:(k + 1) * P], m.o[:, k, a:b],
                          start=k == 0, stop=k == self.half - 1)
        if hi > lo and hi % self.half == 0:
            mm.then_inc(m.proj_ready, 1)

    def slot(self, w):
        if self.looped:
            return w % 2 if w < self.filled else (w - self.filled + 2) % 4
        return (self.base // 3 + w) % self.ring

    def level(self, w, j=0):
        if self.looped:
            before = self.base // 3 // self.ring
            if w < self.filled:
                return j * 16 + 16 * (before + 1)
            if self.slot(w) < 2:
                before += self.filled // 2
            return 16 * (before + (w - self.filled) // 4 + 1)
        return 16 * ((self.base // 3 + w) // self.ring + 1)

    def leave(self, e, j, step):
        m = self.m
        if step > 0 and step % self.steps == 0:
            n = step // self.steps - 1
            a, b = CUTS[n % 3]
            e.wait_ge(m.proj_ready, j * self.per_pair + self.base + n + 1)
            if self.looped:
                m.apart(e)
                x = m.x[:, bass.ds(j * 2 + n // 3, 1), a:b].rearrange("p a c -> p (a c)")
            else:
                x = m.x[:, n // 3, a:b]
            e.tensor_tensor(x, m.pnext[:, 0:b - a], x, ALU.add).then_inc(self.bank_free, 1)

    def tensor(self, e):
        m = self.m
        n = 0
        e.wait_ge(self.bank_free, 3 * self.filled + 1)
        for w in range(self.filled, 2 * KT):
            e.wait_ge(m.w_in[self.slot(w)], self.level(w))
            for a, b in CUTS:
                if n >= 4:
                    e.wait_ge(self.left, n - 3)
                pb, off = bank_of(n)
                for k in range(self.half):
                    mm = e.matmul(m.ps[pb][:, off:off + b - a], m.w[:, self.slot(w), k * P:(k + 1) * P],
                                  m.o[:, self.half * (w // KT) + k, a:b], start=k == 0, stop=k == self.half - 1)
                mm.then_inc(m.proj_ready, 1)
                n += 1

    def vector(self, e):
        m = self.m
        for n in range(3 * (2 * KT - self.filled)):
            w, c = self.filled + n // 3, n % 3
            a, b = CUTS[c]
            pb, off = bank_of(n)
            e.wait_ge(m.proj_ready, self.base + 3 * self.filled + n + 1)
            x = m.x[:, w % KT, a:b]
            e.tensor_tensor(x, m.ps[pb][:, off:off + b - a], x, ALU.add).then_inc(self.left, 1)


class Ffn:
    RING = 3

    def __init__(self, nc, ctx, mem, name, weights, params, tails):
        self.nc, self.m, self.weights, self.params, self.tails = nc, mem, weights, params, tails
        sem = lambda s: mem.sem(f"{name}_{s}")
        self.raw_in = [sem(f"raw_in{i}") for i in range(self.RING)]
        self.high, self.low = sem("weight_high"), sem("weight_low")
        self.par_in = [sem(f"params_in{i}") for i in range(2)]
        self.tails_out = sem("tails_out")
        self.up, self.left = sem("up"), sem("up_left_psum")
        self.c1, self.conv = sem("conv_part"), sem("conv")
        self.silu, self.gate, self.ghigh, self.glow = sem("silu"), sem("gate"), sem("gate_high"), sem("gate_low")
        self.down, self.banks_free = sem("down"), sem("down_banks_free")

    def sync(self, e):
        m = self.m
        for s in range(self.RING):
            e.dma_start(m.raw[:, s, :], self.weights[s]).then_inc(self.raw_in[s], 16)
        e.dma_start(m.par[:, 0, :, :], self.params[0]).then_inc(self.par_in[0], 16)
        e.wait_ge(self.low, 1)
        e.dma_start(m.raw[:, 0, :], self.weights[3]).then_inc(self.raw_in[0], 16)
        with e.Fori(0, (GROUPS - 1) // 2) as i:
            for s in range(12):
                n = 4 + s
                e.wait_ge(self.low, i * 12 + n - 2)
                e.dma_start(m.raw[:, n % 3, :], self.weights[bass.ds(i * 12 + n, 1)].rearrange("a p c -> (a p) c")).then_inc(self.raw_in[n % 3], 16)
                if s in (0, 6):
                    q = 1 if s == 0 else 0
                    e.wait_ge(self.conv, i * 8 + (1 if s == 0 else 4))
                    e.dma_start(m.par[:, q, :, :], self.params[bass.ds(i * 2 + (1 if s == 0 else 2), 1)].rearrange("a p t c -> (a p) t c")).then_inc(self.par_in[q], 16)
        for n in (64, 65):
            e.wait_ge(self.low, n - 2)
            e.dma_start(m.raw[:, n % 3, :], self.weights[n]).then_inc(self.raw_in[n % 3], 16)

    def pe_up(self, e, i, g):
        m = self.m
        for tile in range(4):
            n = tile if g == 0 else 4 + 6 * (g - 1) + tile
            e.wait_ge(self.low, i * 12 + n + 1)
            for c, (a, b) in enumerate(CUTS):
                q = 12 * g + 3 * tile + c
                if q >= 4:
                    e.wait_ge(self.left, i * 24 + q - 3)
                bank = m.ps4[q % 4]
                for k in range(KT):
                    for x, w, first in ((m.hh, m.wh, True), (m.hl, m.wh, False), (m.hh, m.wl, False)):
                        mm = e.matmul(bank[:, 0:b - a], w[:, n % 3, k * P:(k + 1) * P], x[:, k, a:b],
                                      start=k == 0 and first, stop=k == KT - 1 and w is m.wl)
                mm.then_inc(self.up, 1)

    def pe_down(self, e, i, g, last=False):
        m = self.m
        par = g % 2
        e.wait_ge(self.glow, i * 4 + 2 * g + 2)
        for mt in range(KT):
            n = (4 if last else 8) + 6 * g + mt // 4
            if mt % 4 == 0:
                e.wait_ge(self.low, i * 12 + n + 1)
            for c, (a, b) in enumerate(CUTS):
                q = 24 * g + 3 * mt + c
                e.wait_ge(self.banks_free, i * 48 + q + 1)
                bank = m.ps4[4 + q % 4]
                for k in range(2):
                    col = (mt % 4) * 2 * P + k * P
                    for x, w, first in ((m.gh, m.wh, True), (m.gl, m.wh, False), (m.gh, m.wl, False)):
                        mm = e.matmul(bank[:, 0:b - a], w[:, n % 3, col:col + P], x[:, 2 * par + k, a:b],
                                      start=k == 0 and first, stop=k == 1 and w is m.wl)
                mm.then_inc(self.down, 1)

    def tensor(self, e):
        self.pe_up(e, 0, 0)
        with e.Fori(0, (GROUPS - 1) // 2) as i:
            self.pe_up(e, i, 1)
            self.pe_down(e, i, 0)
            self.pe_up(e, i, 2)
            self.pe_down(e, i, 1)
        self.pe_down(e, (GROUPS - 1) // 2, 0, last=True)

    def wait_used(self, e, i, n):
        if n < 3:
            e.wait_ge(self.up, i * 24 + 3 * (n + 1))
            return
        if n == 3:
            e.wait_ge(self.up, i * 24 + 13)
            return
        g, s = divmod(n - 4, 6)
        if s < 4:
            e.wait_ge(self.up, i * 24 + 12 * (g + 1) + 3 * (s + 1))
        else:
            e.wait_ge(self.down, i * 48 + 24 * g + 12 * (s - 3))

    def sc_high(self, e, i, n):
        m = self.m
        s = n % 3
        e.wait_ge(self.raw_in[s], i * 64 + 16 * (n // 3 + 1))
        if n >= 3:
            self.wait_used(e, i, n - 3)
        e.activation(m.wh[:, s, :], m.raw[:, s, :], ACT.Copy).then_inc(self.high, 1)

    def sc_leave(self, e, i, g, tile, c):
        m = self.m
        q = 12 * g + 3 * tile + c
        tt = 4 * g + tile
        row = m.u[:, tt % 2, :]
        a, b = CUTS[c]
        bank = m.ps4[q % 4]
        e.wait_ge(self.up, i * 24 + q + 1)
        if c == 0:
            if tt >= 2:
                e.wait_ge(self.conv, i * 8 + tt - 1)
            if tile == 0:
                e.wait_ge(self.par_in[g % 2], i * 16 + 16 * (g // 2 + 1))
            e.activation(row[:, S0:S0 + 2], m.par[:, g % 2, tile, 4:6], ACT.Copy)
        if c < 2:
            e.activation(row[:, 2 + a:2 + b], bank[:, 0:b - a], ACT.Copy).then_inc(self.left, 1)
        else:
            if tile == 0 and g:
                e.wait_ge(self.tails_out, i * 32 + 16 * g)
            e.activation(row[:, 2 + a:2 + SEQ], bank[:, 0:SEQ - a], ACT.Copy)
            e.activation(row[:, 2 + S0:2 + T], bank[:, S0 - a:b - a], ACT.Copy)
            e.activation(m.tail[:, g % 2, 2 * tile, :], bank[:, SEQ - 2 - a:SEQ - a], ACT.Copy)
            e.activation(m.tail[:, g % 2, 2 * tile + 1, :], bank[:, T - 2 - a:T - a], ACT.Copy).then_inc(self.left, 1)

    def sc_up(self, e, i, g):
        m = self.m
        for tile in range(4):
            n = tile if g == 0 else 4 + 6 * (g - 1) + tile
            for c in range(3):
                self.sc_leave(e, i, g, tile, c)
                if c == 0:
                    self.sc_high(e, i, n + 2)
                    if tile % 2 == 0 and (g or tile):
                        self.sc_ghigh(e, i, 2 * g + tile // 2 - 1)
            if tile == 3:
                e.wait_ge(self.left, i * 24 + 12 * g + 12)
                dst = self.tails[0] if g == 0 else self.tails[bass.ds(i * 2 + g, 1)].rearrange("a p t c -> (a p) t c")
                e.dma_start(dst, m.tail[:, g % 2, :, :]).then_inc(self.tails_out, 16)
            if tile % 2:
                f = 2 * g + tile // 2
                e.wait_ge(self.conv, i * 8 + 2 * f + 1)
                if f:
                    e.wait_ge(self.glow, i * 4 + f)
                e.activation(m.sa[:, :], m.ca[:, :], ACT.Silu).then_inc(self.silu, 1)

    def sc_ghigh(self, e, i, f):
        m = self.m
        e.wait_ge(self.gate, i * 4 + f + 1)
        e.activation(m.gh[:, f % 4, :], m.sa[:, :], ACT.Copy).then_inc(self.ghigh, 1)

    def scalar(self, e):
        L = (GROUPS - 1) // 2
        self.sc_high(e, 0, 0)
        self.sc_high(e, 0, 1)
        self.sc_up(e, 0, 0)
        with e.Fori(0, L) as i:
            self.sc_up(e, i, 1)
            self.sc_high(e, i, 4 + 6)
            self.sc_high(e, i, 4 + 7)
            self.sc_up(e, i, 2)
            self.sc_high(e, i, 4 + 12)
            self.sc_high(e, i, 4 + 13)
        self.sc_ghigh(e, L, 1)
        e.wait_ge(self.tails_out, 16 * GROUPS)

    def po_low(self, e, i, n):
        m = self.m
        e.wait_ge(self.high, i * 12 + n + 1)
        e.tensor_tensor(m.wl[:, n % 3, :], m.raw[:, n % 3, :], m.wh[:, n % 3, :].bitcast(F32),
                        ALU.subtract).then_inc(self.low, 1)

    def po_glow(self, e, i, f):
        m = self.m
        e.wait_ge(self.ghigh, i * 4 + f + 1)
        e.tensor_tensor(m.gl[:, f % 4, :], m.sa[:, :], m.gh[:, f % 4, :].bitcast(F32), ALU.subtract).then_inc(self.glow, 1)

    def po_up(self, e, i, g):
        for tile in range(4):
            n = tile if g == 0 else 4 + 6 * (g - 1) + tile
            self.po_low(e, i, n + 2)
            if tile % 2 == 0 and (g or tile):
                self.po_glow(e, i, 2 * g + tile // 2 - 1)

    def gpsimd(self, e):
        L = (GROUPS - 1) // 2
        self.po_low(e, 0, 0)
        self.po_low(e, 0, 1)
        self.po_up(e, 0, 0)
        with e.Fori(0, L) as i:
            self.po_up(e, i, 1)
            self.po_low(e, i, 10)
            self.po_low(e, i, 11)
            self.po_up(e, i, 2)
            self.po_low(e, i, 16)
            self.po_low(e, i, 17)
        self.po_glow(e, L, 1)

    def ve_conv(self, e, i, g, tile):
        m = self.m
        tt = 4 * g + tile
        out = m.ca if tile % 2 == 0 else m.cb
        row = m.u[:, tt % 2, :]
        w = lambda x: m.par[:, g % 2, tile, x:x + 1]
        e.wait_ge(self.left, i * 24 + 3 * tt + 3)
        if tile % 2 == 0 and tt >= 2:
            e.wait_ge(self.silu, i * 4 + tt // 2)
        if tile % 2 and tt >= 2:
            e.wait_ge(self.gate, i * 4 + tt // 2)
        e.tensor_scalar(out[:, :], row[:, 0:T], w(0), w(3), ALU.mult, ALU.add).then_inc(self.c1, 1)
        e.wait_ge(self.c1, i * 16 + 2 * tt + 1)
        e.scalar_tensor_tensor(out[:, :], row[:, 1:T + 1], w(1), out[:, :], ALU.mult, ALU.add).then_inc(self.c1, 1)
        e.wait_ge(self.c1, i * 16 + 2 * tt + 2)
        e.scalar_tensor_tensor(out[:, :], row[:, 2:T + 2], w(2), out[:, :], ALU.mult, ALU.add).then_inc(self.conv, 1)

    def ve_gate(self, e, i, f):
        m = self.m
        e.wait_ge(self.silu, i * 4 + f + 1)
        e.wait_ge(self.conv, i * 8 + 2 * f + 2)
        e.tensor_tensor(m.sa[:, :], m.sa[:, :], m.cb[:, :], ALU.mult).then_inc(self.gate, 1)

    def ve_add(self, e, i, g, q0, q1):
        m = self.m
        for q in range(q0, q1):
            mt, c = divmod(q, 3)
            a, b = CUTS[c]
            bank = m.ps4[4 + (24 * g + q) % 4]
            e.wait_ge(self.down, i * 48 + 24 * g + q + 1)
            e.tensor_tensor(m.x[:, mt, a:b], bank[:, 0:b - a], m.x[:, mt, a:b], ALU.add).then_inc(self.banks_free, 1)

    def ve_up(self, e, i, g, head=0):
        self.ve_conv(e, i, g, 0)
        self.ve_conv(e, i, g, 1)
        self.ve_gate(e, i, 2 * g)
        self.ve_conv(e, i, g, 2)
        self.ve_conv(e, i, g, 3)
        if head:
            self.ve_add(e, i, g - 1, 0, head)
        self.ve_gate(e, i, 2 * g + 1)

    def vector(self, e):
        L = (GROUPS - 1) // 2
        e.sem_inc(self.banks_free, 4)
        self.ve_up(e, 0, 0)
        with e.Fori(0, L) as i:
            for g in (1, 2):
                self.ve_up(e, i, g, head=6)
                self.ve_add(e, i, g - 1, 6, 24)
        self.ve_add(e, L, 0, 0, 24)



def build(nc, io):
    with ExitStack() as top:
        m = Mem()
        sem = lambda s: top.enter_context(nc.semaphore(s))

        def sb(ctx, name, shape, dt=F32):
            return ctx.enter_context(nc.sbuf_tensor(name, shape, dt))

        m.ps = [top.enter_context(nc.psum_tensor(f"ps{i}", [P, 1024], F32)) for i in range(2)]
        m.pst = [top.enter_context(nc.psum_tensor(f"pst{i}", [P, 512], F32)) for i in range(2)]
        m.po = top.enter_context(nc.psum_tensor("po", [P, 512], F32))
        m.pot = top.enter_context(nc.psum_tensor("pot", [P, 512], F32))
        m.pnext = m.pot
        m.ps4 = [m.ps[0][:, 0:512], m.ps[0][:, 512:1024], m.ps[1][:, 0:512], m.ps[1][:, 512:1024],
                 m.pst[0], m.pst[1], m.po, m.pot]
        m.x = sb(top, "x", [P, KT, T])
        m.ident = sb(top, "ident", [P, P])
        m.ones = sb(top, "ones", [P, P])
        m.causal = sb(top, "causal", [P, P])
        m.gains = sb(top, "gains", [P, N_GAINS])
        loaded, consts = sem("loaded"), sem("consts")
        waited = sem("waited")

        def apart(e):
            e.sem_inc(waited, 1)
        m.apart = apart

        phase = []

        def phase_sem(name):
            phase.append(nc.alloc_semaphore(name))
            return phase[-1]
        m.sem = phase_sem

        def end_phase():
            nums = sorted(s.num for s in phase)
            runs = [[nums[0], nums[0]]]
            for n in nums[1:]:
                if n == runs[-1][1] + 1:
                    runs[-1][1] = n
                else:
                    runs.append([n, n])
            with nc.Block() as block:
                @block.gpsimd
                def _(e):
                    for a, b in runs:
                        e.sem_clear(range(a, b + 1))
            for s in phase:
                nc.release_semaphore(s)
            phase.clear()

        def norm_scratch(ctx, tag):
            m.sq = sb(ctx, f"sq{tag}", [P, 4, 384])
            m.tmp = sb(ctx, f"tmp{tag}", [P, 4, 384])
            m.rms = sb(ctx, f"rms{tag}", [P, 3, 384])

        def norm_block(name, gain0, dst=None, split=None, before=None):
            with ExitStack() as ctx:
                norm_scratch(ctx, name)
                norm = Norm(nc, ctx, m, name, lambda k, a, b: m.x[:, k, a:b], CUTS, KT, D_MODEL, gain0, dst, split)
                with nc.Block() as block:
                    @block.sync
                    def _(e):
                        if before:
                            e.dma_start(m.gains[:, :], io.gains).then_inc(loaded, 16)
                            for k in range(KT):
                                e.dma_start(m.x[:, k, :], io.x[:, k, :]).then_inc(loaded, 16)

                    @block.gpsimd
                    def _(e):
                        if before:
                            e.memset(m.ident[:, :], 0.0).then_inc(consts, 1)
                            e.memset(m.causal[:, :], 0.0).then_inc(consts, 1)
                            e.memset(m.ones[:, :], 1.0).then_inc(consts, 1)
                            e.wait_ge(consts, 3)
                            e.affine_select(out=m.ident[:, :], in_=m.ident[:, :], compare_op=ALU.not_equal, fill=1.0,
                                            base=0, pattern=[[-1, P]], channel_multiplier=1).then_inc(consts, 1)
                            e.affine_select(out=m.causal[:, :], in_=m.causal[:, :], compare_op=ALU.is_gt, fill=MASKED,
                                            base=0, pattern=[[-1, P]], channel_multiplier=1).then_inc(consts, 1)
                        norm.gpsimd(e)

                    @block.scalar
                    def _(e):
                        if before:
                            e.wait_ge(loaded, 16 * (KT + 1))
                        norm.scalar(e)

                    @block.tensor
                    def _(e):
                        if before:
                            e.wait_ge(consts, 5)
                        norm.tensor(e)

                    @block.vector
                    def _(e):
                        if before:
                            e.wait_ge(loaded, 16 * (KT + 1))
                        norm.vector(e)

        def ffn_layer(layer):
            with ExitStack() as ctx:
                m.hh = sb(ctx, f"hh{layer}", [P, KT, T], F32R)
                m.hl = sb(ctx, f"hl{layer}", [P, KT, T], F32R)
                norm_block(f"norm_ffn{layer}", GAIN_FFN[layer], split=(m.hh, m.hl))
                m.raw = sb(ctx, f"raw{layer}", [P, 3, 1024])
                m.wh = sb(ctx, f"wh{layer}", [P, 3, 1024], F32R)
                m.wl = sb(ctx, f"wl{layer}", [P, 3, 1024], F32R)
                m.u = sb(ctx, f"u{layer}", [P, 2, T + 2])
                m.ca, m.cb, m.sa = (sb(ctx, f"{n}{layer}", [P, T]) for n in ("ca", "cb", "sa"))
                m.gh = sb(ctx, f"gh{layer}", [P, 4, T], F32R)
                m.gl = sb(ctx, f"gl{layer}", [P, 4, T], F32R)
                m.par = sb(ctx, f"par{layer}", [P, 2, 4, 6])
                m.tail = sb(ctx, f"tail{layer}", [P, 2, 8, 2])
                f = Ffn(nc, ctx, m, f"ffn{layer}", io.ffn_w[layer], io.ffn_p[layer], io.tails[layer])
                halo0 = m.sem(f"halo_zero{layer}")
                with nc.Block() as block:
                    @block.sync
                    def _(e):
                        f.sync(e)

                    @block.gpsimd
                    def _(e):
                        e.memset(m.u[:, :, 0:2], 0.0).then_inc(halo0, 1)
                        f.gpsimd(e)

                    @block.scalar
                    def _(e):
                        f.scalar(e)

                    @block.tensor
                    def _(e):
                        f.tensor(e)

                    @block.vector
                    def _(e):
                        e.wait_ge(halo0, 1)
                        f.vector(e)

        def attention_scratch(ctx, layer, ring):
            m.w = sb(ctx, f"w{layer}", [P, ring, 1024])
            m.o = sb(ctx, f"o{layer}", [P, KT, T])
            m.wk = sb(ctx, f"wk{layer}", [P, 2, 1024])
            m.run = sb(ctx, f"run{layer}", [P, KEYS_D])
            m.pt = sb(ctx, f"pt{layer}", [P, 1024])
            m.strip = sb(ctx, f"strip{layer}", [P, 2, 640])
            m.otok = sb(ctx, f"otok{layer}", [P, P])
            m.mx, m.negmax = sb(ctx, f"mx{layer}", [P, 2]), sb(ctx, f"negmax{layer}", [P, 2])
            m.rowsum, m.esink = sb(ctx, f"rowsum{layer}", [P, 8]), sb(ctx, f"esink{layer}", [P, 8])
            m.sink = sb(ctx, f"sink{layer}", [P, 2])
            m.w_in = [m.sem(f"w_in{layer}_{i}") for i in range(ring)]
            m.proj_ready = m.sem(f"projected{layer}")

        with ExitStack() as ctx:
            m.hn = sb(ctx, "hn0", [P, KT, T])
            norm_block("norm_mix0", GAIN_MIX[0], dst=lambda k, a, b: m.hn[:, k, a:b], before=True)
            attention_scratch(ctx, 0, 3)
            m.q, m.k, m.vt = sb(ctx, "q", [P, T]), sb(ctx, "k", [P, KEYS]), sb(ctx, "vt", [P, KEYS])
            m.q_next, m.k_next = sb(ctx, "q_next", [P, T]), sb(ctx, "k_next", [P, KEYS])
            m.cache_in = nc.alloc_semaphore("cache_in0")
            m.vtok = sb(ctx, "vtok", [P, 11, P])
            st = Stream(nc, m, "pairs0", ("q", "k", "v"), 0, 3, 2 * PAIRS)
            a = Attend(nc, m, "A", 0, io, st, 0)
            b = Attend(nc, m, "B", PAIRS, io, st, PAIRS)
            out = b.tail = OutProject(nc, m, "out0", 72, 3, filled=UNITS // 3, per_pair=UNITS)
            gap = m.sem("gap0")
            with nc.Block() as block:
                @block.sync
                def _(e):
                    weight_stream(e, m, [(io.w0, 1024, 24), (io.w0_out, 512, 16)], 3)

                @block.gpsimd
                def _(e):
                    e.memset(m.o[:, :, SEQ:S0], 0.0).then_inc(gap, 1)
                    load_caches(e, m, io, 0)
                    a.load_strip(e, 0)
                    a.pairs(e, a.gpsimd)
                    e.wait_ge(a.strip_in, 16 * (PAIRS + 1))
                    b.pairs(e, b.gpsimd, last=True)

                @block.scalar
                def _(e):
                    st.first(e, "s")
                    a.pairs(e, a.scalar)
                    b.pairs(e, b.scalar, last=True)

                @block.tensor
                def _(e):
                    st.products(e, 0, 0, len(st.pieces))
                    a.pairs(e, a.tensor)
                    e.wait_ge(gap, 1)
                    a.wait_all(e)
                    b.pairs(e, b.tensor, last=True)
                    b.wait_all(e)
                    out.tensor(e)

                @block.vector
                def _(e):
                    st.first(e, "v")
                    a.pairs(e, a.vector)
                    e.sem_inc(out.bank_free, 1)
                    b.pairs(e, b.vector, last=True)
                    out.vector(e)
        ffn_layer(0)
        end_phase()

        with ExitStack() as ctx:
            m.hn = sb(ctx, "hn1", [P, KT, T])
            norm_block("norm_mix1", GAIN_MIX[1], dst=lambda k, a, b: m.hn[:, k, a:b])
            attention_scratch(ctx, 1, 4)
            m.q = sb(ctx, "q1", [P, T])
            m.cq, m.ckv = sb(ctx, "cq", [P, C_Q // P, T]), sb(ctx, "ckv", [P, C_KV // P, KEYS])
            m.kd, m.vtok_d = sb(ctx, "kd", [P, KEYS_D]), sb(ctx, "vtok_d", [P, 10, P])
            m.kp, m.rot = sb(ctx, "kp", [P, KEYS]), sb(ctx, "rot", [P, T])
            m.rms = sb(ctx, "rms1", [P, 4, 384])
            m.sq = m.wk[:, :, :].rearrange("p a b -> p (a b)")[:, 0:4 * 384].rearrange("p (a b) -> p a b", a=4)
            flat = m.hn[:, :, :].rearrange("p a b -> p (a b)")
            m.qh = [flat[:, i * T:(i + 1) * T] for i in range(2)]
            m.kh = [flat[:, 2 * T + i * KEYS:2 * T + (i + 1) * KEYS] for i in range(2)]
            at = 2 * T + 2 * KEYS
            m.vt = flat[:, at:at + KEYS]
            m.qr_next = flat[0:64, at + KEYS + 11 * P:at + KEYS + 11 * P + T]
            m.q_next, m.k_next = sb(ctx, "qn_next", [P, T]), sb(ctx, "kn_next", [P, KEYS])
            m.ropes = sb(ctx, "ropes", [64, 2, 384])
            m.vtok = flat[:, at + KEYS:at + KEYS + 11 * P].rearrange("p (b f) -> p b f", f=P)
            inp = Project(nc, ctx, m, "in1", 0, 4, 12, lambda k, a, b: m.hn[:, k, a:b])
            kv_cols = [(0, 384), (384, 768), (768, SEQ), (SEQ + PAST, KEYS)]
            nq = Norm(nc, ctx, m, "norm_q", lambda k, a, b: m.cq[:, k, a:b], CUTS, 3, C_Q, GAIN_Q, lambda k, a, b: m.cq[:, k, a:b])
            nkv = Norm(nc, ctx, m, "norm_kv", lambda k, a, b: m.ckv[:, k, a:b], kv_cols, 2, C_KV, GAIN_KV, lambda k, a, b: m.ckv[:, k, a:b])
            st = Stream(nc, m, "pairs1", ("qn", "qr", "kn", "v"), 36, 4, PAIRS)
            c = Attend(nc, m, "C", 0, io, st, 0)
            d = Attend(nc, m, "D", PAIRS, io)
            out = d.tail = OutProject(nc, m, "out1", 84, 4, filled=KT, per_pair=3 * KT // PAIRS)
            s = m.sem
            gap, roped, vturned, vleft = s("gap1"), s("roped1"), s("vd_turned"), s("vd_left")
            cache_in, stored = nc.alloc_semaphore("cache_in1"), nc.alloc_semaphore("stored1")
            new0 = SEQ + PAST
            vd_uses = ((0, 1, 2, 3), (4, 5, 6, 7), (8,), (9,))
            with nc.Block() as block:
                @block.sync
                def _(e):
                    weight_stream(e, m, [(io.w1, 1024, 12)], 4)
                    with e.Fori(0, PAIRS) as j:
                        for s, (src, width) in enumerate(((io.c_q, 384), (io.c_q, 384), (io.c_kv, 256), (io.c_kv, 256))):
                            e.wait_ge(m.proj_ready, j * 12 + 3 * (12 + s - 3))
                            e.dma_start(m.w[:, s, 0:width], src[bass.ds(j * 2 + s % 2, 1)].rearrange("a p c -> (a p) c")).then_inc(m.w_in[s], 16)
                    with e.Fori(0, PAIRS) as j:
                        for w in range(2):
                            e.wait_ge(m.proj_ready, j * 6 + out.base - 3 + 3 * w)
                            e.dma_start(m.w[:, w, 0:512], io.w1_out[bass.ds(j * 2 + w, 1)].rearrange("a p c -> (a p) c")).then_inc(m.w_in[w], 16)
                    for w in range(KT, 2 * KT):
                        if w >= KT + 2:
                            e.wait_ge(m.proj_ready, out.base + 3 * (w - 3 if w >= KT + 4 else w - 4 + 1))
                        e.dma_start(m.w[:, out.slot(w), 0:512], io.w1_out[w]).then_inc(m.w_in[out.slot(w)], 16)

                @block.gpsimd
                def _(e):
                    e.dma_start(m.rot[:, :], io.rot).then_inc(cache_in, 16)
                    e.dma_start(m.ckv[:, :, SEQ:new0], io.cache_c).then_inc(cache_in, 16)
                    e.dma_start(m.kp[HEAD:HEAD + C_ROPE, SEQ:new0], io.cache_pe).then_inc(cache_in, 16)
                    e.dma_start(m.kd[:, SEQ:SEQ + D_CACHE], io.cache_dk).then_inc(cache_in, 16)
                    e.dma_start(m.run[:, SEQ:SEQ + D_CACHE], io.cache_dv).then_inc(cache_in, 16)
                    e.memset(m.o[:, 0:PAIRS, SEQ:S0], 0.0).then_inc(gap, 1)
                    e.wait_ge(inp.left, 36)
                    e.wait_ge(cache_in, 80)
                    for dst, src in ((io.dk, m.kd[:, SEQ - P:SEQ]), (io.dks, m.kd[:, KEYS_D - D_CACHE:KEYS_D]),
                                     (io.dv, m.run[:, SEQ - P:SEQ]), (io.dvs, m.run[:, KEYS_D - D_CACHE:KEYS_D]),
                                     (io.kpe, m.kp[HEAD:HEAD + C_ROPE, 0:SEQ]), (io.kpes, m.kp[HEAD:HEAD + C_ROPE, new0:KEYS])):
                        e.dma_start(dst, src).then_inc(stored, 16)
                    e.wait_ge(nkv.normed, 8)
                    e.dma_start(io.ckv, m.ckv[:, :, 0:SEQ]).then_inc(stored, 16)
                    e.dma_start(io.ckvs, m.ckv[:, :, new0:KEYS]).then_inc(stored, 16)
                    e.wait_ge(stored, 128)
                    d.load_strip(e, 0)
                    c.pairs(e, c.gpsimd, last=True)
                    d.pairs(e, d.gpsimd)
                    e.wait_ge(d.strip_in, 32 * (PAIRS + 1))

                @block.scalar
                def _(e):
                    e.wait_ge(inp.left, 36)
                    e.wait_ge(roped, 3)
                    nq.scalar(e)
                    e.wait_ge(nq.normed, 9)
                    nkv.scalar(e)
                    e.wait_ge(nkv.normed, 8)
                    st.first(e, "s")
                    c.pairs(e, c.scalar, last=True)
                    d.pairs(e, d.scalar)

                @block.tensor
                def _(e):
                    inp.tensor(e)
                    e.wait_ge(inp.left, 36)
                    e.wait_ge(cache_in, 80)
                    for r, blocks in enumerate(vd_uses):
                        if r >= 2:
                            e.wait_ge(vleft, r - 1)
                        for i, blk in enumerate(blocks):
                            kw = min(P, KEYS_D - P * blk)
                            mm = e.transpose(m.pst[r % 2][0:kw, P * i:P * i + P], m.run[:, P * blk:P * blk + kw], m.ident[:, :])
                        mm.then_inc(vturned, 1)
                    nq.tensor(e)
                    e.wait_ge(nq.normed, 9)
                    nkv.tensor(e)
                    e.wait_ge(nkv.normed, 8)
                    st.products(e, 0, 0, len(st.pieces))
                    c.pairs(e, c.tensor, last=True)
                    e.wait_ge(gap, 1)
                    c.wait_all(e)
                    d.pairs(e, d.tensor)
                    d.wait_all(e)
                    out.tensor(e)

                @block.vector
                def _(e):
                    for n, w, cut, a_, b_, ps, off in inp.results(e):
                        src = ps[:, off:off + b_ - a_]
                        if w < 3:
                            e.tensor_copy(m.cq[:, w, a_:b_], src).then_inc(inp.left, 1)
                        elif w < 5 or w in (6, 7):
                            dst = m.ckv[:, w - 3, :] if w < 5 else (m.kd if w == 6 else m.run)
                            end = KEYS if w < 5 else KEYS_D
                            if cut < 2:
                                e.tensor_copy(dst[:, a_:b_], src).then_inc(inp.left, 1)
                            else:
                                e.tensor_copy(dst[:, a_:SEQ], src[:, 0:SEQ - a_])
                                e.tensor_copy(dst[:, end - DEC_SEQ:end], src[:, S0 - a_:b_ - a_]).then_inc(inp.left, 1)
                        elif w == 5:
                            n_ = b_ - a_
                            ta, tb = m.wk[0:32, 0, 0:n_], m.wk[0:32, 1, 0:n_]
                            if cut == 0:
                                e.wait_ge(cache_in, 80)
                            else:
                                e.wait_ge(inp.left, n)
                            e.tensor_tensor(ta, src[0:32, :], m.rot[0:32, a_:b_], ALU.mult)
                            e.tensor_tensor(tb, src[64:96, :], m.rot[64:96, a_:b_], ALU.mult).then_inc(roped, 1)
                            e.wait_ge(roped, cut + 1)
                            kp = m.kp[HEAD:HEAD + C_ROPE, :]
                            if cut < 2:
                                e.tensor_tensor(kp[:, a_:b_], ta, tb, ALU.add).then_inc(inp.left, 1)
                            else:
                                e.tensor_tensor(kp[:, a_:SEQ], ta[:, 0:SEQ - a_], tb[:, 0:SEQ - a_], ALU.add)
                                e.tensor_tensor(kp[:, new0:KEYS], ta[:, S0 - a_:n_], tb[:, S0 - a_:n_], ALU.add).then_inc(inp.left, 1)
                        else:
                            e.tensor_scalar(m.o[:, PAIRS + w - 8, a_:b_], src, SCALE, None, ALU.mult).then_inc(inp.left, 1)
                    for r, blocks in enumerate(vd_uses):
                        rows = min(P, KEYS_D - P * blocks[0])
                        e.wait_ge(vturned, r + 1)
                        e.tensor_copy(m.vtok_d[0:rows, blocks[0]:blocks[-1] + 1, :],
                                      m.pst[r % 2][0:rows, 0:P * len(blocks)].rearrange("p (b f) -> p b f", f=P)).then_inc(vleft, 1)
                    nq.vector(e)
                    nkv.vector(e)
                    st.first(e, "v")
                    for h in range(2):
                        e.tensor_copy(m.kh[h][HEAD:HEAD + C_ROPE, :], m.kp[HEAD:HEAD + C_ROPE, :])
                    c.pairs(e, c.vector, last=True)
                    e.sem_inc(out.bank_free, 1)
                    d.pairs(e, d.vector)
                    out.vector(e)
        end_phase()
        ffn_layer(1)
        norm_block("norm_final", GAIN_FINAL, dst=lambda k, a, b: m.x[:, k, a:b])
        with nc.Block() as block:
            @block.sync
            def _(e):
                for k in range(KT):
                    e.dma_start(io.y[:, k, :], m.x[:, k, :]).then_inc(loaded, 16)
                e.wait_ge(loaded, 16 * (2 * KT + 1))


def kernel(**inputs):
    import numpy as np
    import concourse.bacc as bacc
    from concourse.bass_utils import run_bass_kernel_spmd

    g = {k: np.asarray(v) for k, v in inputs.items()}
    f32 = np.float32
    feat = lambda a, n=P: np.ascontiguousarray(a)

    def tiles(w):
        k, n = w.shape
        return w.reshape(k // P, P, n // P, P).transpose(2, 1, 0, 3).reshape(n // P, P, k)

    def cols(w, size=HEAD):
        return w.reshape(w.shape[0], -1, size)

    arrays = {}
    x = np.zeros((T, D_MODEL), f32)
    x[:SEQ], x[S0:] = g["x_prompt"][0], g["x_sample"][0]
    arrays["x"] = x.T.reshape(KT, P, T).transpose(1, 0, 2)
    gains = [g["norm_mix"][0], g["norm_mix"][1], g["norm_ffn"][0], g["norm_ffn"][1], g["norm_final"],
             g["odd_norm_q"][0], g["odd_norm_kv"][0]]
    arrays["gains"] = np.concatenate(gains).reshape(N_GAINS, P).T
    w = g["even_w_in"][0]
    a_and_b = tiles(w).reshape(2, 3, PAIRS, P, D_MODEL).transpose(0, 2, 1, 3, 4).reshape(24, P, D_MODEL)
    arrays["w0"] = a_and_b
    halves = lambda w: w.reshape(KT, P, 2, 512).transpose(2, 0, 1, 3).reshape(2 * KT, P, 512)
    arrays["w0_out"] = halves(tiles(g["even_w_out"][0]))
    idx = np.clip(512 + np.arange(P)[:, None] - np.arange(640), -256, 256) + 256
    more = lambda z: np.concatenate([z, z[:1]])
    arrays["bias"] = more(g["even_rel_bias"][0].reshape(PAIRS, 2, -1)[:, :, idx].transpose(0, 2, 1, 3))
    pair = lambda c: np.moveaxis(c.reshape(c.shape[-3], PAIRS, P), 0, -1)
    for kv in "kv":
        arrays[f"cache_{kv}"] = np.concatenate([pair(g[f"cache_{n}_{kv}"][0, 0]) for n in "ab"])
    w = g["odd_w_in"][0]
    o = np.cumsum([0, C_Q, C_KV, C_ROPE, 512, 128, 128])
    part = [w[:, o[i]:o[i + 1]] for i in range(6)]
    swap = lambda z: np.concatenate([z[..., C_ROPE // 2:], z[..., :C_ROPE // 2]], axis=-1)
    kpe = part[2]
    qd = cols(part[3])
    qd = np.stack([qd[:, :PAIRS], qd[:, PAIRS:]], axis=2).reshape(D_MODEL, 512)
    arrays["w1"] = tiles(np.concatenate([part[0], part[1], kpe, kpe, swap(kpe), swap(kpe), part[4], part[5], qd], axis=1))
    uq = g["odd_w_uq"][0]
    nope, rope = uq[:, :, :C_NOPE], uq[:, :, C_NOPE:]
    both = lambda z: z.reshape(C_Q, PAIRS, 1, -1)
    r2 = np.concatenate([both(rope), both(swap(rope))], axis=2).reshape(C_Q, PAIRS, 1, P)
    arrays["c_q"] = tiles(np.concatenate([both(nope), r2], axis=2).reshape(C_Q, 2 * PAIRS * P))
    ukv = g["odd_w_ukv"][0].reshape(C_KV, PAIRS, 2, 2, HEAD).transpose(0, 1, 3, 2, 4)
    arrays["c_kv"] = tiles(ukv.reshape(C_KV, 2 * PAIRS * P))
    wo = g["odd_w_out"][0]
    d_rows = wo[512:].reshape(2, PAIRS, HEAD, D_MODEL).transpose(1, 0, 2, 3).reshape(512, D_MODEL)
    arrays["w1_out"] = halves(tiles(np.concatenate([wo[:512], d_rows])))
    arrays["cache_c"] = g["cache_c_kv"][0, 0].T.reshape(C_KV // P, P, PAST).transpose(1, 0, 2)
    arrays["cache_pe"] = g["cache_c_kpe"][0, 0].T
    arrays["cache_dk"] = g["cache_d_k"][0, 0].reshape(D_CACHE, P).T
    arrays["cache_dv"] = g["cache_d_v"][0, 0].reshape(D_CACHE, P).T
    arrays["sinks"] = more(g["odd_sinks"][0].reshape(2, PAIRS).T)
    pos = np.zeros(T, f32)
    pos[:SEQ], pos[S0:] = np.arange(SEQ), PAST + np.arange(DEC_SEQ)
    inv = (f32(10000.0) ** (-np.arange(16, dtype=f32) / f32(16))).astype(f32)
    ang = (pos[None, :] * inv[:, None]).astype(f32)
    cos, sin = np.cos(ang).astype(f32), np.sin(ang).astype(f32)
    arrays["rot"] = np.concatenate([cos, cos, cos, cos, -sin, sin, -sin, sin])
    p_, c_ = np.arange(P)[:, None], np.arange(256)[None, :]
    seen = np.where(p_ < CHUNK, c_ < 192, c_ >= 64)
    slopes = (f32(2.0) ** (f32(-8.0) * np.arange(1, 9, dtype=f32) / f32(8))).astype(f32)
    pen = np.where(seen[None], -slopes[:, None, None] * np.abs(128 + p_ - c_)[None].astype(f32), f32(MASKED)).astype(f32)
    arrays["alibi"] = more(pen.reshape(2, PAIRS, P, 256).transpose(1, 2, 0, 3))
    for layer in range(2):
        wi = tiles(g["ffn_w_in"][layer]).reshape(2, GROUPS, 2, P, D_MODEL).transpose(1, 2, 0, 3, 4).reshape(GROUPS, 4, P, 1024)
        wo = g["ffn_w_out"][layer].reshape(GROUPS, 2, P, 2, 4, P).transpose(0, 3, 2, 4, 1, 5).reshape(GROUPS, 2, P, 1024)
        order = [wi[0]] + [z for k in range(1, GROUPS) for z in (wi[k], wo[k - 1])] + [wo[GROUPS - 1]]
        arrays[f"ffn_w{layer}"] = np.concatenate(order)
        pr = np.concatenate([g["ffn_conv_w"][layer], g["ffn_conv_b"][layer][None], g["state_ffn_conv"][layer, 0]])
        arrays[f"ffn_p{layer}"] = pr.reshape(6, 2, GROUPS, 2, P).transpose(2, 4, 3, 1, 0).reshape(GROUPS, P, 4, 6)
    arrays = {k: np.ascontiguousarray(v, dtype=v.dtype) for k, v in arrays.items()}

    outs = {"y": (P, KT, T), "ckv": (P, 2, SEQ), "ckvs": (P, 2, DEC_SEQ), "kpe": (C_ROPE, SEQ), "kpes": (C_ROPE, DEC_SEQ),
            "dk": (P, P), "dv": (P, P), "dks": (P, P), "dvs": (P, P)}
    for kv in "kv":
        outs |= {f"a{kv}": (PAIRS, P, 512), f"a{kv}s": (PAIRS, P, PAST), f"b{kv}": (PAIRS, P, SEQ), f"b{kv}s": (PAIRS, P, DEC_SEQ)}
    for layer in range(2):
        outs[f"tails{layer}"] = (GROUPS, P, 8, 2)

    nc = bacc.Bacc("TRN2", target_bir_lowering=False, num_devices=1)
    ap = {k: nc.dram_tensor(f"in_{k}", a.shape, mybir.dt.from_np(a.dtype), kind="ExternalInput").ap() for k, a in arrays.items()}
    ap |= {f"o_{k}": nc.dram_tensor(f"out_{k}", s, F32, kind="ExternalOutput").ap() for k, s in outs.items()}
    program(nc, ap)
    r = run_bass_kernel_spmd(nc, [{f"in_{k}": a for k, a in arrays.items()}], core_ids=[0]).results[0]
    r = {k: np.asarray(r[f"out_{k}"]) for k in outs}

    y = r["y"].transpose(2, 1, 0).reshape(T, D_MODEL)
    rows = lambda z, heads: np.moveaxis(z, -1, 0).reshape(1, 1, z.shape[-1], heads, HEAD)
    seq = lambda z: z.transpose(2, 1, 0).reshape(1, 1, z.shape[2], C_KV)
    tails = [r[f"tails{l}"].reshape(GROUPS, P, 2, 2, 2, 2).transpose(4, 5, 3, 0, 2, 1).reshape(2, 2, 2 * D_FF) for l in range(2)]
    conv = [np.stack([t[s] for t in tails])[:, None] for s in range(2)]
    return (y[None, :SEQ], y[None, S0:],
            rows(r["ak"], 8), rows(r["av"], 8), rows(r["aks"], 8), rows(r["avs"], 8),
            rows(r["bk"], 8), rows(r["bv"], 8), rows(r["bks"], 8), rows(r["bvs"], 8),
            seq(r["ckv"]), r["kpe"].T[None, None], seq(r["ckvs"]), r["kpes"].T[None, None],
            rows(r["dk"], 2), rows(r["dv"], 2), rows(r["dks"], 2), rows(r["dvs"], 2),
            conv[0], conv[1])


def program(nc, ap):
    io = Mem()
    io.x, io.gains, io.w0, io.w1, io.c_q, io.c_kv, io.w1_out, io.w0_out = (
        ap[k] for k in ("x", "gains", "w0", "w1", "c_q", "c_kv", "w1_out", "w0_out"))
    io.cache_c, io.cache_pe, io.cache_dk, io.cache_dv = (ap[f"cache_{k}"] for k in ("c", "pe", "dk", "dv"))
    io.rot, io.alibi, io.bias = ap["rot"], ap["alibi"], ap["bias"]
    io.y, io.ckv, io.ckvs, io.kpe, io.kpes = (ap[f"o_{k}"] for k in ("y", "ckv", "ckvs", "kpe", "kpes"))
    io.dk, io.dv, io.dks, io.dvs = (ap[f"o_{k}"] for k in ("dk", "dv", "dks", "dvs"))
    io.sinks = bass.AP(ap["sinks"].tensor, 0, [[2, PAIRS + 1], [0, P], [1, 2]])
    io.cache_k, io.cache_v = ap["cache_k"], ap["cache_v"]
    io.stores = {n.upper(): tuple(ap[f"o_{n}{k}"] for k in ("k", "v", "ks", "vs"))
                 + ((SEQ - 512, SEQ + DEC_SEQ) if n == "a" else (0, SEQ + PAST)) for n in "ab"}
    io.ffn_w = [ap["ffn_w0"], ap["ffn_w1"]]
    io.ffn_p = [ap["ffn_p0"], ap["ffn_p1"]]
    io.tails = [ap["o_tails0"], ap["o_tails1"]]
    build(nc, io)
```

```python
from contextlib import ExitStack

import concourse.bass as bass
from concourse import mybir

ALU = mybir.AluOpType
ACT = mybir.ActivationFunctionType
AX = mybir.AxisListType
F32 = mybir.dt.float32
F32R = mybir.dt.float32r

P = 128
D_MODEL, SEQ, DEC_SEQ, PAST = 1024, 1024, 64, 256
KT = D_MODEL // P
HEAD = 64
PAIRS = 4
CHUNK = 64
D_FF = 2816
GAP = 2
S0 = SEQ + GAP
T = S0 + DEC_SEQ
CUTS = [(0, 384), (384, 768), (768, T)]
KEYS = SEQ + PAST + DEC_SEQ
D_CACHE = 128
KEYS_D = SEQ + D_CACHE + DEC_SEQ
NQT = SEQ // P + 1
UNITS = 2 * NQT
MASKED = -1e30
EPS = 1e-6
C_Q, C_KV, C_ROPE, C_NOPE = 384, 256, 32, 64
C_SCALE = float(C_NOPE + C_ROPE) ** -0.5
SCALE = float(HEAD) ** -0.5
GROUPS = D_FF // 256
GAIN_MIX, GAIN_FFN, GAIN_FINAL, GAIN_Q, GAIN_KV, N_GAINS = (0, KT), (2 * KT, 3 * KT), 4 * KT, 5 * KT, 5 * KT + 3, 5 * KT + 5


def bank_of(n):
    return (n % 4) // 2, 512 * (n % 2)


class Norm:

    def __init__(self, nc, mem, name, src, cols, tiles, width, gain0, dst=None, split=None, banks=None,
                 arrived=None):
        self.banks, self.arrived = banks, arrived
        self.nc, self.mem, self.src, self.cols, self.tiles = nc, mem, src, cols, tiles
        self.width, self.gain0, self.dst, self.split = width, gain0, dst, split
        sem = lambda s: mem.sem(f"{name}_{s}")
        self.squared, self.summed = sem("squared"), sem("summed")
        self.var, self.std, self.inv = sem("var"), sem("std"), sem("inv")
        self.normed = sem("normed")
        if split:
            self.high, self.low_v, self.low_p = sem("high"), sem("low_v"), sem("low_p")
        self.items = [(c, k) for c in range(len(cols)) for k in range(tiles)]

    def scalar(self, e, before_high=None):
        m = self.mem
        for i, (c, k) in enumerate(self.items):
            a, b = self.cols[c]
            if i >= 4:
                e.wait_ge(self.summed, i - 3)
            if k == 0 and self.arrived:
                self.arrived(e, c)
            e.activation(m.sq[:, i % 4, 0:b - a], self.src(k, a, b), ACT.Square).then_inc(self.squared, 1)
            if k == self.tiles - 1 and c == 1:
                self.root(e, 0)
        if before_high:
            before_high(e)
        for c in range(len(self.cols)):
            if c:
                self.root(e, c)
            if self.split:
                self.highs(e, c)
    def highs(self, e, c):
        m = self.mem
        a, b = self.cols[c]
        for k in range(self.tiles):
            i = self.tiles * c + k
            e.wait_ge(self.normed, i + 1)
            e.activation(self.split[0][:, k, a:b], m.tmp[:, i % 4, 0:b - a], ACT.Copy).then_inc(self.high, 1)

    def bank(self, c):
        return self.banks[c] if self.banks else self.mem.ps4[c]

    def root(self, e, c):
        m = self.mem
        n = self.cols[c][1] - self.cols[c][0]
        e.wait_ge(self.var, c + 1)
        e.activation(m.rms[:, c, 0:n], m.rms[:, c, 0:n], ACT.Sqrt).then_inc(self.std, 1)

    def tensor(self, e):
        m = self.mem
        for i, (c, k) in enumerate(self.items):
            a, b = self.cols[c]
            e.wait_ge(self.squared, i + 1)
            e.matmul(self.bank(c)[:, 0:b - a], m.ones[:, :], m.sq[:, i % 4, 0:b - a],
                     start=k == 0, stop=k == self.tiles - 1).then_inc(self.summed, 1)

    def low(self, e, i, sem):
        c, k = self.items[i]
        a, b = self.cols[c]
        e.wait_ge(self.high, i + 1)
        e.tensor_tensor(self.split[1][:, k, a:b], self.mem.tmp[:, i % 4, 0:b - a],
                        self.split[0][:, k, a:b].bitcast(F32), ALU.subtract).then_inc(sem, 1)

    def vector(self, e):
        m = self.mem
        for i, (c, k) in enumerate(self.items):
            a, b = self.cols[c]
            if k == 0:
                if c == 0 and self.arrived:
                    self.arrived(e, len(self.cols) - 1)
                e.wait_ge(self.summed, self.tiles * (c + 1))
                e.tensor_scalar(m.rms[:, c, 0:b - a], self.bank(c)[:, 0:b - a], 1.0 / self.width, EPS,
                                ALU.mult, ALU.add).then_inc(self.var, 1)
                e.wait_ge(self.std, c + 1)
                e.reciprocal(m.rms[:, c, 0:b - a], m.rms[:, c, 0:b - a]).then_inc(self.inv, 1)
                e.wait_ge(self.inv, c + 1)
            g = m.gains[:, self.gain0 + k:self.gain0 + k + 1]
            if self.split:
                if i >= 4:
                    e.wait_ge(self.low_p if i % 2 else self.low_v, (i - 4) // 2 + 1)
                out = m.tmp[:, i % 4, 0:b - a]
            else:
                out = self.dst(k, a, b)
            e.scalar_tensor_tensor(out, self.src(k, a, b), g, m.rms[:, c, 0:b - a],
                                   ALU.mult, ALU.mult).then_inc(self.normed, 1)
            if self.split and i % 2 == 1:
                self.low(e, i - 1, self.low_v)
        e.wait_ge(self.normed, len(self.items))

    def wait_cut(self, e, c):
        n = self.tiles * (c + 1)
        e.wait_ge(self.normed, n)
        if self.split:
            e.wait_ge(self.high, n)
            e.wait_ge(self.low_v, n // 2)
            e.wait_ge(self.low_p, n // 2)

    def gpsimd(self, e):
        if self.split:
            for i in range(1, len(self.items), 2):
                self.low(e, i, self.low_p)


class Stream:
    STEPS = UNITS + 1

    def __init__(self, nc, mem, name, what, base, ring):
        self.m, self.what, self.base, self.ring = mem, what, base, ring
        self.latent = "qn" in what
        self.results = [(w, x, c) for w, x in enumerate(what) for c in range(3)]
        self.by = ["v" if x == "qr" or n % 2 else "s" for n, (w, x, c) in enumerate(self.results)]
        sem = lambda s: mem.sem(f"{name}_{s}")
        if not self.latent:
            self.high, self.low = sem("weights_high"), sem("weights_low")
        self.left_s, self.left_v = sem("left_by_scalar"), sem("left_by_vector")
        self.moved_s, self.moved_v = sem("moved_by_scalar"), sem("moved_by_vector")
        self.roped = sem("rope_parts")
        self.pieces = [(n, k) for n, (w, x, c) in enumerate(self.results) for k in range(self.depth(x))]

    def depth(self, what):
        return {"q": KT, "k": KT, "v": KT}[what] if not self.latent else (C_Q // P if what[0] == "q" else C_KV // P)

    def source(self, what):
        return self.m.hn if not self.latent else (self.m.cq if what[0] == "q" else self.m.ckv)

    def cut(self, what, c):
        return CUTS[c] if not self.latent or what[0] == "q" else (448 * c, 448 * c + 448)

    def wait_left(self, e, p, n):
        for who, s in (("s", self.left_s), ("v", self.left_v)):
            c = self.by[:n].count(who)
            if c:
                e.wait_ge(s, p * self.by.count(who) + c)

    def wait_moved(self, e, p):
        e.wait_ge(self.moved_s, p + 1)
        e.wait_ge(self.moved_v, p + 1)

    def products(self, e, p, lo, hi, norm=None):
        m = self.m
        for n, k in self.pieces[lo:hi]:
            w, what, c = self.results[n]
            a, b = self.cut(what, c)
            if k == 0:
                if c == 0 and self.latent:
                    unit = self.base // 3 + w
                    e.wait_ge(m.w_in[unit % self.ring], p * (16 * len(self.what) // self.ring) + 16 * (unit // self.ring + 1))
                if n:
                    e.wait_ge(self.left_s if self.by[n - 1] == "s" else self.left_v,
                              p * self.by.count(self.by[n - 1]) + self.by[:n].count(self.by[n - 1]))
            if norm and n < 3 and k == 0:
                norm.wait_cut(e, c)
            last = k == self.depth(what) - 1
            if self.latent:
                mm = e.matmul(m.pnext[:, 0:b - a], m.w[:, (self.base // 3 + w) % self.ring, k * P:(k + 1) * P],
                              self.source(what)[:, k, a:b], start=k == 0, stop=last)
            else:
                half = 2 * w + k // 4
                if c == 0 and k % 4 == 0:
                    e.wait_ge(self.low, p * 6 + half + 1)
                at = slice(k % 4 * P, k % 4 * P + P)
                for x, y, start in ((m.hh, m.wh, k == 0), (m.hl, m.wh, False), (m.hh, m.wl, False)):
                    mm = e.matmul(m.pnext[:, 0:b - a], y[:, half % 3, at], x[:, k, a:b], start=start,
                                  stop=last and y is m.wl)
            if last:
                mm.then_inc(m.proj_ready, 1)

    def split_high(self, e, p, i):
        m = self.m
        e.wait_ge(m.w_in[i % 3], p * 32 + 16 * (i // 3 + 1))
        if i >= 3:
            unit = i // 2 - 2 if i % 2 == 0 else i // 2 - 1
            e.wait_ge(m.proj_ready, p * 9 + 3 * (unit + 1))
        e.activation(m.wh[:, i % 3, :], m.w[:, i % 3, :], ACT.Copy).then_inc(self.high, 1)

    def split_low(self, e, p, i):
        m = self.m
        e.wait_ge(self.high, p * 6 + i + 1)
        e.tensor_tensor(m.wl[:, i % 3, :], m.w[:, i % 3, :], m.wh[:, i % 3, :].bitcast(F32), ALU.subtract).then_inc(self.low, 1)

    SPLITS = {2: 8, 5: 9, 8: 10, 11: 11, 14: 12, 18: 13}

    def leave(self, e, who, p, n, out_sem=None):
        m = self.m
        w, what, c = self.results[n]
        a, b = self.cut(what, c)
        src = m.pnext[:, 0:b - a]
        sem = self.left_s if who == "s" else self.left_v
        e.wait_ge(m.proj_ready, p * len(self.results) + self.base + n + 1)

        def move(dst, src, scale=1.0):
            if who == "s":
                return e.activation(dst, src, ACT.Copy, scale=scale)
            return e.tensor_scalar(dst, src, scale, None, ALU.mult) if scale != 1.0 else e.tensor_copy(dst, src)

        if what == "qr":
            x = m.ropes[:, 0, 0:b - a]
            y = m.ropes[:, 1, 0:b - a]
            e.tensor_tensor(x, src[0:64, :], m.rot[0:64, a:b], ALU.mult)
            e.tensor_tensor(y, src[64:128, :], m.rot[64:128, a:b], ALU.mult).then_inc(self.roped, 1)
            e.wait_ge(self.roped, p * 3 + c + 1)
            e.tensor_tensor(m.qr_next[0:64, a:b], x, y, ALU.add).then_inc(sem, 1)
            e.wait_ge(sem, p * self.by.count("v") + self.by[:n + 1].count("v"))
        elif what in ("q", "qn"):
            move(m.q_next[:, a:b], src, SCALE if what == "q" else 1.0).then_inc(sem, 1)
        elif self.latent:
            dst = m.k_next if what == "kn" else m.vt
            move(dst[:, a:b], src).then_inc(sem, 1)
        else:
            dst = m.k_next if what == "k" else m.vt
            if c < 2:
                move(dst[:, a:b], src).then_inc(sem, 1)
            else:
                move(dst[:, a:SEQ], src[:, 0:SEQ - a])
                move(dst[:, KEYS - DEC_SEQ:KEYS], src[:, S0 - a:b - a]).then_inc(sem, 1)

    def move_scalar(self, e, p):
        m = self.m
        self.wait_left(e, p, len(self.results))
        if self.latent:
            e.activation(m.qh[0][0:HEAD, :], m.q_next[0:HEAD, :], ACT.Copy)
            e.activation(m.qh[1][0:HEAD, :], m.q_next[HEAD:P, :], ACT.Copy).then_inc(self.moved_s, 1)
        else:
            e.activation(m.q[:, :], m.q_next[:, :], ACT.Copy).then_inc(self.moved_s, 1)

    def move_vector(self, e, p):
        m = self.m
        self.wait_left(e, p, len(self.results))
        if self.latent:
            for h in range(2):
                e.tensor_copy(m.kh[h][0:HEAD, :], m.k_next[HEAD * h:HEAD * h + HEAD, :])
                ins = e.tensor_copy(m.qh[h][HEAD:HEAD + C_ROPE, :], m.qr_next[C_ROPE * h:C_ROPE * h + C_ROPE, :])
            ins.then_inc(self.moved_v, 1)
        else:
            e.tensor_copy(m.k[:, :], m.k_next[:, :]).then_inc(self.moved_v, 1)

    def first(self, e, who):
        splits = {3: (3, 4), 6: (5, 6), 9: (7,)}
        for n in range(len(self.by) + 1):
            if who == "s" and not self.latent:
                for i in splits.get(n, ()):
                    self.split_high(e, 0, i)
            if n < len(self.by) and self.by[n] == who:
                self.leave(e, who, 0, n)

    def share(self, step):
        if step < 0:
            return 0
        count = len(self.results)
        n = next(n for n in range(count) if (n + 1) * self.STEPS // count > step)
        first, end = n * self.STEPS // count, (n + 1) * self.STEPS // count
        before = sum(self.depth(x) for _, x, _ in self.results[:n])
        return before + -(-self.depth(self.results[n][1]) * (step + 1 - first) // (end - first))

    def done_by(self, step):
        count = len(self.results)
        return sum(1 for n in range(count) if (n + 1) * self.STEPS // count <= step)


class Attend:

    def __init__(self, nc, mem, kind, otile, io, stream=None, first=0):
        self.nc, self.m, self.kind, self.otile, self.io = nc, mem, kind, otile, io
        self.stream, self.p0 = stream, first
        self.tail = None
        sem = lambda s: mem.sem(f"{kind}_{s}")
        self.opened = sem("opened")
        if kind in "AB":
            self.kv_out = nc.alloc_semaphore(f"{kind}_kv_out")
        if kind in "AD":
            self.strip_in = nc.alloc_semaphore(f"{kind}_strip_in")
        self.strip_masked = sem("strip_masked")
        if kind == "B":
            self.rest = sem("above_cut")
        self.turned, self.back_s, self.back_v = sem("turned"), sem("turned_read_by_scalar"), sem("turned_read_by_vector")
        self.scores = sem("scores")
        self.biased, self.maxed, self.front = sem("scores_biased"), sem("maximum"), sem("front")
        self.exps, self.logs, self.summed, self.sticks = sem("exps"), sem("logs"), sem("summed"), sem("sticks")
        self.probs = sem("probs")
        self.out, self.inv, self.normed = sem("out"), sem("inverse"), sem("normed")
        self.qcopied = sem("q_copied")
        self.uses = []
        if kind != "D":
            for blocks in ((0, 1, 2, 3), (4, 5, 6, 7), (8, 9), (10,)):
                self.uses.append(("v", blocks))
        self.unit_uses, self.out_use = [], {}
        for u in range(UNITS):
            nb = len(self.blocks(u))
            mine = []
            for g in range(0, nb, 4):
                mine.append(len(self.uses))
                self.uses.append((u, tuple(range(g, min(g + 4, nb)))))
            self.unit_uses.append(mine)
            if u >= 2 and u % 2 == 0:
                self.out_use[u // 2 - 1] = len(self.uses)
                self.uses.append(("o", (u // 2 - 1,)))
        self.out_use[NQT - 1] = len(self.uses)
        self.uses.append(("o", (NQT - 1,)))
        self.use_by = []
        for n, (u, bl) in enumerate(self.uses):
            if u == "v":
                self.use_by.append("s" if n % 2 == 0 else "v")
            elif u == "o" or kind == "B":
                self.use_by.append("s" if u == "o" else "v")
            else:
                self.use_by.append("v" if bl[0] >= 4 else "s")

    def keys(self, u):
        t = u // 2
        if t == NQT - 1:
            return (SEQ, KEYS_D) if self.kind == "D" else (SEQ, KEYS)
        back = {"A": 512, "D": 128, "B": SEQ, "C": SEQ}[self.kind]
        return max(0, P * t - back), P * t + P

    def nq(self, u):
        return DEC_SEQ if u // 2 == NQT - 1 else P

    def qcol(self, u):
        return S0 if u // 2 == NQT - 1 else P * (u // 2)

    def blocks(self, u):
        a, b = self.keys(u)
        return [(k, min(P, b - k)) for k in range(a, b, P)]

    def strip0(self, u):
        if self.kind == "A":
            return 256 if u // 2 == NQT - 1 else self.keys(u)[0] - (P * (u // 2) - 512)
        return 0 if u // 2 == NQT - 1 else self.keys(u)[0] - (P * (u // 2) - 128)

    def count(self, listing, n, who):
        return sum(1 for x in listing[:n] if x == who)

    def wait_back(self, e, j, n):
        for who, s in (("s", self.back_s), ("v", self.back_v)):
            c = self.count(self.use_by, n, who)
            if c:
                e.wait_ge(s, j * self.use_by.count(who) + c)

    def wait_turned_unit(self, e, j, u):
        e.wait_ge(self.turned, j * len(self.uses) + self.unit_uses[u][-1] + 1)

    def open(self, e, j):
        e.drain().then_inc(self.opened, 1)
        e.wait_ge(self.opened, j * 4 + 4)

    def wait_output(self, e, j, t):
        e.wait_ge(self.turned, j * len(self.uses) + self.out_use[t] + 1)

    def wait_all(self, e):
        e.wait_ge(self.back_s, PAIRS * self.use_by.count("s"))

    def pairs(self, e, body, last=False):
        if body == self.scalar:
            e.preload_act_table_set("natural_log_exp_and_others")
        if last:
            with e.Fori(0, PAIRS - 1) as j:
                body(e, j, True)
            body(e, PAIRS - 1, False)
        else:
            with e.Fori(0, PAIRS) as j:
                body(e, j, self.stream is not None)

    def tensor(self, e, j, more):
        m, st = self.m, self.stream
        self.open(e, j)
        if st:
            st.wait_left(e, j + self.p0, len(st.results))
            if self.kind != "C":
                e.wait_ge(m.cache_in, (j + self.p0) * 32 + 32)
            st.wait_moved(e, j + self.p0)
        else:
            e.wait_ge(self.qcopied, j + 1)
        for step in range(-1, UNITS + 2):
            if step + 1 < UNITS:
                self.pe_scores(e, j, step + 1)
            if step == -1 and st:
                self.pe_turn_v(e, j)
            if 1 <= step <= UNITS:
                self.pe_out(e, j, step - 1)
            if step >= 3 and step % 2:
                self.pe_turn_out(e, j, (step - 3) // 2)
            if more and step < UNITS:
                lo, hi = st.share(step), st.share(step + 1)
                mid = (lo + hi) // 2
                st.products(e, j + self.p0 + 1, lo, mid)
            elif self.tail and 0 <= step < UNITS:
                lo, hi = self.tail.share(step - 1) if step else 0, self.tail.share(step)
                mid = (lo + hi) // 2
                self.tail.products(e, j if self.kind == "D" else 0, lo, mid)
            if 0 <= step < UNITS:
                self.pe_turn(e, j, step)
            if more and step < UNITS:
                st.products(e, j + self.p0 + 1, mid, hi)
            elif self.tail and 0 <= step < UNITS:
                self.tail.products(e, j if self.kind == "D" else 0, mid, hi)

    def pe_turn_out(self, e, j, t):
        m = self.m
        nq, r = self.nq(2 * t), self.out_use[t]
        e.wait_ge(self.normed, j * NQT + t + 1)
        self.wait_back(e, j, r - 1)
        m.apart(e)
        e.transpose(m.pst[r % 2][:, 0:nq], m.otok[0:nq, :], m.ident[0:nq, 0:nq]).then_inc(self.turned, 1)

    def pe_turn_v(self, e, j):
        m = self.m
        for r in range(4):
            blocks = self.uses[r][1]
            if r >= 2:
                self.wait_back(e, j, r - 1)
            m.apart(e)
            for i, blk in enumerate(blocks):
                kw = min(P, KEYS - P * blk)
                mm = e.transpose(m.pst[r % 2][0:kw, P * i:P * i + P], m.vt[:, P * blk:P * blk + kw], m.ident[:, :])
            mm.then_inc(self.turned, 1)

    def pe_scores(self, e, j, u):
        m, hh = self.m, u % 2
        a, b = self.keys(u)
        nq, q0 = self.nq(u), self.qcol(u)
        if u >= 2:
            e.wait_ge({"A": self.front, "D": self.front, "B": self.sticks, "C": self.probs}[self.kind], j * UNITS + u - 1)
        if self.kind == "C":
            q, k = m.qh[hh], m.kh[hh]
            lo, hi = 0, C_NOPE + C_ROPE
        else:
            q, k = m.q, (m.kd if self.kind == "D" else m.k)
            lo, hi = HEAD * hh, HEAD * hh + HEAD
        if nq < P:
            m.apart(e)
        for c in range(0, b - a, 512):
            n = min(512, b - a - c)
            mm = e.matmul(m.ps[u % 2][0:nq, c:c + n], q[lo:hi, q0:q0 + nq], k[lo:hi, a + c:a + c + n], start=True, stop=True)
        w = b - a
        if self.kind == "B":
            d0 = lo if nq < P else 0
            mm = e.matmul(m.ps[u % 2][0:nq, w - nq:w], m.ident[d0:d0 + nq, d0:d0 + nq], m.causal[d0:d0 + nq, d0:d0 + nq],
                          start=False, stop=True,
                          skip_group_check=True)
        if self.kind == "C" and nq == P:
            mm = e.matmul(m.ps[u % 2][0:CHUNK, w - CHUNK:w], m.ones[:, 0:CHUNK], m.causal[:, P - CHUNK:P], start=True, stop=True,
                          skip_group_check=True)
        mm.then_inc(self.scores, 1)

    def pe_turn(self, e, j, u):
        m, nq = self.m, self.nq(u)
        e.wait_ge(self.probs, j * UNITS + u + 1)
        for r in self.unit_uses[u]:
            if r >= 2:
                self.wait_back(e, j, r - 1)
            m.apart(e)
            for i, blk in enumerate(self.uses[r][1]):
                kw = self.blocks(u)[blk][1]
                mm = e.transpose(m.pst[r % 2][0:kw, P * i:P * i + nq], m.wk[0:nq, u % 2, P * blk:P * blk + kw],
                                 m.ident[0:nq, 0:nq])
            mm.then_inc(self.turned, 1)

    def pe_out(self, e, j, u):
        m, nq, hh = self.m, self.nq(u), u % 2
        self.wait_back(e, j, self.unit_uses[u][-1] + 1)
        if hh == 0 and u >= 2:
            e.wait_ge(self.normed, j * NQT + u // 2)
        bl = self.blocks(u)
        v = m.vtok_d if self.kind == "D" else m.vtok
        m.apart(e)
        for i, (k, kw) in enumerate(bl):
            mm = e.matmul(m.po[0:nq, HEAD * hh:HEAD * hh + HEAD], m.pt[0:kw, P * i:P * i + nq],
                          v[0:kw, k // P, HEAD * hh:HEAD * hh + HEAD], start=i == 0, stop=i == len(bl) - 1,
                          skip_group_check=True)
        mm.then_inc(self.out, 1)

    def scalar(self, e, j, more):
        m, kind, st = self.m, self.kind, self.stream
        self.open(e, j)
        if st:
            st.move_scalar(e, j + self.p0)
        else:
            e.activation(m.q[:, :], m.o[:, bass.ds(j + self.otile, 1), :], ACT.Copy).then_inc(self.qcopied, 1)
        if more:
            st.wait_moved(e, j + self.p0)
        for step in range(-1, UNITS + 2):
            self.leave_next(e, "s", j, step, more)
            if more and not st.latent and step in st.SPLITS:
                st.split_high(e, j + self.p0, st.SPLITS[step])
            if kind == "B" and step + 1 < UNITS:
                u = step + 1
                nq, w = self.nq(u), self.keys(u)[1] - self.keys(u)[0]
                e.wait_ge(self.scores, j * UNITS + u + 1)
                if u:
                    e.wait_ge(self.summed, j * UNITS + u)
                e.activation(m.over[0:nq, 0:w], m.ps[u % 2][0:nq, 0:w], ACT.Relu, bias=m.cut[0:nq, :]).then_inc(self.rest, 1)
            if kind == "B" and 0 <= step < UNITS:
                nq, w = self.nq(step), self.keys(step)[1] - self.keys(step)[0]
                e.wait_ge(self.sticks, j * UNITS + step + 1)
                e.activation(m.wk[0:nq, step % 2, 0:w], m.wk[0:nq, step % 2, 0:w], ACT.Exp).then_inc(self.probs, 1)
            if step >= 3 and step % 2 == 1:
                self.sc_output(e, j, (step - 3) // 2)
            if step + 1 < UNITS:
                self.sc_weights(e, j, step + 1)
            if step == -1:
                self.read_v(e, "s", j)
            if 0 <= step < UNITS:
                for r in self.unit_uses[step]:
                    if self.use_by[r] == "s":
                        self.read_turned(e, "s", j, r)

    def leave_next(self, e, who, j, step, more):
        st = self.stream
        if more and 0 <= step <= UNITS:
            for n in range(st.done_by(step), st.done_by(step + 1)):
                if st.by[n] == who:
                    if st.results[n][1] == "v":
                        self.wait_v_free(e, j)
                    st.leave(e, who, j + self.p0 + 1, n)

    def wait_v_free(self, e, j):
        e.wait_ge(self.turned, j * len(self.uses) + 4)
        if self.kind in "AB":
            e.wait_ge(self.kv_out, j * 64 + 64)

    def sc_output(self, e, j, t):
        m = self.m
        nq, q0, r = self.nq(2 * t), self.qcol(2 * t), self.out_use[t]
        e.wait_ge(self.turned, j * len(self.uses) + r + 1)
        m.apart(e)
        e.activation(m.o[:, bass.ds(j + self.otile, 1), q0:q0 + nq], m.pst[r % 2][:, 0:nq], ACT.Copy).then_inc(self.back_s, 1)

    def sc_weights(self, e, j, u):
        m, kind = self.m, self.kind
        nq, w = self.nq(u), self.keys(u)[1] - self.keys(u)[0]
        wk = m.wk[0:nq, u % 2, 0:w]
        s8 = u % 8
        total = m.rowsum[0:nq, s8:s8 + 1]
        neg = m.negmax[0:nq, u % 2:u % 2 + 1]
        e.wait_ge(self.front, j * UNITS + u + 1)
        if kind == "B":
            e.activation(wk, wk, ACT.Exp).then_inc(self.exps, 1)
            e.wait_ge(self.exps, j * UNITS + u + 1)
            e.activation(wk, wk, ACT.Ln, bias=1.0).then_inc(self.logs, 1)
        elif kind == "C":
            if u >= 2:
                self.wait_turned_unit(e, j, u - 2)
            e.activation(wk, m.ps[u % 2][0:nq, 0:w], ACT.Exp, bias=neg, scale=C_SCALE, accum_out=total).then_inc(self.probs, 1)
        else:
            if kind == "D":
                e.activation(m.esink[0:nq, s8:s8 + 1], m.sink[0:nq, u % 2:u % 2 + 1], ACT.Exp, bias=neg)
            e.activation(wk, wk, ACT.Exp, bias=neg, accum_out=total).then_inc(self.probs, 1)

    def read_turned(self, e, who, j, r):
        m = self.m
        u, bl = self.uses[r]
        bank = m.pst[r % 2]
        e.wait_ge(self.turned, j * len(self.uses) + r + 1)
        sem = self.back_s if who == "s" else self.back_v

        def move(dst, src):
            return e.activation(dst, src, ACT.Copy) if who == "s" else e.tensor_copy(dst, src)

        if u == "v":
            rows = min(P, KEYS - P * bl[0])
            move(m.vtok[0:rows, bl[0]:bl[-1] + 1, :],
                 bank[0:rows, 0:P * len(bl)].rearrange("p (b f) -> p b f", f=P)).then_inc(sem, 1)
            return
        nq = self.nq(u)
        kws = [self.blocks(u)[b][1] for b in bl]
        full = [b for b, kw in zip(bl, kws) if kw == P]
        ops = []
        if nq == P:
            ops.append((m.pt[:, P * bl[0]:P * (bl[-1] + 1)], bank[:, 0:P * len(bl)]))
        else:
            n = len(full)
            v = lambda x: x.rearrange("p (b f) -> p b f", f=P)[:, :, 0:nq]
            ops.append((v(m.pt[:, P * bl[0]:P * (bl[0] + n)]), v(bank[:, 0:P * n])))
            if len(full) < len(bl):
                ops.append((m.pt[0:HEAD, P * (bl[0] + n):P * (bl[0] + n) + nq], bank[0:HEAD, P * n:P * n + nq]))
        for dst, src in ops:
            ins = move(dst, src)
        ins.then_inc(sem, 1)

    def read_v(self, e, who, j):
        for r, (u, _) in enumerate(self.uses):
            if u == "v" and self.use_by[r] == who:
                self.read_turned(e, who, j, r)

    def vector(self, e, j, more):
        m, kind, st = self.m, self.kind, self.stream
        self.open(e, j)
        if st:
            if kind != "C":
                e.wait_ge(m.cache_in, (j + self.p0) * 32 + 32)
            st.move_vector(e, j + self.p0)
        if kind == "A":
            e.wait_ge(self.strip_in, j * 16 + 16)
            e.memset(m.strip[0:64, :, 576:640], MASKED)
            e.memset(m.strip[64:128, :, 0:64], MASKED).then_inc(self.strip_masked, 1)
        if kind == "D":
            e.wait_ge(self.strip_in, j * 32 + 32)
        if kind == "A":
            e.wait_ge(self.strip_masked, j + 1)
        if more:
            st.wait_moved(e, j + self.p0)
        for step in range(-1, UNITS + 1):
            self.leave_next(e, "v", j, step, more)
            if not more and self.tail:
                self.tail.leave(e, j if kind == "D" else 0, step)
            if kind == "B" and 0 <= step < UNITS:
                self.ve_sticks(e, j, step)
            if step + 1 < UNITS:
                self.ve_front(e, j, step + 1)
            if step == -1:
                self.read_v(e, "v", j)
            if step >= 1 and step % 2 == 0:
                self.ve_normalise(e, j, step // 2 - 1)
            if 0 <= step < UNITS:
                for r in self.unit_uses[step]:
                    if self.use_by[r] == "v":
                        self.read_turned(e, "v", j, r)

    def ve_front(self, e, j, u):
        m, kind = self.m, self.kind
        nq, w = self.nq(u), self.keys(u)[1] - self.keys(u)[0]
        ps = m.ps[u % 2]
        wk = m.wk[0:nq, u % 2, 0:w]
        mx, neg = m.mx[0:nq, u % 2:u % 2 + 1], m.negmax[0:nq, u % 2:u % 2 + 1]
        e.wait_ge(self.scores, j * UNITS + u + 1)
        if u >= 2:
            self.wait_turned_unit(e, j, u - 2)
        if kind in "AD":
            s0 = self.strip0(u)
            m.apart(e)
            e.tensor_tensor_reduce(wk, ps[0:nq, 0:w], m.strip[0:nq, u % 2, s0:s0 + w], 1.0, -3e38,
                                   ALU.add, ALU.max, mx).then_inc(self.biased, 1)
            e.wait_ge(self.biased, j * UNITS + u + 1)
            if kind == "A":
                e.tensor_scalar(neg, mx, -1.0, None, ALU.mult).then_inc(self.front, 1)
            else:
                e.tensor_scalar(neg, mx, m.sink[0:nq, u % 2:u % 2 + 1], -1.0, ALU.max, ALU.mult).then_inc(self.front, 1)
        elif kind == "C":
            e.tensor_reduce(mx, ps[0:nq, 0:w], AX.X, ALU.max).then_inc(self.maxed, 1)
            e.wait_ge(self.maxed, j * UNITS + u + 1)
            e.tensor_scalar(neg, mx, -C_SCALE, None, ALU.mult).then_inc(self.front, 1)
        else:
            e.wait_ge(self.rest, j * UNITS + u + 1)
            e.tensor_scalar(wk, ps[0:nq, 0:w], 44.0, None, ALU.min).then_inc(self.front, 1)

    def ve_sticks(self, e, j, u):
        m = self.m
        nq, w = self.nq(u), self.keys(u)[1] - self.keys(u)[0]
        wk, run, over = m.wk[0:nq, u % 2, 0:w], m.run[0:nq, 0:w], m.over[0:nq, 0:w]
        z = m.ps[u % 2][0:nq, 0:w]
        e.wait_ge(self.logs, j * UNITS + u + 1)
        if u:
            e.wait_ge(self.sticks, j * UNITS + u)
        e.tensor_tensor_scan(run[:, ::-1], wk[:, ::-1], over[:, ::-1], 0.0, ALU.add, ALU.add).then_inc(self.summed, 1)
        e.wait_ge(self.summed, j * UNITS + u + 1)
        e.tensor_tensor(wk, z, run, ALU.subtract).then_inc(self.sticks, 1)

    def ve_normalise(self, e, j, t):
        m, kind = self.m, self.kind
        nq = self.nq(2 * t)
        e.wait_ge(self.out, j * UNITS + 2 * t + 2)
        if t >= 1:
            self.wait_output(e, j, t - 1)
        if kind == "B":
            e.tensor_copy(m.otok[0:nq, :], m.po[0:nq, 0:P]).then_inc(self.normed, 1)
            return
        s8 = (2 * t) % 8
        total = m.rowsum[0:nq, s8:s8 + 2]
        per = 2 if kind == "D" else 1
        if kind == "D":
            e.tensor_tensor(total, total, m.esink[0:nq, s8:s8 + 2], ALU.add).then_inc(self.inv, 1)
            e.wait_ge(self.inv, j * per * NQT + per * t + 1)
        e.reciprocal(total, total).then_inc(self.inv, 1)
        e.wait_ge(self.inv, j * per * NQT + per * t + per)
        for hh in range(2):
            ins = e.tensor_scalar(m.otok[0:nq, HEAD * hh:HEAD * hh + HEAD], m.po[0:nq, HEAD * hh:HEAD * hh + HEAD],
                                  total[:, hh:hh + 1], None, ALU.mult)
        ins.then_inc(self.normed, 1)

    def gpsimd(self, e, j, more):
        m, kind, io, st = self.m, self.kind, self.io, self.stream
        self.open(e, j)
        if kind in "AB":
            ok, ov, oks, ovs, k0, s0 = io.stores[kind]
            st.wait_left(e, j + self.p0, len(st.results))
            e.wait_ge(m.cache_in, (j + self.p0) * 32 + 32)
            m.apart(e)
            for dst, a, b in ((ov, k0, SEQ), (ovs, s0, KEYS)):
                e.dma_start(dst[bass.ds(j, 1)].rearrange("a p c -> (a p) c"), m.vt[:, a:b]).then_inc(self.kv_out, 16)
            st.wait_moved(e, j + self.p0)
            m.apart(e)
            for dst, a, b in ((ok, k0, SEQ), (oks, s0, KEYS)):
                e.dma_start(dst[bass.ds(j, 1)].rearrange("a p c -> (a p) c"), m.k[:, a:b]).then_inc(self.kv_out, 16)
            if more:
                e.wait_ge(self.kv_out, j * 64 + 64)
                e.wait_ge(self.turned, j * len(self.uses) + 4)
                m.apart(e)
                load_caches(e, m, io, j + self.p0 + 1)
            else:
                e.wait_ge(self.kv_out, j * 64 + 64)
        if more and not st.latent:
            for i in range(8, 13):
                st.split_low(e, j + self.p0, i)
        if kind in "AD":
            e.wait_ge(self.front, j * UNITS + UNITS)
            e.wait_ge(self.probs, j * UNITS + UNITS)
            m.apart(e)
            self.load_strip(e, j + 1)
        if more and not st.latent:
            st.split_low(e, j + self.p0, 13)

    def load_strip(self, e, j):
        m, io = self.m, self.io
        if self.kind == "A":
            e.dma_start(m.strip[:, :, :], io.bias[bass.ds(j, 1)].rearrange("a p h c -> p (a h) c")).then_inc(self.strip_in, 16)
        else:
            e.dma_start(m.strip[:, :, 0:256], io.alibi[bass.ds(j, 1)].rearrange("a p h c -> p (a h) c")).then_inc(self.strip_in, 16)
            with self.nc.allow_non_contiguous_dma(reason="two sinks per row"):
                e.dma_start(m.sink[:, :], io.sinks[bass.ds(j, 1)].rearrange("a p h -> p (a h)")).then_inc(self.strip_in, 16)


def load_caches(e, m, io, p):
    e.dma_start(m.k_next[:, SEQ:SEQ + PAST], io.cache_k[bass.ds(p, 1)].rearrange("a p c -> (a p) c")).then_inc(m.cache_in, 16)
    e.dma_start(m.vt[:, SEQ:SEQ + PAST], io.cache_v[bass.ds(p, 1)].rearrange("a p c -> (a p) c")).then_inc(m.cache_in, 16)


class Mem:
    pass


def weight_stream(e, m, src, count, ring):
    for s in range(ring):
        e.dma_start(m.w[:, s, :], src[s]).then_inc(m.w_in[s], 16)
    with e.Fori(0, count // ring - 1) as i:
        for s in range(ring):
            e.wait_ge(m.proj_ready, i * (3 * ring) + 3 * (s + 1))
            e.dma_start(m.w[:, s, :], src[bass.ds(i * ring + ring + s, 1)].rearrange("a p c -> (a p) c")).then_inc(m.w_in[s], 16)


class Project:

    def __init__(self, nc, mem, name, base, ring, units, moving, norm):
        self.m, self.base, self.ring, self.units, self.moving, self.norm = mem, base, ring, units, moving, norm
        self.left = mem.sem(f"{name}_left_psum")

    def tensor(self, e, between):
        m = self.m
        n = 0
        for w in range(self.units):
            if w in between:
                between[w](e)
            unit = self.base // 3 + w
            e.wait_ge(m.w_in[unit % self.ring], 16 * (unit // self.ring + 1))
            for c, (a, b) in enumerate(CUTS):
                if n >= 4:
                    e.wait_ge(self.left, n - 3)
                if w == 0:
                    self.norm.wait_cut(e, c)
                pb, off = bank_of(n)
                for k in range(KT):
                    mm = e.matmul(m.ps[pb][:, off:off + b - a], m.w[:, unit % self.ring, k * P:(k + 1) * P],
                                  self.moving(k, a, b), start=k == 0, stop=k == KT - 1)
                mm.then_inc(m.proj_ready, 1)
                n += 1

    def results(self, e, between):
        m = self.m
        for n in range(3 * self.units):
            w, c = divmod(n, 3)
            if c == 0 and w in between:
                between[w](e)
            a, b = CUTS[c]
            pb, off = bank_of(n)
            e.wait_ge(m.proj_ready, self.base + n + 1)
            yield n, w, c, a, b, m.ps[pb], off


class OutProject:

    def __init__(self, nc, mem, name, base, ring, first, filled, per_pair):
        self.m, self.base, self.ring, self.filled, self.per_pair = mem, base, ring, filled, per_pair
        self.first = first
        self.looped = filled > per_pair // 3
        self.bank_free, self.left = mem.sem(f"{name}_bank_free"), mem.sem(f"{name}_left")
        self.steps = UNITS // per_pair
        self.half = KT // 2

    def share(self, step):
        n, s = divmod(step, self.steps)
        return self.half * n + -(-self.half * (s + 1) // self.steps)

    def products(self, e, j, lo, hi):
        m = self.m
        for i in range(lo, hi):
            n, k = divmod(i, self.half)
            c = n % 3
            a, b = CUTS[c]
            if k == 0:
                if c == 0:
                    e.wait_ge(m.w_in[self.slot(n // 3)], self.level(n // 3, j))
                e.wait_ge(self.bank_free, j * self.per_pair + n + 1)
            mm = e.matmul(m.pnext[:, 0:b - a], m.w[:, self.slot(n // 3), k * P:(k + 1) * P], m.o[:, k, a:b],
                          start=k == 0, stop=k == self.half - 1)
        if hi > lo and hi % self.half == 0:
            mm.then_inc(m.proj_ready, 1)

    def slot(self, w):
        if self.looped:
            return w % 2 if w < self.filled else (w - self.filled + 2) % 4
        return (self.first + w) % self.ring

    def level(self, w, j=0):
        if self.looped:
            before = self.first // self.ring
            if w < self.filled:
                return j * 16 + 16 * (before + 1)
            if self.slot(w) < 2:
                before += self.filled // 2
            return 16 * (before + (w - self.filled) // 4 + 1)
        return 16 * ((self.first + w) // self.ring + 1)

    def leave(self, e, j, step):
        m = self.m
        if step > 0 and step % self.steps == 0:
            n = step // self.steps - 1
            a, b = CUTS[n % 3]
            e.wait_ge(m.proj_ready, j * self.per_pair + self.base + n + 1)
            if self.looped:
                m.apart(e)
                x = m.x[:, bass.ds(j * 2 + n // 3, 1), a:b].rearrange("p a c -> p (a c)")
            else:
                x = m.x[:, n // 3, a:b]
            e.tensor_tensor(x, m.pnext[:, 0:b - a], x, ALU.add).then_inc(self.bank_free, 1)

    def tensor(self, e):
        m = self.m
        n = 0
        e.wait_ge(self.bank_free, 3 * self.filled + 1)
        for w in range(self.filled, 2 * KT):
            e.wait_ge(m.w_in[self.slot(w)], self.level(w))
            for a, b in CUTS:
                if n >= 4:
                    e.wait_ge(self.left, n - 3)
                pb, off = bank_of(n)
                for k in range(self.half):
                    mm = e.matmul(m.ps[pb][:, off:off + b - a], m.w[:, self.slot(w), k * P:(k + 1) * P],
                                  m.o[:, self.half * (w // KT) + k, a:b], start=k == 0, stop=k == self.half - 1)
                mm.then_inc(m.proj_ready, 1)
                n += 1

    def vector(self, e):
        m = self.m
        for n in range(3 * (2 * KT - self.filled)):
            w, c = self.filled + n // 3, n % 3
            a, b = CUTS[c]
            pb, off = bank_of(n)
            e.wait_ge(m.proj_ready, self.base + 3 * self.filled + n + 1)
            x = m.x[:, w % KT, a:b]
            e.tensor_tensor(x, m.ps[pb][:, off:off + b - a], x, ALU.add).then_inc(self.left, 1)


class Ffn:
    RING = 3

    def __init__(self, nc, ctx, mem, name, weights, params, tails):
        self.nc, self.m, self.weights, self.params, self.tails = nc, mem, weights, params, tails
        sem = lambda s: mem.sem(f"{name}_{s}")
        self.raw_in = [sem(f"raw_in{i}") for i in range(self.RING)]
        self.high, self.low = sem("weight_high"), sem("weight_low")
        self.par_in = [sem(f"params_in{i}") for i in range(2)]
        self.tails_out = sem("tails_out")
        self.up, self.left = sem("up"), sem("up_left_psum")
        self.c1, self.conv = sem("conv_part"), sem("conv")
        self.silu, self.gate, self.ghigh, self.glow = sem("silu"), sem("gate"), sem("gate_high"), sem("gate_low")
        self.down, self.banks_free = sem("down"), sem("down_banks_free")

    def sync(self, e):
        m = self.m
        for s in range(self.RING):
            e.dma_start(m.raw[:, s, :], self.weights[s]).then_inc(self.raw_in[s], 16)
        e.dma_start(m.par[:, 0, :, :], self.params[0]).then_inc(self.par_in[0], 16)
        e.wait_ge(self.low, 1)
        e.dma_start(m.raw[:, 0, :], self.weights[3]).then_inc(self.raw_in[0], 16)
        with e.Fori(0, (GROUPS - 1) // 2) as i:
            for s in range(12):
                n = 4 + s
                e.wait_ge(self.low, i * 12 + n - 2)
                e.dma_start(m.raw[:, n % 3, :], self.weights[bass.ds(i * 12 + n, 1)].rearrange("a p c -> (a p) c")).then_inc(self.raw_in[n % 3], 16)
                if s in (0, 6):
                    q = 1 if s == 0 else 0
                    e.wait_ge(self.conv, i * 8 + (1 if s == 0 else 4))
                    e.dma_start(m.par[:, q, :, :], self.params[bass.ds(i * 2 + (1 if s == 0 else 2), 1)].rearrange("a p t c -> (a p) t c")).then_inc(self.par_in[q], 16)
        for n in (64, 65):
            e.wait_ge(self.low, n - 2)
            e.dma_start(m.raw[:, n % 3, :], self.weights[n]).then_inc(self.raw_in[n % 3], 16)

    def pe_up(self, e, i, g, norm=None):
        m = self.m
        for tile in range(4):
            n = tile if g == 0 else 4 + 6 * (g - 1) + tile
            e.wait_ge(self.low, i * 12 + n + 1)
            for c, (a, b) in enumerate(CUTS):
                q = 12 * g + 3 * tile + c
                if q >= 4:
                    e.wait_ge(self.left, i * 24 + q - 3)
                if norm and tile == 0:
                    norm.wait_cut(e, c)
                bank = m.ps4[q % 4]
                for k in range(KT):
                    for x, w, first in ((m.hh, m.wh, True), (m.hl, m.wh, False), (m.hh, m.wl, False)):
                        mm = e.matmul(bank[:, 0:b - a], w[:, n % 3, k * P:(k + 1) * P], x[:, k, a:b],
                                      start=k == 0 and first, stop=k == KT - 1 and w is m.wl)
                mm.then_inc(self.up, 1)

    def pe_down(self, e, i, g, last=False):
        m = self.m
        par = g % 2
        e.wait_ge(self.glow, i * 4 + 2 * g + 2)
        for mt in range(KT):
            n = (4 if last else 8) + 6 * g + mt // 4
            if mt % 4 == 0:
                e.wait_ge(self.low, i * 12 + n + 1)
            for c, (a, b) in enumerate(CUTS):
                q = 24 * g + 3 * mt + c
                e.wait_ge(self.banks_free, i * 48 + q + 1)
                bank = m.ps4[4 + q % 4]
                for k in range(2):
                    col = (mt % 4) * 2 * P + k * P
                    for x, w, first in ((m.gh, m.wh, True), (m.gl, m.wh, False), (m.gh, m.wl, False)):
                        mm = e.matmul(bank[:, 0:b - a], w[:, n % 3, col:col + P], x[:, 2 * par + k, a:b],
                                      start=k == 0 and first, stop=k == 1 and w is m.wl)
                mm.then_inc(self.down, 1)

    def tensor(self, e, norm):
        self.pe_up(e, 0, 0, norm)
        with e.Fori(0, (GROUPS - 1) // 2) as i:
            self.pe_up(e, i, 1)
            self.pe_down(e, i, 0)
            self.pe_up(e, i, 2)
            self.pe_down(e, i, 1)
        self.pe_down(e, (GROUPS - 1) // 2, 0, last=True)

    def wait_used(self, e, i, n):
        if n < 3:
            e.wait_ge(self.up, i * 24 + 3 * (n + 1))
            return
        if n == 3:
            e.wait_ge(self.up, i * 24 + 13)
            return
        g, s = divmod(n - 4, 6)
        if s < 4:
            e.wait_ge(self.up, i * 24 + 12 * (g + 1) + 3 * (s + 1))
        else:
            e.wait_ge(self.down, i * 48 + 24 * g + 12 * (s - 3))

    def sc_high(self, e, i, n):
        m = self.m
        s = n % 3
        e.wait_ge(self.raw_in[s], i * 64 + 16 * (n // 3 + 1))
        if n >= 3:
            self.wait_used(e, i, n - 3)
        e.activation(m.wh[:, s, :], m.raw[:, s, :], ACT.Copy).then_inc(self.high, 1)

    def sc_leave(self, e, i, g, tile, c):
        m = self.m
        q = 12 * g + 3 * tile + c
        tt = 4 * g + tile
        row = m.u[:, tt % 2, :]
        a, b = CUTS[c]
        bank = m.ps4[q % 4]
        e.wait_ge(self.up, i * 24 + q + 1)
        if c == 0:
            if tt >= 2:
                e.wait_ge(self.conv, i * 8 + tt - 1)
            if tile == 0:
                e.wait_ge(self.par_in[g % 2], i * 16 + 16 * (g // 2 + 1))
            e.activation(row[:, S0:S0 + 2], m.par[:, g % 2, tile, 4:6], ACT.Copy)
        if c < 2:
            e.activation(row[:, 2 + a:2 + b], bank[:, 0:b - a], ACT.Copy).then_inc(self.left, 1)
        else:
            if tile == 0 and g:
                e.wait_ge(self.tails_out, i * 32 + 16 * g)
            e.activation(row[:, 2 + a:2 + SEQ], bank[:, 0:SEQ - a], ACT.Copy)
            e.activation(row[:, 2 + S0:2 + T], bank[:, S0 - a:b - a], ACT.Copy)
            e.activation(m.tail[:, g % 2, 2 * tile, :], bank[:, SEQ - 2 - a:SEQ - a], ACT.Copy)
            e.activation(m.tail[:, g % 2, 2 * tile + 1, :], bank[:, T - 2 - a:T - a], ACT.Copy).then_inc(self.left, 1)

    def sc_up(self, e, i, g):
        m = self.m
        for tile in range(4):
            n = tile if g == 0 else 4 + 6 * (g - 1) + tile
            for c in range(3):
                self.sc_leave(e, i, g, tile, c)
                if c == 0:
                    self.sc_high(e, i, n + 2)
                    if tile % 2 == 0 and (g or tile):
                        self.sc_ghigh(e, i, 2 * g + tile // 2 - 1)
            if tile == 3:
                e.wait_ge(self.left, i * 24 + 12 * g + 12)
                dst = self.tails[0] if g == 0 else self.tails[bass.ds(i * 2 + g, 1)].rearrange("a p t c -> (a p) t c")
                e.dma_start(dst, m.tail[:, g % 2, :, :]).then_inc(self.tails_out, 16)
            if tile % 2:
                f = 2 * g + tile // 2
                e.wait_ge(self.conv, i * 8 + 2 * f + 1)
                if f:
                    e.wait_ge(self.glow, i * 4 + f)
                e.activation(m.sa[:, :], m.ca[:, :], ACT.Silu).then_inc(self.silu, 1)

    def sc_ghigh(self, e, i, f):
        m = self.m
        e.wait_ge(self.gate, i * 4 + f + 1)
        e.activation(m.gh[:, f % 4, :], m.sa[:, :], ACT.Copy).then_inc(self.ghigh, 1)

    def scalar(self, e, norm):
        L = (GROUPS - 1) // 2
        self.sc_high(e, 0, 0)
        self.sc_high(e, 0, 1)
        norm.scalar(e)
        self.sc_up(e, 0, 0)
        with e.Fori(0, L) as i:
            self.sc_up(e, i, 1)
            self.sc_high(e, i, 4 + 6)
            self.sc_high(e, i, 4 + 7)
            self.sc_up(e, i, 2)
            self.sc_high(e, i, 4 + 12)
            self.sc_high(e, i, 4 + 13)
        self.sc_ghigh(e, L, 1)
        e.wait_ge(self.tails_out, 16 * GROUPS)

    def po_low(self, e, i, n):
        m = self.m
        e.wait_ge(self.high, i * 12 + n + 1)
        e.tensor_tensor(m.wl[:, n % 3, :], m.raw[:, n % 3, :], m.wh[:, n % 3, :].bitcast(F32),
                        ALU.subtract).then_inc(self.low, 1)

    def po_glow(self, e, i, f):
        m = self.m
        e.wait_ge(self.ghigh, i * 4 + f + 1)
        e.tensor_tensor(m.gl[:, f % 4, :], m.sa[:, :], m.gh[:, f % 4, :].bitcast(F32), ALU.subtract).then_inc(self.glow, 1)

    def po_up(self, e, i, g):
        for tile in range(4):
            n = tile if g == 0 else 4 + 6 * (g - 1) + tile
            self.po_low(e, i, n + 2)
            if tile % 2 == 0 and (g or tile):
                self.po_glow(e, i, 2 * g + tile // 2 - 1)

    def gpsimd(self, e, norm):
        L = (GROUPS - 1) // 2
        self.po_low(e, 0, 0)
        self.po_low(e, 0, 1)
        norm.gpsimd(e)
        self.po_up(e, 0, 0)
        with e.Fori(0, L) as i:
            self.po_up(e, i, 1)
            self.po_low(e, i, 10)
            self.po_low(e, i, 11)
            self.po_up(e, i, 2)
            self.po_low(e, i, 16)
            self.po_low(e, i, 17)
        self.po_glow(e, L, 1)

    def ve_conv(self, e, i, g, tile):
        m = self.m
        tt = 4 * g + tile
        out = m.ca if tile % 2 == 0 else m.cb
        row = m.u[:, tt % 2, :]
        w = lambda x: m.par[:, g % 2, tile, x:x + 1]
        e.wait_ge(self.left, i * 24 + 3 * tt + 3)
        if tile % 2 == 0 and tt >= 2:
            e.wait_ge(self.silu, i * 4 + tt // 2)
        if tile % 2 and tt >= 2:
            e.wait_ge(self.gate, i * 4 + tt // 2)
        e.tensor_scalar(out[:, :], row[:, 0:T], w(0), w(3), ALU.mult, ALU.add).then_inc(self.c1, 1)
        e.wait_ge(self.c1, i * 16 + 2 * tt + 1)
        e.scalar_tensor_tensor(out[:, :], row[:, 1:T + 1], w(1), out[:, :], ALU.mult, ALU.add).then_inc(self.c1, 1)
        e.wait_ge(self.c1, i * 16 + 2 * tt + 2)
        e.scalar_tensor_tensor(out[:, :], row[:, 2:T + 2], w(2), out[:, :], ALU.mult, ALU.add).then_inc(self.conv, 1)

    def ve_gate(self, e, i, f):
        m = self.m
        e.wait_ge(self.silu, i * 4 + f + 1)
        e.wait_ge(self.conv, i * 8 + 2 * f + 2)
        e.tensor_tensor(m.sa[:, :], m.sa[:, :], m.cb[:, :], ALU.mult).then_inc(self.gate, 1)

    def ve_add(self, e, i, g, q0, q1):
        m = self.m
        for q in range(q0, q1):
            mt, c = divmod(q, 3)
            a, b = CUTS[c]
            bank = m.ps4[4 + (24 * g + q) % 4]
            e.wait_ge(self.down, i * 48 + 24 * g + q + 1)
            e.tensor_tensor(m.x[:, mt, a:b], bank[:, 0:b - a], m.x[:, mt, a:b], ALU.add).then_inc(self.banks_free, 1)

    def ve_up(self, e, i, g, head=0):
        self.ve_conv(e, i, g, 0)
        self.ve_conv(e, i, g, 1)
        self.ve_gate(e, i, 2 * g)
        self.ve_conv(e, i, g, 2)
        self.ve_conv(e, i, g, 3)
        if head:
            self.ve_add(e, i, g - 1, 0, head)
        self.ve_gate(e, i, 2 * g + 1)

    def vector(self, e):
        L = (GROUPS - 1) // 2
        e.sem_inc(self.banks_free, 4)
        self.ve_up(e, 0, 0)
        with e.Fori(0, L) as i:
            for g in (1, 2):
                self.ve_up(e, i, g, head=6)
                self.ve_add(e, i, g - 1, 6, 24)
        self.ve_add(e, L, 0, 0, 24)



def build(nc, io):
    with ExitStack() as top:
        m = Mem()
        sem = lambda s: top.enter_context(nc.semaphore(s))

        def sb(ctx, name, shape, dt=F32):
            return ctx.enter_context(nc.sbuf_tensor(name, shape, dt))

        m.ps = [top.enter_context(nc.psum_tensor(f"ps{i}", [P, 1024], F32)) for i in range(2)]
        m.pst = [top.enter_context(nc.psum_tensor(f"pst{i}", [P, 512], F32)) for i in range(2)]
        m.po = top.enter_context(nc.psum_tensor("po", [P, 512], F32))
        m.pot = top.enter_context(nc.psum_tensor("pot", [P, 512], F32))
        m.pnext = m.pot
        m.ps4 = [m.ps[0][:, 0:512], m.ps[0][:, 512:1024], m.ps[1][:, 0:512], m.ps[1][:, 512:1024],
                 m.pst[0], m.pst[1], m.po, m.pot]
        m.x = sb(top, "x", [P, KT, T])
        m.ident = sb(top, "ident", [P, P])
        m.ones = sb(top, "ones", [P, P])
        m.causal = sb(top, "causal", [P, P])
        m.gains = sb(top, "gains", [P, N_GAINS])
        loaded, consts, x_in = sem("loaded"), sem("consts"), [sem(f"x_in{c}") for c in range(3)]
        waited = sem("waited")

        def apart(e):
            e.sem_inc(waited, 1)
        m.apart = apart

        phase = []

        def phase_sem(name):
            phase.append(nc.alloc_semaphore(name))
            return phase[-1]
        m.sem = phase_sem

        def end_phase():
            nums = sorted(s.num for s in phase)
            runs = [[nums[0], nums[0]]]
            for n in nums[1:]:
                if n == runs[-1][1] + 1:
                    runs[-1][1] = n
                else:
                    runs.append([n, n])
            with nc.Block() as block:
                @block.gpsimd
                def _(e):
                    for a, b in runs:
                        e.sem_clear(range(a, b + 1))
            for s in phase:
                nc.release_semaphore(s)
            phase.clear()

        def norm_of_x(name, gain0, dst=None, split=None, arrived=None):
            return Norm(nc, m, name, lambda k, a, b: m.x[:, k, a:b], CUTS, KT, D_MODEL, gain0, dst, split, arrived=arrived)

        def ring4(flat):
            return flat[:, 0:4 * 384].rearrange("p (a b) -> p a b", a=4)

        def load_x(e):
            e.dma_start(m.gains[:, :], io.gains).then_inc(loaded, 16)
            for c, (a, b) in enumerate(CUTS):
                for h in range(2):
                    e.dma_start(m.x[:, 4 * h:4 * h + 4, a:b], io.x[:, 4 * h:4 * h + 4, a:b]).then_inc(x_in[c], 16)

        def make_constants(e):
            e.memset(m.ones[:, :], 1.0).then_inc(consts, 1)
            e.memset(m.cut[:, :], -44.0)
            e.memset(m.ident[:, :], 0.0).then_inc(consts, 1)
            e.memset(m.causal[:, :], 0.0).then_inc(consts, 1)
            e.wait_ge(consts, 3)
            e.affine_select(out=m.ident[:, :], in_=m.ident[:, :], compare_op=ALU.not_equal, fill=1.0,
                            base=0, pattern=[[-1, P]], channel_multiplier=1).then_inc(consts, 1)
            e.affine_select(out=m.causal[:, :], in_=m.causal[:, :], compare_op=ALU.is_gt, fill=MASKED,
                            base=0, pattern=[[-1, P]], channel_multiplier=1).then_inc(consts, 1)

        def ffn_layer(layer):
            with ExitStack() as ctx:
                m.hh = sb(ctx, f"hh{layer}", [P, KT, T], F32R)
                m.hl = sb(ctx, f"hl{layer}", [P, KT, T], F32R)
                norm = norm_of_x(f"norm_ffn{layer}", GAIN_FFN[layer], split=(m.hh, m.hl))
                m.raw = sb(ctx, f"raw{layer}", [P, 3, 1024])
                m.wh = sb(ctx, f"wh{layer}", [P, 3, 1024], F32R)
                m.wl = sb(ctx, f"wl{layer}", [P, 3, 1024], F32R)
                m.u = sb(ctx, f"u{layer}", [P, 2, T + 2])
                gates = sb(ctx, f"gates{layer}", [P, 3 * T])
                m.ca, m.cb, m.sa = (gates[:, i * T:(i + 1) * T] for i in range(3))
                m.sq, m.tmp = ring4(gates), ring4(gates[:, 4 * 384:8 * 384])
                m.rms = sb(ctx, f"rms_ffn{layer}", [P, 3, 384])
                m.gh = sb(ctx, f"gh{layer}", [P, 4, T], F32R)
                m.gl = sb(ctx, f"gl{layer}", [P, 4, T], F32R)
                m.par = sb(ctx, f"par{layer}", [P, 2, 4, 6])
                m.tail = sb(ctx, f"tail{layer}", [P, 2, 8, 2])
                f = Ffn(nc, ctx, m, f"ffn{layer}", io.ffn_w[layer], io.ffn_p[layer], io.tails[layer])
                halo0 = m.sem(f"halo_zero{layer}")
                with nc.Block() as block:
                    @block.sync
                    def _(e):
                        f.sync(e)

                    @block.gpsimd
                    def _(e):
                        e.memset(m.u[:, :, 0:2], 0.0).then_inc(halo0, 1)
                        f.gpsimd(e, norm)

                    @block.scalar
                    def _(e):
                        f.scalar(e, norm)

                    @block.tensor
                    def _(e):
                        norm.tensor(e)
                        f.tensor(e, norm)

                    @block.vector
                    def _(e):
                        norm.vector(e)
                        e.wait_ge(halo0, 1)
                        norm.wait_cut(e, 2)
                        f.vector(e)

        def attention_scratch(ctx, layer, ring, width):
            m.w = sb(ctx, f"w{layer}", [P, ring, width])
            m.o = sb(ctx, f"o{layer}", [P, KT, T])
            m.wk = sb(ctx, f"wk{layer}", [P, 2, 1024])
            m.pt = sb(ctx, f"pt{layer}", [P, 1024])
            m.strip = sb(ctx, f"strip{layer}", [P, 2, 640])
            m.otok = sb(ctx, f"otok{layer}", [P, P])
            m.mx, m.negmax = sb(ctx, f"mx{layer}", [P, 2]), sb(ctx, f"negmax{layer}", [P, 2])
            m.rowsum, m.esink = sb(ctx, f"rowsum{layer}", [P, 8]), sb(ctx, f"esink{layer}", [P, 8])
            m.sink = sb(ctx, f"sink{layer}", [P, 2])
            m.w_in = [m.sem(f"w_in{layer}_{i}") for i in range(ring)]
            m.proj_ready = m.sem(f"projected{layer}")

        with ExitStack() as ctx:
            m.hh, m.hl = sb(ctx, "hh_mix0", [P, KT, T], F32R), sb(ctx, "hl_mix0", [P, KT, T], F32R)
            norm = norm_of_x("norm_mix0", GAIN_MIX[0], split=(m.hh, m.hl),
                             arrived=lambda e, c: e.wait_ge(x_in[c], 32))
            attention_scratch(ctx, 0, 3, 512)
            m.wh, m.wl = sb(ctx, "wh_mix0", [P, 3, 512], F32R), sb(ctx, "wl_mix0", [P, 3, 512], F32R)
            m.over = sb(ctx, "over", [P, 1024])
            m.cut = sb(ctx, "cut", [P, 1])
            m.run = m.strip[:, :, :].rearrange("p a b -> p (a b)")
            free = m.o[:, :, :].rearrange("p a b -> p (a b)")
            m.tmp, m.rms = ring4(free), free[:, 4 * 384:7 * 384].rearrange("p (a b) -> p a b", a=3)
            m.sq = ring4(m.wk[:, :, :].rearrange("p a b -> p (a b)"))
            m.q, m.k, m.vt = sb(ctx, "q", [P, T]), sb(ctx, "k", [P, KEYS]), sb(ctx, "vt", [P, KEYS])
            m.q_next, m.k_next = sb(ctx, "q_next", [P, T]), sb(ctx, "k_next", [P, KEYS])
            m.cache_in = nc.alloc_semaphore("cache_in0")
            m.vtok = sb(ctx, "vtok", [P, 11, P])
            st = Stream(nc, m, "pairs0", ("q", "k", "v"), 0, 3)
            a = Attend(nc, m, "A", 0, io, st, 0)
            b = Attend(nc, m, "B", PAIRS, io, st, PAIRS)
            out = b.tail = OutProject(nc, m, "out0", 72, 3, 48, filled=UNITS // 3, per_pair=UNITS)
            gap = m.sem("gap0")
            with nc.Block() as block:
                @block.sync
                def _(e):
                    load_x(e)
                    for i in range(3):
                        e.dma_start(m.w[:, i, :], io.w0[i]).then_inc(m.w_in[i], 16)
                    with e.Fori(0, 16) as i:
                        for s in range(3):
                            e.wait_ge(st.low, i * 3 + s + 1)
                            e.dma_start(m.w[:, s, :], io.w0[bass.ds(i * 3 + 3 + s, 1)].rearrange("a p c -> (a p) c")).then_inc(m.w_in[s], 16)
                    e.wait_ge(st.low, 50)
                    with e.Fori(0, 4) as i:
                        for s in range(3):
                            e.wait_ge(m.proj_ready, i * 9 + out.base + 3 * (s + 1))
                            e.dma_start(m.w[:, s, :], io.w0[bass.ds(i * 3 + 51 + s, 1)].rearrange("a p c -> (a p) c")).then_inc(m.w_in[s], 16)
                    e.wait_ge(m.proj_ready, out.base + 39)
                    e.dma_start(m.w[:, 0, :], io.w0[63]).then_inc(m.w_in[0], 16)

                @block.gpsimd
                def _(e):
                    make_constants(e)
                    load_caches(e, m, io, 0)
                    a.load_strip(e, 0)
                    for i in range(3):
                        st.split_low(e, 0, i)
                    norm.gpsimd(e)
                    for i in range(3, 8):
                        st.split_low(e, 0, i)
                    norm.wait_cut(e, 2)
                    e.memset(m.o[:, :, SEQ:S0], 0.0).then_inc(gap, 1)
                    a.pairs(e, a.gpsimd)
                    e.wait_ge(a.strip_in, 16 * (PAIRS + 1))
                    b.pairs(e, b.gpsimd, last=True)

                @block.scalar
                def _(e):
                    norm.scalar(e, lambda e: [st.split_high(e, 0, i) for i in range(3)])
                    st.first(e, "s")
                    a.pairs(e, a.scalar)
                    b.pairs(e, b.scalar, last=True)

                @block.tensor
                def _(e):
                    e.wait_ge(consts, 5)
                    norm.tensor(e)
                    st.products(e, 0, 0, len(st.pieces), norm)
                    a.pairs(e, a.tensor)
                    e.wait_ge(gap, 1)
                    a.wait_all(e)
                    b.pairs(e, b.tensor, last=True)
                    b.wait_all(e)
                    out.tensor(e)

                @block.vector
                def _(e):
                    e.wait_ge(loaded, 16)
                    norm.vector(e)
                    st.first(e, "v")
                    a.pairs(e, a.vector)
                    e.sem_inc(out.bank_free, 1)
                    b.pairs(e, b.vector, last=True)
                    out.vector(e)
        ffn_layer(0)
        end_phase()

        with ExitStack() as ctx:
            m.hn = sb(ctx, "hn1", [P, KT, T])
            norm = norm_of_x("norm_mix1", GAIN_MIX[1], dst=lambda k, a, b: m.hn[:, k, a:b])
            attention_scratch(ctx, 1, 4, 1024)
            m.run = sb(ctx, "run1", [P, KEYS_D])
            m.q = sb(ctx, "q1", [P, T])
            m.cq, m.ckv = sb(ctx, "cq", [P, C_Q // P, T]), sb(ctx, "ckv", [P, C_KV // P, KEYS])
            m.kd, m.vtok_d = sb(ctx, "kd", [P, KEYS_D]), sb(ctx, "vtok_d", [P, 10, P])
            m.kp, m.rot = sb(ctx, "kp", [P, KEYS]), sb(ctx, "rot", [P, T])
            m.rms = sb(ctx, "rms1", [P, 4, 384])
            m.sq = m.wk[:, :, :].rearrange("p a b -> p (a b)")[:, 0:4 * 384].rearrange("p (a b) -> p a b", a=4)
            flat = m.hn[:, :, :].rearrange("p a b -> p (a b)")
            m.qh = [flat[:, i * T:(i + 1) * T] for i in range(2)]
            m.kh = [flat[:, 2 * T + i * KEYS:2 * T + (i + 1) * KEYS] for i in range(2)]
            at = 2 * T + 2 * KEYS
            m.vt = flat[:, at:at + KEYS]
            m.qr_next = flat[0:64, at + KEYS + 11 * P:at + KEYS + 11 * P + T]
            m.q_next, m.k_next = sb(ctx, "qn_next", [P, T]), sb(ctx, "kn_next", [P, KEYS])
            m.ropes = sb(ctx, "ropes", [64, 2, 384])
            m.vtok = flat[:, at + KEYS:at + KEYS + 11 * P].rearrange("p (b f) -> p b f", f=P)
            inp = Project(nc, m, "in1", 0, 4, 12, lambda k, a, b: m.hn[:, k, a:b], norm)
            kv_cols = [(0, 384), (384, 768), (768, SEQ), (SEQ + PAST, KEYS)]
            free = [m.pst[0], m.pst[1], m.po, m.pot]
            nq = Norm(nc, m, "norm_q", lambda k, a, b: m.cq[:, k, a:b], CUTS, 3, C_Q, GAIN_Q,
                      lambda k, a, b: m.cq[:, k, a:b], banks=free)
            nkv = Norm(nc, m, "norm_kv", lambda k, a, b: m.ckv[:, k, a:b], kv_cols, 2, C_KV, GAIN_KV,
                       lambda k, a, b: m.ckv[:, k, a:b], banks=free)
            st = Stream(nc, m, "pairs1", ("qn", "qr", "kn", "v"), 36, 4)
            c = Attend(nc, m, "C", 0, io, st, 0)
            d = Attend(nc, m, "D", PAIRS, io)
            out = d.tail = OutProject(nc, m, "out1", 84, 4, 28, filled=KT, per_pair=3 * KT // PAIRS)
            s = m.sem
            gap, roped, vturned, vleft = s("gap1"), s("roped1"), s("vd_turned"), s("vd_left")
            cache_in, stored = nc.alloc_semaphore("cache_in1"), nc.alloc_semaphore("stored1")
            new0 = SEQ + PAST
            vd_uses = ((0, 1, 2, 3), (4, 5, 6, 7), (8,), (9,))
            with nc.Block() as block:
                @block.sync
                def _(e):
                    weight_stream(e, m, io.w1, 12, 4)
                    with e.Fori(0, PAIRS) as j:
                        for s, (src, width) in enumerate(((io.c_q, 384), (io.c_q, 384), (io.c_kv, 256), (io.c_kv, 256))):
                            e.wait_ge(m.proj_ready, j * 12 + 3 * (12 + s - 3))
                            e.dma_start(m.w[:, s, 0:width], src[bass.ds(j * 2 + s % 2, 1)].rearrange("a p c -> (a p) c")).then_inc(m.w_in[s], 16)
                    with e.Fori(0, PAIRS) as j:
                        for w in range(2):
                            e.wait_ge(m.proj_ready, j * 6 + out.base - 3 + 3 * w)
                            e.dma_start(m.w[:, w, 0:512], io.w1_out[bass.ds(j * 2 + w, 1)].rearrange("a p c -> (a p) c")).then_inc(m.w_in[w], 16)
                    for w in range(KT, 2 * KT):
                        if w >= KT + 2:
                            e.wait_ge(m.proj_ready, out.base + 3 * (w - 3 if w >= KT + 4 else w - 4 + 1))
                        e.dma_start(m.w[:, out.slot(w), 0:512], io.w1_out[w]).then_inc(m.w_in[out.slot(w)], 16)

                @block.gpsimd
                def _(e):
                    e.dma_start(m.rot[:, :], io.rot).then_inc(cache_in, 16)
                    e.dma_start(m.ckv[:, :, SEQ:new0], io.cache_c).then_inc(cache_in, 16)
                    e.dma_start(m.kp[HEAD:HEAD + C_ROPE, SEQ:new0], io.cache_pe).then_inc(cache_in, 16)
                    e.dma_start(m.kd[:, SEQ:SEQ + D_CACHE], io.cache_dk).then_inc(cache_in, 16)
                    e.dma_start(m.run[:, SEQ:SEQ + D_CACHE], io.cache_dv).then_inc(cache_in, 16)
                    e.memset(m.o[:, 0:PAIRS, SEQ:S0], 0.0).then_inc(gap, 1)
                    e.wait_ge(inp.left, 36)
                    e.wait_ge(cache_in, 80)
                    for dst, src in ((io.dk, m.kd[:, SEQ - P:SEQ]), (io.dks, m.kd[:, KEYS_D - D_CACHE:KEYS_D]),
                                     (io.dv, m.run[:, SEQ - P:SEQ]), (io.dvs, m.run[:, KEYS_D - D_CACHE:KEYS_D]),
                                     (io.kpe, m.kp[HEAD:HEAD + C_ROPE, 0:SEQ]), (io.kpes, m.kp[HEAD:HEAD + C_ROPE, new0:KEYS])):
                        e.dma_start(dst, src).then_inc(stored, 16)
                    e.wait_ge(nkv.normed, 8)
                    e.dma_start(io.ckv, m.ckv[:, :, 0:SEQ]).then_inc(stored, 16)
                    e.dma_start(io.ckvs, m.ckv[:, :, new0:KEYS]).then_inc(stored, 16)
                    e.wait_ge(stored, 128)
                    d.load_strip(e, 0)
                    c.pairs(e, c.gpsimd, last=True)
                    d.pairs(e, d.gpsimd)
                    e.wait_ge(d.strip_in, 32 * (PAIRS + 1))

                @block.scalar
                def _(e):
                    norm.scalar(e)
                    e.wait_ge(inp.left, 18)
                    nq.scalar(e)
                    e.wait_ge(nq.normed, 9)
                    nkv.scalar(e)
                    e.wait_ge(nkv.normed, 8)
                    st.first(e, "s")
                    c.pairs(e, c.scalar, last=True)
                    d.pairs(e, d.scalar)

                @block.tensor
                def _(e):
                    norm.tensor(e)
                    def sum_kv(e):
                        e.wait_ge(nq.normed, 9)
                        nkv.tensor(e)
                    inp.tensor(e, {8: nq.tensor, 10: sum_kv})
                    e.wait_ge(nkv.normed, 8)
                    e.wait_ge(inp.left, 36)
                    e.wait_ge(cache_in, 80)
                    for r, blocks in enumerate(vd_uses):
                        if r >= 2:
                            e.wait_ge(vleft, r - 1)
                        for i, blk in enumerate(blocks):
                            kw = min(P, KEYS_D - P * blk)
                            mm = e.transpose(m.pst[r % 2][0:kw, P * i:P * i + P], m.run[:, P * blk:P * blk + kw], m.ident[:, :])
                        mm.then_inc(vturned, 1)
                    st.products(e, 0, 0, len(st.pieces))
                    c.pairs(e, c.tensor, last=True)
                    e.wait_ge(gap, 1)
                    c.wait_all(e)
                    d.pairs(e, d.tensor)
                    d.wait_all(e)
                    out.tensor(e)

                @block.vector
                def _(e):
                    norm.vector(e)
                    for n, w, cut, a_, b_, ps, off in inp.results(e, {8: nq.vector, 10: nkv.vector}):
                        src = ps[:, off:off + b_ - a_]
                        if w < 3:
                            e.tensor_copy(m.cq[:, w, a_:b_], src).then_inc(inp.left, 1)
                        elif w < 5 or w in (6, 7):
                            dst = m.ckv[:, w - 3, :] if w < 5 else (m.kd if w == 6 else m.run)
                            end = KEYS if w < 5 else KEYS_D
                            if cut < 2:
                                e.tensor_copy(dst[:, a_:b_], src).then_inc(inp.left, 1)
                            else:
                                e.tensor_copy(dst[:, a_:SEQ], src[:, 0:SEQ - a_])
                                e.tensor_copy(dst[:, end - DEC_SEQ:end], src[:, S0 - a_:b_ - a_]).then_inc(inp.left, 1)
                        elif w == 5:
                            n_ = b_ - a_
                            ta, tb = m.wk[0:32, 0, 0:n_], m.wk[0:32, 1, 0:n_]
                            if cut == 0:
                                e.wait_ge(cache_in, 80)
                            else:
                                e.wait_ge(inp.left, n)
                            e.tensor_tensor(ta, src[0:32, :], m.rot[0:32, a_:b_], ALU.mult)
                            e.tensor_tensor(tb, src[64:96, :], m.rot[64:96, a_:b_], ALU.mult).then_inc(roped, 1)
                            e.wait_ge(roped, cut + 1)
                            kp = m.kp[HEAD:HEAD + C_ROPE, :]
                            if cut < 2:
                                e.tensor_tensor(kp[:, a_:b_], ta, tb, ALU.add).then_inc(inp.left, 1)
                            else:
                                e.tensor_tensor(kp[:, a_:SEQ], ta[:, 0:SEQ - a_], tb[:, 0:SEQ - a_], ALU.add)
                                e.tensor_tensor(kp[:, new0:KEYS], ta[:, S0 - a_:n_], tb[:, S0 - a_:n_], ALU.add).then_inc(inp.left, 1)
                        else:
                            e.tensor_scalar(m.o[:, PAIRS + w - 8, a_:b_], src, SCALE, None, ALU.mult).then_inc(inp.left, 1)
                    for r, blocks in enumerate(vd_uses):
                        rows = min(P, KEYS_D - P * blocks[0])
                        e.wait_ge(vturned, r + 1)
                        e.tensor_copy(m.vtok_d[0:rows, blocks[0]:blocks[-1] + 1, :],
                                      m.pst[r % 2][0:rows, 0:P * len(blocks)].rearrange("p (b f) -> p b f", f=P)).then_inc(vleft, 1)
                    st.first(e, "v")
                    for h in range(2):
                        e.tensor_copy(m.kh[h][HEAD:HEAD + C_ROPE, :], m.kp[HEAD:HEAD + C_ROPE, :])
                    c.pairs(e, c.vector, last=True)
                    e.sem_inc(out.bank_free, 1)
                    d.pairs(e, d.vector)
                    out.vector(e)
        end_phase()
        ffn_layer(1)
        with ExitStack() as ctx:
            norm = norm_of_x("norm_final", GAIN_FINAL, dst=lambda k, a, b: m.x[:, k, a:b])
            m.sq, m.rms = sb(ctx, "sq_final", [P, 4, 384]), sb(ctx, "rms_final", [P, 3, 384])
            with nc.Block() as block:
                @block.sync
                def _(e):
                    for c, (a, b) in enumerate(CUTS):
                        norm.wait_cut(e, c)
                        e.dma_start(io.y[:, :, a:b], m.x[:, :, a:b]).then_inc(loaded, 16)
                    e.wait_ge(loaded, 16 * 4)

                @block.scalar
                def _(e):
                    norm.scalar(e)

                @block.tensor
                def _(e):
                    norm.tensor(e)

                @block.vector
                def _(e):
                    norm.vector(e)


def kernel(**inputs):
    import numpy as np
    import concourse.bacc as bacc
    from concourse.bass_utils import run_bass_kernel_spmd

    g = {k: np.asarray(v) for k, v in inputs.items()}
    f32 = np.float32

    def tiles(w):
        k, n = w.shape
        return w.reshape(k // P, P, n // P, P).transpose(2, 1, 0, 3).reshape(n // P, P, k)

    def cols(w, size=HEAD):
        return w.reshape(w.shape[0], -1, size)

    arrays = {}
    x = np.zeros((T, D_MODEL), f32)
    x[:SEQ], x[S0:] = g["x_prompt"][0], g["x_sample"][0]
    arrays["x"] = x.T.reshape(KT, P, T).transpose(1, 0, 2)
    gains = [g["norm_mix"][0], g["norm_mix"][1], g["norm_ffn"][0], g["norm_ffn"][1], g["norm_final"],
             g["odd_norm_q"][0], g["odd_norm_kv"][0]]
    arrays["gains"] = np.concatenate(gains).reshape(N_GAINS, P).T
    w = g["even_w_in"][0]
    a_and_b = tiles(w).reshape(2, 3, PAIRS, P, D_MODEL).transpose(0, 2, 1, 3, 4).reshape(24, P, D_MODEL)
    halves = lambda w: w.reshape(KT, P, 2, 512).transpose(2, 0, 1, 3).reshape(2 * KT, P, 512)
    pair_halves = a_and_b.reshape(24, P, 2, 512).transpose(0, 2, 1, 3).reshape(48, P, 512)
    arrays["w0"] = np.concatenate([pair_halves, halves(tiles(g["even_w_out"][0]))])
    idx = np.clip(512 + np.arange(P)[:, None] - np.arange(640), -256, 256) + 256
    more = lambda z: np.concatenate([z, z[:1]])
    arrays["bias"] = more(g["even_rel_bias"][0].reshape(PAIRS, 2, -1)[:, :, idx].transpose(0, 2, 1, 3))
    pair = lambda c: np.moveaxis(c.reshape(c.shape[-3], PAIRS, P), 0, -1)
    for kv in "kv":
        arrays[f"cache_{kv}"] = np.concatenate([pair(g[f"cache_{n}_{kv}"][0, 0]) for n in "ab"])
    w = g["odd_w_in"][0]
    o = np.cumsum([0, C_Q, C_KV, C_ROPE, 512, 128, 128])
    part = [w[:, o[i]:o[i + 1]] for i in range(6)]
    swap = lambda z: np.concatenate([z[..., C_ROPE // 2:], z[..., :C_ROPE // 2]], axis=-1)
    kpe = part[2]
    qd = cols(part[3])
    qd = np.stack([qd[:, :PAIRS], qd[:, PAIRS:]], axis=2).reshape(D_MODEL, 512)
    arrays["w1"] = tiles(np.concatenate([part[0], part[1], kpe, kpe, swap(kpe), swap(kpe), part[4], part[5], qd], axis=1))
    uq = g["odd_w_uq"][0]
    nope, rope = uq[:, :, :C_NOPE], uq[:, :, C_NOPE:]
    both = lambda z: z.reshape(C_Q, PAIRS, 1, -1)
    r2 = np.concatenate([both(rope), both(swap(rope))], axis=2).reshape(C_Q, PAIRS, 1, P)
    arrays["c_q"] = tiles(np.concatenate([both(nope), r2], axis=2).reshape(C_Q, 2 * PAIRS * P))
    ukv = g["odd_w_ukv"][0].reshape(C_KV, PAIRS, 2, 2, HEAD).transpose(0, 1, 3, 2, 4)
    arrays["c_kv"] = tiles(ukv.reshape(C_KV, 2 * PAIRS * P))
    wo = g["odd_w_out"][0]
    d_rows = wo[512:].reshape(2, PAIRS, HEAD, D_MODEL).transpose(1, 0, 2, 3).reshape(512, D_MODEL)
    arrays["w1_out"] = halves(tiles(np.concatenate([wo[:512], d_rows])))
    arrays["cache_c"] = g["cache_c_kv"][0, 0].T.reshape(C_KV // P, P, PAST).transpose(1, 0, 2)
    arrays["cache_pe"] = g["cache_c_kpe"][0, 0].T
    arrays["cache_dk"] = g["cache_d_k"][0, 0].reshape(D_CACHE, P).T
    arrays["cache_dv"] = g["cache_d_v"][0, 0].reshape(D_CACHE, P).T
    arrays["sinks"] = more(g["odd_sinks"][0].reshape(2, PAIRS).T)
    pos = np.zeros(T, f32)
    pos[:SEQ], pos[S0:] = np.arange(SEQ), PAST + np.arange(DEC_SEQ)
    inv = (f32(10000.0) ** (-np.arange(16, dtype=f32) / f32(16))).astype(f32)
    ang = (pos[None, :] * inv[:, None]).astype(f32)
    cos, sin = np.cos(ang).astype(f32), np.sin(ang).astype(f32)
    arrays["rot"] = np.concatenate([cos, cos, cos, cos, -sin, sin, -sin, sin])
    p_, c_ = np.arange(P)[:, None], np.arange(256)[None, :]
    seen = np.where(p_ < CHUNK, c_ < 192, c_ >= 64)
    slopes = (f32(2.0) ** (f32(-8.0) * np.arange(1, 9, dtype=f32) / f32(8))).astype(f32)
    pen = np.where(seen[None], -slopes[:, None, None] * np.abs(128 + p_ - c_)[None].astype(f32), f32(MASKED)).astype(f32)
    arrays["alibi"] = more(pen.reshape(2, PAIRS, P, 256).transpose(1, 2, 0, 3))
    for layer in range(2):
        wi = tiles(g["ffn_w_in"][layer]).reshape(2, GROUPS, 2, P, D_MODEL).transpose(1, 2, 0, 3, 4).reshape(GROUPS, 4, P, 1024)
        wo = g["ffn_w_out"][layer].reshape(GROUPS, 2, P, 2, 4, P).transpose(0, 3, 2, 4, 1, 5).reshape(GROUPS, 2, P, 1024)
        order = [wi[0]] + [z for k in range(1, GROUPS) for z in (wi[k], wo[k - 1])] + [wo[GROUPS - 1]]
        arrays[f"ffn_w{layer}"] = np.concatenate(order)
        pr = np.concatenate([g["ffn_conv_w"][layer], g["ffn_conv_b"][layer][None], g["state_ffn_conv"][layer, 0]])
        arrays[f"ffn_p{layer}"] = pr.reshape(6, 2, GROUPS, 2, P).transpose(2, 4, 3, 1, 0).reshape(GROUPS, P, 4, 6)
    arrays = {k: np.ascontiguousarray(v, dtype=v.dtype) for k, v in arrays.items()}

    outs = {"y": (P, KT, T), "ckv": (P, 2, SEQ), "ckvs": (P, 2, DEC_SEQ), "kpe": (C_ROPE, SEQ), "kpes": (C_ROPE, DEC_SEQ),
            "dk": (P, P), "dv": (P, P), "dks": (P, P), "dvs": (P, P)}
    for kv in "kv":
        outs |= {f"a{kv}": (PAIRS, P, 512), f"a{kv}s": (PAIRS, P, PAST), f"b{kv}": (PAIRS, P, SEQ), f"b{kv}s": (PAIRS, P, DEC_SEQ)}
    for layer in range(2):
        outs[f"tails{layer}"] = (GROUPS, P, 8, 2)

    nc = bacc.Bacc("TRN2", target_bir_lowering=False, num_devices=1)
    ap = {k: nc.dram_tensor(f"in_{k}", a.shape, mybir.dt.from_np(a.dtype), kind="ExternalInput").ap() for k, a in arrays.items()}
    ap |= {f"o_{k}": nc.dram_tensor(f"out_{k}", s, F32, kind="ExternalOutput").ap() for k, s in outs.items()}
    program(nc, ap)
    r = run_bass_kernel_spmd(nc, [{f"in_{k}": a for k, a in arrays.items()}], core_ids=[0]).results[0]
    r = {k: np.asarray(r[f"out_{k}"]) for k in outs}

    y = r["y"].transpose(2, 1, 0).reshape(T, D_MODEL)
    rows = lambda z, heads: np.moveaxis(z, -1, 0).reshape(1, 1, z.shape[-1], heads, HEAD)
    seq = lambda z: z.transpose(2, 1, 0).reshape(1, 1, z.shape[2], C_KV)
    tails = [r[f"tails{l}"].reshape(GROUPS, P, 2, 2, 2, 2).transpose(4, 5, 3, 0, 2, 1).reshape(2, 2, 2 * D_FF) for l in range(2)]
    conv = [np.stack([t[s] for t in tails])[:, None] for s in range(2)]
    return (y[None, :SEQ], y[None, S0:],
            rows(r["ak"], 8), rows(r["av"], 8), rows(r["aks"], 8), rows(r["avs"], 8),
            rows(r["bk"], 8), rows(r["bv"], 8), rows(r["bks"], 8), rows(r["bvs"], 8),
            seq(r["ckv"]), r["kpe"].T[None, None], seq(r["ckvs"]), r["kpes"].T[None, None],
            rows(r["dk"], 2), rows(r["dv"], 2), rows(r["dks"], 2), rows(r["dvs"], 2),
            conv[0], conv[1])


def program(nc, ap):
    io = Mem()
    io.x, io.gains, io.w0, io.w1, io.c_q, io.c_kv, io.w1_out = (
        ap[k] for k in ("x", "gains", "w0", "w1", "c_q", "c_kv", "w1_out"))
    io.cache_c, io.cache_pe, io.cache_dk, io.cache_dv = (ap[f"cache_{k}"] for k in ("c", "pe", "dk", "dv"))
    io.rot, io.alibi, io.bias = ap["rot"], ap["alibi"], ap["bias"]
    io.y, io.ckv, io.ckvs, io.kpe, io.kpes = (ap[f"o_{k}"] for k in ("y", "ckv", "ckvs", "kpe", "kpes"))
    io.dk, io.dv, io.dks, io.dvs = (ap[f"o_{k}"] for k in ("dk", "dv", "dks", "dvs"))
    io.sinks = bass.AP(ap["sinks"].tensor, 0, [[2, PAIRS + 1], [0, P], [1, 2]])
    io.cache_k, io.cache_v = ap["cache_k"], ap["cache_v"]
    io.stores = {n.upper(): tuple(ap[f"o_{n}{k}"] for k in ("k", "v", "ks", "vs"))
                 + ((SEQ - 512, SEQ + DEC_SEQ) if n == "a" else (0, SEQ + PAST)) for n in "ab"}
    io.ffn_w = [ap["ffn_w0"], ap["ffn_w1"]]
    io.ffn_p = [ap["ffn_p0"], ap["ffn_p1"]]
    io.tails = [ap["o_tails0"], ap["o_tails1"]]
    build(nc, io)
```
